# Optimizing a Trainium2 kernel written in Bass

```python
import math
import jax
import jax.numpy as jnp
from jax import lax
import numpy as np

D_MODEL = 1024
BATCH = 1
SEQ = 256
DEPTH = 1

HEAD_DIM = 64
A_Q_HEADS = 8
A_KV_HEADS = 2
A_WINDOW = 128
B_GROUPS = ((128, 1), (512, 4), (2048, 16))
B_HEADS_PER_GROUP = 8
A_WIDTH = A_Q_HEADS * HEAD_DIM
B_WIDTH = B_HEADS_PER_GROUP * HEAD_DIM
N_BRANCHES = 2
N_BUCKETS = 32
MAX_DISTANCE = 1024
REL_HEADS = A_Q_HEADS + len(B_GROUPS) * B_HEADS_PER_GROUP
PROJ_SIZES = (A_WIDTH, A_KV_HEADS * HEAD_DIM, A_KV_HEADS * HEAD_DIM,
              len(B_GROUPS) * B_WIDTH, len(B_GROUPS) * B_WIDTH, len(B_GROUPS) * B_WIDTH,
              A_WIDTH, B_WIDTH, N_BRANCHES * D_MODEL)
IN_WIDTH = sum(PROJ_SIZES)
EPS = 1e-6
NEG_INF = -1e30


def rms_norm(x, gain):
    xf = x.astype(jnp.float32)
    y = xf * lax.rsqrt(jnp.mean(xf * xf, axis=-1, keepdims=True) + EPS)
    return (y * gain.astype(jnp.float32)).astype(x.dtype)

def t5_bucket(rel):
    half = N_BUCKETS // 2
    max_exact = half // 2
    ret = (rel > 0).astype(jnp.int32) * half
    n = jnp.abs(rel)
    nf = jnp.maximum(n, max_exact).astype(jnp.float32)
    large = max_exact + (jnp.log(nf / max_exact) / math.log(MAX_DISTANCE / max_exact)
                         * (half - max_exact)).astype(jnp.int32)
    large = jnp.minimum(large, half - 1)
    return ret + jnp.where(n < max_exact, n, large)

def banded_attention(q, k, v, half_window, stride, bias_table, sink):
    bsz, L, H, dh = q.shape
    KV = k.shape[2]
    G = H // KV
    blk = half_window
    nb = -(-L // blk)
    Lp = nb * blk
    pad = Lp - L
    qb = jnp.pad(q, ((0, 0), (0, pad), (0, 0), (0, 0))).reshape(bsz, nb, blk, KV, G, dh)

    def windows(t):
        tp = jnp.pad(t, ((0, 0), (blk, blk + pad), (0, 0), (0, 0))).reshape(bsz, nb + 2, blk, KV, dh)
        return jnp.concatenate([tp[:, :-2], tp[:, 1:-1], tp[:, 2:]], axis=2)

    kw = windows(k)
    vw = windows(v)
    scores = jnp.einsum('bnqkgd,bnmkd->bkgnqm', qb, kw).astype(jnp.float32)

    qi = jnp.arange(blk)
    mi = jnp.arange(3 * blk)
    rel = mi[None, :] - blk - qi[:, None]
    bias = bias_table[t5_bucket(rel * stride)]
    bias = bias.transpose(2, 0, 1).reshape(KV, G, 1, blk, 3 * blk).astype(jnp.float32)
    blocks = jnp.arange(nb)[:, None, None] * blk
    qpos = blocks + qi[None, :, None]
    kpos = blocks - blk + mi[None, None, :]
    valid = (kpos >= 0) & (kpos < L) & (jnp.abs(kpos - qpos) <= half_window)

    logits = jnp.where(valid, scores + bias, NEG_INF)
    lse = jax.nn.logsumexp(logits, axis=-1)
    if sink is not None:
        lse = jnp.logaddexp(lse, sink.astype(jnp.float32).reshape(KV, G, 1, 1))
    probs = jnp.exp(logits - lse[..., None])
    out = jnp.einsum('bkgnqm,bnmkd->bnqkgd', probs.astype(v.dtype), vw)
    out = out.reshape(bsz, Lp, H, dh)[:, :L]
    lse = lse.transpose(0, 3, 4, 1, 2).reshape(bsz, Lp, H)[:, :L]
    return out, lse

def dilated_group(q, k, v, window, dilation, bias_table):
    bsz, S, H, dh = q.shape
    L = S // dilation

    def to_sub(t):
        return t.reshape(bsz, L, dilation, H, dh).transpose(0, 2, 1, 3, 4).reshape(bsz * dilation, L, H, dh)

    out, lse = banded_attention(to_sub(q), to_sub(k), to_sub(v), window // (2 * dilation),
                                dilation, bias_table, None)
    out = out.reshape(bsz, dilation, L, H, dh).transpose(0, 2, 1, 3, 4).reshape(bsz, S, H, dh)
    lse = lse.reshape(bsz, dilation, L, H).transpose(0, 2, 1, 3).reshape(bsz, S, H)
    return out, lse

def head_rms_norm(t, gain):
    return rms_norm(t, gain)

def first_inputs(seed: int = 0) -> dict:
    key = jax.random.key(seed)
    ks = jax.random.split(key, 16)
    f32 = jnp.float32
    x = jax.random.normal(ks[0], (BATCH, SEQ, D_MODEL), f32)
    norm_gain = 1.0 + 0.02 * jax.random.normal(ks[1], (DEPTH, D_MODEL), f32)
    w_in = jax.random.normal(ks[2], (DEPTH, D_MODEL, IN_WIDTH), f32) * D_MODEL ** -0.5
    q_norm_a = 1.0 + 0.02 * jax.random.normal(ks[3], (DEPTH, HEAD_DIM), f32)
    k_norm_a = 1.0 + 0.02 * jax.random.normal(ks[4], (DEPTH, HEAD_DIM), f32)
    q_norm_b = 1.0 + 0.02 * jax.random.normal(ks[5], (DEPTH, HEAD_DIM), f32)
    k_norm_b = 1.0 + 0.02 * jax.random.normal(ks[6], (DEPTH, HEAD_DIM), f32)
    sink_a = 0.5 * jax.random.normal(ks[7], (DEPTH, A_Q_HEADS), f32)
    rel_bias = 0.5 * jax.random.normal(ks[8], (N_BUCKETS, REL_HEADS), f32)
    w_branch_a = jax.random.normal(ks[9], (DEPTH, A_WIDTH, D_MODEL), f32) * A_WIDTH ** -0.5
    w_branch_b = jax.random.normal(ks[10], (DEPTH, B_WIDTH, D_MODEL), f32) * B_WIDTH ** -0.5
    b_merge = 0.1 * jax.random.normal(ks[11], (DEPTH, N_BRANCHES, D_MODEL), f32)
    w_out = jax.random.normal(ks[12], (DEPTH, D_MODEL, D_MODEL), f32) * D_MODEL ** -0.5
    return {"x": x, "norm_gain": norm_gain, "w_in": w_in, "q_norm_a": q_norm_a,
            "k_norm_a": k_norm_a, "q_norm_b": q_norm_b, "k_norm_b": k_norm_b,
            "sink_a": sink_a, "rel_bias": rel_bias, "w_branch_a": w_branch_a,
            "w_branch_b": w_branch_b, "b_merge": b_merge, "w_out": w_out}

def first_block(x, norm_gain, w_in, q_norm_a, k_norm_a, q_norm_b, k_norm_b, sink_a,
              rel_bias, w_branch_a, w_branch_b, b_merge, w_out):
    bsz, S, D = x.shape
    n_groups = len(B_GROUPS)
    scale = HEAD_DIM ** -0.5
    split_idx = [int(i) for i in np.cumsum(PROJ_SIZES)[:-1]]
    for layer in range(DEPTH):
        h = rms_norm(x, norm_gain[layer])
        proj = h @ w_in[layer]
        qa, ka, va, qb, kb, vb, ga, gb, mg = jnp.split(proj, split_idx, axis=-1)

        qa = head_rms_norm(qa.reshape(bsz, S, A_Q_HEADS, HEAD_DIM), q_norm_a[layer]) * scale
        ka = head_rms_norm(ka.reshape(bsz, S, A_KV_HEADS, HEAD_DIM), k_norm_a[layer])
        va = va.reshape(bsz, S, A_KV_HEADS, HEAD_DIM)
        ya, _ = banded_attention(qa, ka, va, A_WINDOW, 1, rel_bias[:, :A_Q_HEADS], sink_a[layer])
        ya = ya.reshape(bsz, S, A_WIDTH) * jax.nn.silu(ga)

        qb = head_rms_norm(qb.reshape(bsz, S, n_groups, B_HEADS_PER_GROUP, HEAD_DIM), q_norm_b[layer]) * scale
        kb = head_rms_norm(kb.reshape(bsz, S, n_groups, B_HEADS_PER_GROUP, HEAD_DIM), k_norm_b[layer])
        vb = vb.reshape(bsz, S, n_groups, B_HEADS_PER_GROUP, HEAD_DIM)
        outs = []
        lses = []
        for g, (window, dilation) in enumerate(B_GROUPS):
            c0 = A_Q_HEADS + g * B_HEADS_PER_GROUP
            o, l = dilated_group(qb[:, :, g], kb[:, :, g], vb[:, :, g], window, dilation,
                                 rel_bias[:, c0:c0 + B_HEADS_PER_GROUP])
            outs.append(o)
            lses.append(l)
        alpha = jax.nn.softmax(jnp.stack(lses, axis=0), axis=0)
        yb = jnp.sum(alpha[..., None].astype(x.dtype) * jnp.stack(outs, axis=0), axis=0)
        yb = yb.reshape(bsz, S, B_WIDTH) * jax.nn.silu(gb)

        br_a = ya @ w_branch_a[layer]
        br_b = yb @ w_branch_b[layer]
        gates = jax.nn.sigmoid(mg.reshape(bsz, S, N_BRANCHES, D).astype(jnp.float32)
                               + b_merge[layer].astype(jnp.float32)).astype(x.dtype)
        merged = gates[:, :, 0] * br_a + gates[:, :, 1] * br_b
        x = x + merged @ w_out[layer]
    return x


DEPTH_2 = 2

BRANCH_W = D_MODEL // 2
N_BRANCH = 3
NSA_HEADS = 8
NSA_GROUPS = 2
NSA_HPG = NSA_HEADS // NSA_GROUPS
NSA_DH = BRANCH_W // NSA_HEADS
NSA_KV = NSA_GROUPS * NSA_DH
CMP_BLOCK = 32
CMP_STRIDE = 16
CMP_HIDDEN = 2 * NSA_DH
SEL_BLOCK = 64
SEL_TOPK = 8
WINDOW = 512
Q_BLOCK = 128
RET_HEADS = 4
RET_DV = BRANCH_W // RET_HEADS
RET_DK = RET_DV // 2
RET_CHUNK = 128
ROPE_BASE = 10000.0
CONV_CH = BRANCH_W
CONV_WIDTH = 31
REL_BUCKETS = 32
REL_MAX_DIST = 128
D_FF = 4 * D_MODEL
IN_WIDTHS = (NSA_HEADS * NSA_DH, NSA_KV, NSA_KV, NSA_KV, NSA_KV, NSA_KV, NSA_KV, 3 * NSA_HEADS,
             RET_HEADS * RET_DK, RET_HEADS * RET_DK, RET_HEADS * RET_DV, RET_HEADS * RET_DV,
             CONV_CH, CONV_CH, N_BRANCH * D_MODEL)
IN_TOTAL = sum(IN_WIDTHS)


def _rmsnorm(x, g):
    x32 = x.astype(jnp.float32)
    y = x32 * lax.rsqrt(jnp.mean(x32 * x32, axis=-1, keepdims=True) + EPS)
    return (y * g.astype(jnp.float32)).astype(x.dtype)

def _layernorm(x, g, b=None):
    x32 = x.astype(jnp.float32)
    mu = jnp.mean(x32, axis=-1, keepdims=True)
    var = jnp.mean(jnp.square(x32 - mu), axis=-1, keepdims=True)
    y = (x32 - mu) * lax.rsqrt(var + EPS) * g.astype(jnp.float32)
    if b is not None:
        y = y + b.astype(jnp.float32)
    return y

def _split_cols(z):
    parts = []
    start = 0
    for w in IN_WIDTHS:
        parts.append(z[..., start:start + w])
        start += w
    return parts

def _rel_bucket(dist):
    n = jnp.maximum(dist, 0)
    max_exact = REL_BUCKETS // 2
    nf = jnp.maximum(n, 1).astype(jnp.float32)
    large = max_exact + (jnp.log(nf / max_exact) / math.log(REL_MAX_DIST / max_exact)
                         * (REL_BUCKETS - max_exact)).astype(jnp.int32)
    large = jnp.minimum(large, REL_BUCKETS - 1)
    return jnp.where(n < max_exact, n, large)

def _masked_softmax(s, mask):
    s = jnp.where(mask, s, -1e30)
    m = jnp.max(s, axis=-1, keepdims=True)
    p = jnp.exp(s - m) * mask
    den = jnp.sum(p, axis=-1, keepdims=True)
    return p / jnp.maximum(den, 1e-30)

def _rotary(x, pos):
    half = x.shape[-1] // 2
    inv = ROPE_BASE ** (-jnp.arange(half, dtype=jnp.float32) / half)
    ang = pos[:, None] * inv[None, :]
    cos = jnp.cos(ang)[:, None, :]
    sin = jnp.sin(ang)[:, None, :]
    x32 = x.astype(jnp.float32)
    x1, x2 = x32[..., :half], x32[..., half:]
    return jnp.concatenate([x1 * cos - x2 * sin, x1 * sin + x2 * cos], axis=-1).astype(x.dtype)

def _compress(x, pe, w1, w2):
    B, S, G, DH = x.shape
    n_ch = S // CMP_STRIDE
    r = CMP_BLOCK // CMP_STRIDE
    n_c = n_ch - r + 1
    ch = x.reshape(B, n_ch, CMP_STRIDE, G, DH)
    blocks = jnp.concatenate([ch[:, i:i + n_c] for i in range(r)], axis=2) + pe[None, None, :, None, :]
    hid = jax.nn.gelu(jnp.einsum('bnlgd,ldf->bngf', blocks, w1))
    return jnp.einsum('bngf,fd->bngd', hid, w2)

def _nsa(q, kc, vc, ks, vs, kw, vw, gl, pe_k, w1_k, w2_k, pe_v, w1_v, w2_v, rel_table):
    B, S, _ = q.shape
    G, HPG, DH = NSA_GROUPS, NSA_HPG, NSA_DH
    dt = q.dtype
    q = q.reshape(B, S, G, HPG, DH) * (DH ** -0.5)
    kc, vc, ks, vs, kw, vw = [a.reshape(B, S, G, DH) for a in (kc, vc, ks, vs, kw, vw)]
    k_cmp = _compress(kc, pe_k, w1_k, w2_k)
    v_cmp = _compress(vc, pe_v, w1_v, w2_v)
    n_c = k_cmp.shape[1]
    cmp_start = jnp.arange(n_c) * CMP_STRIDE
    cmp_end = cmp_start + (CMP_BLOCK - 1)
    n_s = S // SEL_BLOCK
    k_eff = min(SEL_TOPK, n_s)
    sel_start = jnp.arange(n_s) * SEL_BLOCK
    overlap = ((cmp_start[:, None] <= sel_start[None, :] + SEL_BLOCK - 1)
               & (cmp_end[:, None] >= sel_start[None, :])).astype(jnp.float32)
    ks_blk = ks.reshape(B, n_s, SEL_BLOCK, G, DH).transpose(0, 3, 1, 2, 4)
    vs_blk = vs.reshape(B, n_s, SEL_BLOCK, G, DH).transpose(0, 3, 1, 2, 4)
    kw_pad = jnp.pad(kw, ((0, 0), (WINDOW, 0), (0, 0), (0, 0)))
    vw_pad = jnp.pad(vw, ((0, 0), (WINDOW, 0), (0, 0), (0, 0)))
    tb = rel_table.reshape(REL_BUCKETS, G, HPG).transpose(1, 0, 2)
    b_idx = jnp.arange(B)[:, None, None, None]
    g_idx = jnp.arange(G)[None, :, None, None]
    sb_ar = jnp.arange(SEL_BLOCK)

    def head_bias(dist):
        bias = rel_table[_rel_bucket(dist)]
        return jnp.transpose(bias, (2, 0, 1)).reshape(G, HPG, dist.shape[0], dist.shape[1]).astype(jnp.float32)

    def block_fn(args):
        c, qb, gb = args
        t = c * Q_BLOCK + jnp.arange(Q_BLOCK)
        dist_c = t[:, None] - cmp_end[None, :]
        s_c = jnp.einsum('bqghd,bngd->bghqn', qb, k_cmp).astype(jnp.float32) + head_bias(dist_c)
        p_c = _masked_softmax(s_c, dist_c >= 0)
        o_c = jnp.einsum('bghqn,bngd->bqghd', p_c, v_cmp)
        imp = jnp.einsum('bghqn,ns->bgqs', p_c, overlap)
        jb = jnp.arange(n_s)[None, :]
        cur = (t // SEL_BLOCK)[:, None]
        valid = jb <= cur
        forced = (jb == 0) | (jb == cur) | (jb == cur - 1)
        score = jnp.where(forced, imp + 1e4, jnp.where(valid, imp, -1e4))
        _, idx = lax.top_k(score, k_eff)
        kg = ks_blk[b_idx, g_idx, idx]
        vg = vs_blk[b_idx, g_idx, idx]
        pos_s = idx[..., None] * SEL_BLOCK + sb_ar
        dist_s = t[None, None, :, None, None] - pos_s
        bias_s = tb[g_idx[..., None], _rel_bucket(dist_s)]
        s_s = jnp.einsum('bqghd,bgqkld->bghqkl', qb, kg).astype(jnp.float32) + jnp.moveaxis(bias_s, -1, 2).astype(jnp.float32)
        mask_s = (dist_s >= 0)[:, :, None]
        p_s = _masked_softmax(s_s.reshape(B, G, HPG, Q_BLOCK, k_eff * SEL_BLOCK),
                              mask_s.reshape(B, G, 1, Q_BLOCK, k_eff * SEL_BLOCK))
        p_s = p_s.reshape(B, G, HPG, Q_BLOCK, k_eff, SEL_BLOCK)
        o_s = jnp.einsum('bghqkl,bgqkld->bqghd', p_s, vg)
        start = c * Q_BLOCK
        kwb = lax.dynamic_slice_in_dim(kw_pad, start, WINDOW + Q_BLOCK, axis=1)
        vwb = lax.dynamic_slice_in_dim(vw_pad, start, WINDOW + Q_BLOCK, axis=1)
        pos_w = start - WINDOW + jnp.arange(WINDOW + Q_BLOCK)
        dist_w = t[:, None] - pos_w[None, :]
        mask_w = (dist_w >= 0) & (dist_w < WINDOW) & (pos_w[None, :] >= 0)
        s_w = jnp.einsum('bqghd,bkgd->bghqk', qb, kwb).astype(jnp.float32) + head_bias(dist_w)
        p_w = _masked_softmax(s_w, mask_w)
        o_w = jnp.einsum('bghqk,bkgd->bqghd', p_w, vwb)
        gs = jax.nn.sigmoid(gb.astype(jnp.float32)).reshape(B, Q_BLOCK, G, HPG, 3)
        o = gs[..., 0:1] * o_c + gs[..., 1:2] * o_s + gs[..., 2:3] * o_w
        return o.astype(dt)

    n_qb = S // Q_BLOCK
    q_blocks = q.reshape(B, n_qb, Q_BLOCK, G, HPG, DH).transpose(1, 0, 2, 3, 4, 5)
    g_blocks = gl.reshape(B, n_qb, Q_BLOCK, NSA_HEADS, 3).transpose(1, 0, 2, 3, 4)
    out = lax.map(block_fn, (jnp.arange(n_qb), q_blocks, g_blocks))
    return out.transpose(1, 0, 2, 3, 4, 5).reshape(B, S, NSA_HEADS * DH)

def _retention(q, k, v, g, gn_gain):
    B, S, _ = q.shape
    H, DK, DV, C = RET_HEADS, RET_DK, RET_DV, RET_CHUNK
    dt = q.dtype
    pos = jnp.arange(S, dtype=jnp.float32)
    q = _rotary(q.reshape(B, S, H, DK), pos)
    k = _rotary(k.reshape(B, S, H, DK), pos) * (DK ** -0.5)
    v = v.reshape(B, S, H, DV)
    log_g = jnp.log1p(-jnp.exp2(-5.0 - jnp.arange(H, dtype=jnp.float32)))
    N = S // C
    qc = q.reshape(B, N, C, H, DK)
    kc = k.reshape(B, N, C, H, DK)
    vc = v.reshape(B, N, C, H, DV)
    ar = jnp.arange(C)
    diff = ar[:, None] - ar[None, :]
    decay = jnp.where(diff >= 0, jnp.exp(log_g[:, None, None] * jnp.maximum(diff, 0).astype(jnp.float32)), 0.0)
    inner = jnp.einsum('bnchd,bnehd->bnhce', qc, kc).astype(jnp.float32) * decay
    o_inner = jnp.einsum('bnhce,bnehv->bnchv', inner, vc)
    zeta = jnp.exp(log_g[:, None] * (C - 1 - ar).astype(jnp.float32))
    xi = jnp.exp(log_g[:, None] * (ar + 1).astype(jnp.float32))
    kv = jnp.einsum('bnchd,hc,bnchv->bnhdv', kc, zeta, vc)
    g_chunk = jnp.exp(log_g * C)[None, :, None, None]

    def step(state, kv_n):
        return g_chunk * state + kv_n, state

    init = jnp.zeros((B, H, DK, DV), kv.dtype)
    _, prev = lax.scan(step, init, kv.transpose(1, 0, 2, 3, 4))
    prev = prev.transpose(1, 0, 2, 3, 4)
    o_cross = jnp.einsum('bnchd,hc,bnhdv->bnchv', qc, xi, prev)
    o = (o_inner + o_cross).reshape(B, S, H, DV)
    o = _layernorm(o, jnp.ones((DV,), jnp.float32)).reshape(B, S, H * DV) * gn_gain.astype(jnp.float32)
    return (jax.nn.silu(g.astype(jnp.float32)) * o).astype(dt)

def _conv_module(a, b, dw_w, dw_b, ln_g, ln_b):
    u = a * jax.nn.sigmoid(b)
    kern = dw_w[:, None, :].astype(u.dtype)
    y = lax.conv_general_dilated(u, kern, window_strides=(1,), padding=[(CONV_WIDTH - 1, 0)],
                                 dimension_numbers=('NWC', 'WIO', 'NWC'), feature_group_count=CONV_CH)
    y = y + dw_b
    y = _layernorm(y, ln_g, ln_b)
    return jax.nn.silu(y).astype(a.dtype)

def second_inputs(seed: int = 0) -> dict:
    key = jax.random.key(seed)
    k = jax.random.split(key, 21)
    f32 = jnp.float32

    def nrm(kk, shape, scale):
        return jax.random.normal(kk, shape, f32) * scale

    return {
        'x': nrm(k[0], (BATCH, SEQ, D_MODEL), 1.0),
        'rel_table': nrm(k[1], (REL_BUCKETS, NSA_HEADS), 0.5),
        'norm_mix': 1.0 + nrm(k[2], (DEPTH_2, D_MODEL), 0.05),
        'w_in': nrm(k[3], (DEPTH_2, D_MODEL, IN_TOTAL), D_MODEL ** -0.5),
        'cmp_pe_k': nrm(k[4], (DEPTH_2, CMP_BLOCK, NSA_DH), 0.5),
        'cmp_w1_k': nrm(k[5], (DEPTH_2, CMP_BLOCK, NSA_DH, CMP_HIDDEN), (CMP_BLOCK * NSA_DH) ** -0.5),
        'cmp_w2_k': nrm(k[6], (DEPTH_2, CMP_HIDDEN, NSA_DH), CMP_HIDDEN ** -0.5),
        'cmp_pe_v': nrm(k[7], (DEPTH_2, CMP_BLOCK, NSA_DH), 0.5),
        'cmp_w1_v': nrm(k[8], (DEPTH_2, CMP_BLOCK, NSA_DH, CMP_HIDDEN), (CMP_BLOCK * NSA_DH) ** -0.5),
        'cmp_w2_v': nrm(k[9], (DEPTH_2, CMP_HIDDEN, NSA_DH), CMP_HIDDEN ** -0.5),
        'ret_gn': 1.0 + nrm(k[10], (DEPTH_2, RET_HEADS * RET_DV), 0.05),
        'conv_w': nrm(k[11], (DEPTH_2, CONV_WIDTH, CONV_CH), CONV_WIDTH ** -0.5),
        'conv_b': nrm(k[12], (DEPTH_2, CONV_CH), 0.02),
        'conv_ln_g': 1.0 + nrm(k[13], (DEPTH_2, CONV_CH), 0.05),
        'conv_ln_b': nrm(k[14], (DEPTH_2, CONV_CH), 0.02),
        'w_branch': nrm(k[15], (DEPTH_2, N_BRANCH, BRANCH_W, D_MODEL), BRANCH_W ** -0.5),
        'w_out': nrm(k[16], (DEPTH_2, D_MODEL, D_MODEL), D_MODEL ** -0.5),
        'norm_mlp': 1.0 + nrm(k[17], (DEPTH_2, D_MODEL), 0.05),
        'w_ff1': nrm(k[18], (DEPTH_2, D_MODEL, D_FF), D_MODEL ** -0.5),
        'w_ff2': nrm(k[19], (DEPTH_2, D_FF, D_MODEL), D_FF ** -0.5),
        'norm_final': 1.0 + nrm(k[20], (D_MODEL,), 0.05),
    }

def second_block(x, rel_table, norm_mix, w_in, cmp_pe_k, cmp_w1_k, cmp_w2_k, cmp_pe_v, cmp_w1_v, cmp_w2_v,
              ret_gn, conv_w, conv_b, conv_ln_g, conv_ln_b, w_branch, w_out, norm_mlp, w_ff1, w_ff2,
              norm_final):
    B, S, _ = x.shape
    for l in range(DEPTH_2):
        h = _rmsnorm(x, norm_mix[l])
        z = h @ w_in[l]
        (q_n, kc, vc, ks, vs, kw, vw, g_n, q_r, k_r, v_r, g_r, c_a, c_b, m_g) = _split_cols(z)
        o_nsa = _nsa(q_n, kc, vc, ks, vs, kw, vw, g_n, cmp_pe_k[l], cmp_w1_k[l], cmp_w2_k[l],
                     cmp_pe_v[l], cmp_w1_v[l], cmp_w2_v[l], rel_table)
        o_ret = _retention(q_r, k_r, v_r, g_r, ret_gn[l])
        o_conv = _conv_module(c_a, c_b, conv_w[l], conv_b[l], conv_ln_g[l], conv_ln_b[l])
        br = jnp.stack([o_nsa.astype(x.dtype), o_ret.astype(x.dtype), o_conv.astype(x.dtype)], axis=2)
        proj = jnp.einsum('bsnc,ncd->bsnd', br, w_branch[l])
        gate = jax.nn.sigmoid(m_g.astype(jnp.float32)).reshape(B, S, N_BRANCH, D_MODEL)
        merged = jnp.sum(gate * proj, axis=2).astype(x.dtype)
        x = x + merged @ w_out[l]
        h2 = _rmsnorm(x, norm_mlp[l])
        x = x + jnp.square(jax.nn.relu(h2 @ w_ff1[l])) @ w_ff2[l]
    return _rmsnorm(x, norm_final)


def setup_inputs(seed=0):
    out = dict(first_inputs(seed))
    for name, value in second_inputs(seed + 1).items():
        if name != "x":
            out[name + "_2"] = value
    return out


def reference(
    x, norm_gain, w_in, q_norm_a, k_norm_a, q_norm_b, k_norm_b, sink_a, rel_bias, w_branch_a,
    w_branch_b, b_merge, w_out, rel_table_2, norm_mix_2, w_in_2, cmp_pe_k_2, cmp_w1_k_2,
    cmp_w2_k_2, cmp_pe_v_2, cmp_w1_v_2, cmp_w2_v_2, ret_gn_2, conv_w_2, conv_b_2, conv_ln_g_2,
    conv_ln_b_2, w_branch_2, w_out_2, norm_mlp_2, w_ff1_2, w_ff2_2, norm_final_2,
):
    x = first_block(
        x, norm_gain, w_in, q_norm_a, k_norm_a, q_norm_b, k_norm_b, sink_a, rel_bias,
        w_branch_a, w_branch_b, b_merge, w_out,
    )
    return second_block(
        x, rel_table_2, norm_mix_2, w_in_2, cmp_pe_k_2, cmp_w1_k_2, cmp_w2_k_2, cmp_pe_v_2,
        cmp_w1_v_2, cmp_w2_v_2, ret_gn_2, conv_w_2, conv_b_2, conv_ln_g_2, conv_ln_b_2,
        w_branch_2, w_out_2, norm_mlp_2, w_ff1_2, w_ff2_2, norm_final_2,
    )


_drawn_inputs = setup_inputs


def setup_inputs(seed=0):
    import zlib

    import numpy as np

    out = dict(_drawn_inputs(seed))
    spreads = {}
    factors = {'norm_gain': 8.0,
     'q_norm_a': 8.0,
     'k_norm_a': 8.0,
     'q_norm_b': 8.0,
     'k_norm_b': 8.0,
     'sink_a': 8.0,
     'b_merge': 8.0,
     'cmp_pe_k_2': 29.328,
     'ret_gn_2': 23.12,
     'conv_b_2': 162.706,
     'conv_ln_b_2': 51.696,
     'rel_table_2': 8.0,
     'norm_mix_2': 8.0,
     'cmp_w1_k_2': 8.0,
     'cmp_w2_k_2': 8.0,
     'cmp_pe_v_2': 8.0,
     'cmp_w1_v_2': 8.0,
     'cmp_w2_v_2': 8.0,
     'conv_w_2': 5.464,
     'conv_ln_g_2': 50.353,
     'norm_mlp_2': 8.0}
    for name, (base, spread) in spreads.items():
        noise = np.random.default_rng([zlib.crc32(name.encode()), seed]).standard_normal(out[name].shape)
        drawn = base * np.exp(spread * noise) if base else spread * noise
        out[name] = jnp.asarray(drawn.astype(out[name].dtype))
    for name, factor in factors.items():
        out[name] = (out[name] * factor).astype(out[name].dtype)
    return out
```

```python
from contextlib import ExitStack

import numpy as np

import concourse.bass as bass
from concourse import mybir

F32 = mybir.dt.float32
ALU = mybir.AluOpType
ACT = mybir.ActivationFunctionType
AX = mybir.AxisListType

P = 128
TOKENS, D = 256, 1024
NB = TOKENS // P
KC = D // P
HD = 64
H = 8
HALF = 4 * 512
SLOTS = 6
EPS = 1e-6
MASKED = -1e30
LAYERS = 2
GROUPS = ((128, 1), (512, 4), (2048, 16))
N_CMP, CMP_STRIDE, CMP_LEN = 15, 16, 32
TAPS = 31
RET_H = 4
FF_PANELS = 8
TOEP = 3 * P
GELU_C, GELU_A = 0.7978845608028654, 0.044715

PAR_SIZES = dict(mix=KC, mlp=KC, gn=4, ln_g=4, ln_b=4, conv_b=4, conv_w=4 * TAPS, pe=32, w2k=P, w2v=HD)
PAR_AT, PAR = {}, 0
for _name, _size in PAR_SIZES.items():
    PAR_AT[_name] = (PAR, PAR + _size)
    PAR += _size
FIRST_AT = dict(norm=(0, 8), gains=(8, 12), sink=(12, 20))
FIRST = 20

FIRST_PANELS = ["qa", "kava", "qb0", "qb1", "qb2", "kb0", "kb1", "kb2", "vb0", "vb1", "vb2", "ga", "gb",
                "mg0", "mg1", "mg2", "mg3", "OA", "OB", "br00", "br01", "br10", "br11", "wo0", "wo1"]
NORMED = ["qa", "kava", "qb0", "qb1", "qb2", "kb0", "kb1", "kb2"]
LAYER_PANELS = (["cb", "ca", "q", "k4", "vsg", "qkr", "vr", "gr", "Oc", "mg0", "Or", "mg1", "mg2", "mg3",
                 "mg4", "mg5", "O0", "O1"] + [f"br{i}{c}" for i in range(3) for c in range(2)]
                + ["wo0", "wo1"] + [f"ff{i}" for i in range(FF_PANELS)] + ["down0", "down1"])


def halves_of(panels, skip):
    out = []
    for p in panels:
        if p in skip:
            continue
        n = 1 if p.startswith("br") else 8 if p.startswith("down") else 2
        out += [(f"{p}/{i}", p) for i in range(n)]
        if p == "vsg":
            out += [("w1k", "cmpH"), ("w1v", "cmpH")]
    return out


FIRST_HALVES = halves_of(FIRST_PANELS, ("OA", "OB"))
LAYER_HALVES = halves_of(LAYER_PANELS, ("Oc", "Or", "O0", "O1"))
N_HALVES = len(LAYER_HALVES)
ONE_BY_ONE = ("cb", "ca", "q", "k4", "cmpH", *[f"ff{i}" for i in range(FF_PANELS)])


def units_first():
    return [("A", h, 1) for h in range(H)] + [("B", h, 3) for h in range(H)]


def units_layer():
    return [("s", h, 1) for h in range(H)] + [("w", h, 1) for h in range(H)]


def attention_tiles(units):
    out = []
    for i in range(len(units) + 1):
        if i < len(units):
            out += [f"S{units[i][0]}{units[i][1]}{g}" for g in range(units[i][2])]
        if i >= 1:
            u = units[i - 1]
            out += [f"T{u[0]}{u[1]}{g}" for g in range(u[2])]
    return out


def transposed(name):
    return [f"{name}{b}" for b in range(NB)]


FIRST_TILES = (["bias0", "bias1", "bias2", "bias3", "bias4"] + [f"x{b}{i}" for b in range(NB) for i in range(2)]
               + [t for p in NORMED for t in transposed(p)] + attention_tiles(units_first())
               + transposed("yA") + transposed("yB") + [f"m{b}{i}" for b in range(NB) for i in range(2)])
LAYER_TILES = ([f"x{b}{i}" for b in range(NB) for i in range(2)] + ["cmpH"] + transposed("rot") + ["cmp2", "cmpS0", "cmpS1"]
               + ["PcT"] + [f"R{h}" for h in range(RET_H)] + transposed("oR")
               + transposed("cv") + transposed("cz") + attention_tiles(units_layer()) + transposed("y")
               + [f"m{b}{i}" for b in range(NB) for i in range(2)]
               + [f"z{b}{i}" for b in range(NB) for i in range(2)])


def last_half(name, p, halves):
    i = [h for h, _ in halves].index(name)
    return p in ONE_BY_ONE or i + 1 == len(halves) or halves[i + 1][1] != p


def used_before(name, halves):
    i = [h for h, _ in halves].index(name)
    return sum(not last_half(h, p, halves) for h, p in halves[:i])


PADS = 4
X_UPDATES = 1 + 2 * LAYERS


class Turns:

    def __init__(self, names, buffers, before=None):
        self.before = before or [0] * buffers
        self.at, count = {}, list(self.before)
        start = sum(self.before)
        for i, n in enumerate(names):
            b = (start + i) % buffers
            self.at[n] = (b, count[b])
            count[b] += 1
        self.after = count
        self.each = [c - b for c, b in zip(count, self.before)]


class Part:

    def __init__(self, tiles, panels, halves, l):
        self.turns = dict(tile=tiles, panel=panels, half=halves)
        self.l = l

    def turn(self, kind, name):
        t = self.turns[kind]
        b, before = t.at[name]
        return b, before if self.l is None else self.l * t.each[b] + before


TILES_1 = Turns(FIRST_TILES, 4)
PANELS_1 = Turns(FIRST_PANELS, 2)
HALVES_1 = Turns([h for h, _ in FIRST_HALVES], SLOTS)
TILES_2 = Turns(LAYER_TILES, 4, TILES_1.after)
PANELS_2 = Turns(LAYER_PANELS, 2, PANELS_1.after)
HALVES_2 = Turns([h for h, _ in LAYER_HALVES], SLOTS, HALVES_1.after)
assert sum(PANELS_2.each) % 2 == 0 and sum(HALVES_2.each) % SLOTS == 0


def area_map(sizes):
    at, end = {}, 0
    for name, size in sizes:
        at[name] = (end, end + size)
        end += size
    return at, end


AREA_1, END_1 = area_map([
    ("qaT", 1024), ("kaT", 256), ("va", 256), ("qbT", 3072), ("kbT", 3072), ("vb", 3072), ("sga", 1024),
    ("sgb", 1024), ("mgt", 4096), ("L", 2 * 1536), ("PT", 2 * 1536), ("E", 2 * 3 * TOEP), ("yT", 2048)])
AREA_2, END_2 = area_map([
    ("En", H * TOEP), ("qT", 1024), ("kT", 512), ("vsw", 512), ("gt", 48), ("kcP", 1024), ("blk", 960),
    ("hx", 64), ("hy", 64), ("ht", 64), ("hgk", 32), ("hgv", 256), ("kcmpT", 32), ("vblk", 512), ("Lc", 240),
    ("Pc", 512), ("PcT", 512), ("u", 4 * 288), ("tz", 1024), ("acc", 1024), ("z", 1024), ("rT", 1024),
    ("vr", 1024), ("sgr", 1024), ("tg", 1024), ("PR", 768), ("or", 1024), ("mgt", 6144), ("brT", 3072), ("L", 768),
    ("PT", 768), ("y", 1024), ("tmp", 1024)])
AREA = max(END_1, END_2)


def block_kernel(nc, a, out):
    ctx = ExitStack()
    with ctx:
        def sb(name, *shape):
            return ctx.enter_context(nc.sbuf_tensor(name, [P, *shape], F32))

        def sem(name):
            return ctx.enter_context(nc.semaphore(name))

        ring = sb("ring", SLOTS, HALF)
        x = sb("x", NB, D)
        hT = sb("hT", KC, TOKENS)
        tok = sb("tok", NB, D)
        ident = sb("ident", P)
        decay = sb("decay", RET_H, TOKENS)
        rope = sb("rope", NB, 2, HD // 2)
        par = sb("par", PAR)
        first = sb("first", FIRST)
        cw = sb("cw", 4, TAPS)
        lnh = sb("lnh", 3, 4)
        stat = sb("stat", 256)
        area = sb("area", AREA)
        tile = [ctx.enter_context(nc.psum_tensor(f"tile{i}", [P, 512], F32)) for i in range(4)]
        panel = [ctx.enter_context(nc.psum_tensor(f"panel{i}", [P, 2, 512], F32)) for i in range(2)]
        bias_rows = nc.dram_tensor("bias_rows", (5, H, 512), F32, kind="Internal").ap()
        bias_copies = nc.dram_tensor("bias_copies", (5, H, P, 512), F32, kind="Internal").ap()

        def toeplitz(head, step, n):
            return bass.AP(tensor=bias_copies.tensor, offset=head * P * 512 + 127,
                           ap=[[511, P], [step * P * 512, n], [1, TOEP]])


        def one(name):
            s, e = AREA_1[name]
            return area[:, s:e]

        def two(name):
            s, e = AREA_2[name]
            return area[:, s:e]

        def pars(name):
            s, e = PAR_AT[name]
            return par[:, s:e]

        def st(s, *shape):
            n = int(np.prod(shape))
            v = stat[:, s:s + n]
            if len(shape) == 2:
                v = v.rearrange("p (a b) -> p a b", a=shape[0])
            return v

        ss, rstd = st(0, 2), st(2, 2)
        hs, hr = st(4, 2, 8), st(20, 2, 8)
        mxs = [st(36, 2, 3), st(224, 2, 3)]
        negmax = stat[:, 42:74].rearrange("p (b u) -> p b u", b=2)
        den = stat[:, 74:106].rearrange("p (b u) -> p b u", b=2)
        sinks = stat[:, 106:122].rearrange("p (b u) -> p b u", b=2)
        cmx, cden, coef_c = st(122, 2, 8), st(138, 2, 8), st(154, 2, 8)
        half_power = stat[:, 170:178]
        bns, bna = sb("bns", 8, 6), sb("bna", 8, 2)
        brs = st(178, 2, 4)
        cns, cna, crs = sb("cns", 2, 6), sb("cna", 2, 2), st(186, 2)
        coef = stat[:, 190:222].rearrange("p (b u) -> p b u", b=2)
        zero = stat[:, 222:223]
        low = stat[:, 223:224]

        loaded = sem("constants_loaded")
        x_loaded = sem("x_loaded")
        par_loaded = sem("layer_parameters_loaded")
        bmerge_loaded = sem("merge_bias_loaded")
        final_loaded = sem("final_gain_loaded")
        En_loaded = sem("layer_bias_loaded")
        E_loaded = [sem(f"head_bias{i}_loaded") for i in range(2)]
        E_used = sem("head_bias_used")
        half_loaded = [sem(f"half{i}_loaded") for i in range(SLOTS)]
        half_used = sem("half_used")
        tile_done = [sem(f"tile{i}_done") for i in range(4)]
        tile_evicted = [sem(f"tile{i}_evicted") for i in range(4)]
        panel_done = [sem(f"panel{i}_done") for i in range(2)]
        panel_evicted = [sem(f"panel{i}_evicted") for i in range(2)]
        pad_ready = sem("constant_fill_ready")
        rows_ready = sem("bias_rows_ready")
        rows_stored = sem("bias_rows_stored")
        copies_stored = sem("bias_copies_stored")
        squares = sem("row_squares_ready")
        rstd_ready = sem("row_rstd_ready")
        h_ready = sem("h_ready")
        head_sq = sem("head_squares_ready")
        head_sum = sem("head_sums_ready")
        head_rstd = sem("head_rstd_ready")
        head_normed = sem("heads_normed")
        gate_tanh = sem("gate_tanh_ready")
        merge_sum = sem("merge_bias_added")
        merge_tanh = sem("merge_tanh_ready")
        logits = sem("logits_ready")
        probs = sem("probs_ready")
        pv_done = sem("pv_done")
        sink_diff = sem("sink_minus_max_ready")
        sink_exp = sem("sink_exp_ready")
        y_ready = sem("y_ready")
        merged = sem("merged_ready")
        x_updated = sem("x_updated")
        cw_ready = sem("half_weights_ready")
        conv_tanh = sem("conv_tanh_ready")
        u_ready = sem("conv_input_ready")
        conv_ready = sem("conv_sum_ready")
        conv_stats = sem("conv_stats_ready")
        conv_rstd = sem("conv_rstd_ready")
        conv_normed = sem("conv_normed")
        conv_z = sem("conv_z_tanh_ready")
        pairs_ready = sem("token_pairs_ready")
        blocks_ready = sem("blocks_ready")
        hid_in = sem("gelu_argument_ready")
        hid_tanh = sem("gelu_tanh_ready")
        hid_ready = sem("hidden_ready")
        cmp_logits = sem("compressed_logits_ready")
        cmp_exp = sem("compressed_exp_ready")
        rot_ready = sem("rotated_ready")
        gr_tanh = sem("retention_gate_tanh_ready")
        kept_ready = sem("decayed_scores_ready")
        ret_stats = sem("retention_stats_ready")
        ret_rstd = sem("retention_rstd_ready")
        ret_ready = sem("retention_output_ready")
        branch_ready = sem("conv_branch_ready")
        relu_done = sem("relu_done")
        squared = sem("squares_of_relu_ready")
        stored = sem("output_stored")
        taken = sem("operands_taken")

        block = ctx.enter_context(nc.Block())
        part_1 = Part(TILES_1, PANELS_1, HALVES_1, None)

        def layer(l):
            return Part(TILES_2, PANELS_2, HALVES_2, l)

        def count(part, first_block, each, n):
            return n if part.l is None else part.l * each + (first_block + n)

        PER = dict(half_used=(len([1 for h, p in FIRST_HALVES if not last_half(h, p, FIRST_HALVES)]),
                              len([1 for h, p in LAYER_HALVES if not last_half(h, p, LAYER_HALVES)])))

        def wait_done(eng, sems, part, kind, name):
            b, before = part.turn(kind, name)
            eng.wait_ge(sems[b], before + 1)
            return b

        def tile_of(eng, part, name):
            return tile[wait_done(eng, tile_done, part, "tile", name)]

        def panel_of(eng, part, name):
            return panel[wait_done(eng, panel_done, part, "panel", name)]

        def tile_sem(part, name):
            return tile_evicted[part.turn("tile", name)[0]]

        def panel_sem(part, name):
            return panel_evicted[part.turn("panel", name)[0]]

        def wait_products(eng, part, u):
            per_kind = H - 1
            if u % H == H - 1:
                name = ("OA", "OB")[u // H] if part.l is None else f"O{u // H}"
                b, before = part.turn("panel", name)
                eng.wait_ge(panel_done[b], before + 1)
            else:
                n = (u // H) * per_kind + u % H + 1
                eng.wait_ge(pv_done, count(part, 2 * per_kind, 2 * per_kind + RET_H - 1,
                                           n + (0 if part.l is None else RET_H - 1)))

        def normed_out(v, part, i):
            c = coef[:, :, H * i:H * i + H]
            v.drain()
            v.reciprocal(c, den[:, :, H * i:H * i + H])
            v.drain()
            v.tensor_scalar(c, c, 0.5, None, ALU.mult)
            v.drain()
            ps = panel_of(v, part, ("OA", "OB")[i])
            to = tok[:, :, i * 512:(i + 1) * 512]
            gate = one(("sga", "sgb")[i]).rearrange("p (b n) -> p b n", b=2)
            for b in range(NB):
                v.tensor_tensor(to[:, b, :].rearrange("p (h d) -> p h d", h=H), ps[:, b, :].rearrange("p (h d) -> p h d", h=H),
                                c[:, b, :].unsqueeze(2).broadcast_to([P, H, HD]), ALU.mult)\
                 .then_inc(panel_sem(part, ("OA", "OB")[i]), 1)
            v.drain()
            for b in range(NB):
                v.tensor_tensor(to[:, b, :], to[:, b, :], gate[:, b, :], ALU.mult).then_inc(y_ready, 1)

        def sum_out(v, part, l, w):
            c = coef[:, :, H * w:H * w + H]
            gt = two("gt").rearrange("p (b h i) -> p b h i", b=2, h=H)
            y = two("y").rearrange("p (b n) -> p b n", b=2)
            tmp = two("tmp").rearrange("p (b n) -> p b n", b=2)
            v.wait_ge(probs, l * 16 + (16 + H * (w + 1)))
            ps = panel_of(v, part, f"O{w}")
            v.reciprocal(c, den[:, :, H * w:H * w + H])
            v.drain()
            v.scalar_tensor_tensor(c, gt[:, :, :, 1 + w], 1.0, c, ALU.add, ALU.mult)
            v.drain()
            for b in range(NB):
                v.tensor_tensor(tmp[:, b, :].rearrange("p (h d) -> p h d", h=H), ps[:, b, :].rearrange("p (h d) -> p h d", h=H),
                                c[:, b, :].unsqueeze(2).broadcast_to([P, H, HD]), ALU.mult).then_inc(panel_sem(part, f"O{w}"), 1)
            v.drain()
            for b in range(NB):
                e = v.tensor_tensor(y[:, b, :], y[:, b, :], tmp[:, b, :], ALU.add)
                if w == 1:
                    e.then_inc(y_ready, 1)

        @block.sync
        def _(sp):
            sp.dma_start(x[:, :, :], a["x"].rearrange("(b p) d -> p b d", p=P)).then_inc(x_loaded, 16)
            for name, to in (("ident", ident[:, :]), ("first", first[:, :]), ("decay", decay[:, :, :]),
                             ("rope", rope[:, :, :, :])):
                sp.dma_start(to, a[name]).then_inc(loaded, 16)
            onehot = one("mgt")[0:33, 0:2560]
            sp.dma_start(onehot[0:33, :], a["onehot"]).then_inc(loaded, 16)
            tabs = one("mgt")[0:32, 2560:2600]
            sp.dma_start(tabs[:, 0:32], a["rel_bias"]).then_inc(loaded, 16)
            sp.dma_start(tabs[:, 32:40], a["rel_table"]).then_inc(loaded, 16)
            sp.dma_start(par[:, :], a["par"][0]).then_inc(par_loaded, 16)

            def load_half(part, name, source, halves):
                i = [h for h, _ in halves].index(name)
                slot = part.turn("half", name)[0]
                if i >= SLOTS:
                    wait_used(part, *halves[i - SLOTS], halves)
                w = 4 * 280 if name.startswith("vsg") else 4 * 256 if name.startswith("kava") else HALF
                sp.dma_start(ring[:, slot, 0:w], source[:, 0:w]).then_inc(half_loaded[slot], 16)

            def wait_used(part, prev, p, halves):
                if p == "cmpH":
                    b, before = part.turn("tile", "cmpH")
                    sp.wait_ge(tile_done[b], before + 1)
                elif last_half(prev, p, halves):
                    b, before = part.turn("panel", p)
                    sp.wait_ge(panel_done[b], before + 1)
                else:
                    n = used_before(prev, halves)
                    sp.wait_ge(half_used, count(part, PER["half_used"][0], PER["half_used"][1], n + 1))

            def load_first(i):
                name = FIRST_HALVES[i][0]
                load_half(part_1, name, a["w_first"][i], FIRST_HALVES)
                if name == "mg0/0":
                    sp.dma_start(one("PT")[:, 0:2 * D], a["b_merge"].partition_broadcast(P)).then_inc(bmerge_loaded, 16)

            for i in range(8):
                load_first(i)
            for t in range(5):
                sp.wait_ge(rows_stored, 16 * 5)
                src = bass.AP(tensor=bias_rows.tensor, offset=t * H * 512, ap=[[512, H], [0, P], [1, 512]])
                sp.dma_start(bias_copies[t], src).then_inc(copies_stored, 16)
            for i in range(8, len(FIRST_HALVES) - 2):
                load_first(i)

            sp.wait_ge(copies_stored, 16 * 5)
            Es = one("E").rearrange("p (s t j) -> p s t j", s=2, t=3)
            for n in range(4 + H):
                if n >= 2:
                    sp.wait_ge(E_used, n - 1)
                if n < 4:
                    sp.dma_start(Es[:, n % 2, 0:2, :], toeplitz(2 * n, 1, 2)).then_inc(E_loaded[n % 2], 16)
                else:
                    sp.dma_start(Es[:, n % 2, :, :], toeplitz(H + n - 4, H, 3)).then_inc(E_loaded[n % 2], 16)
            for i in range(len(FIRST_HALVES) - 2, len(FIRST_HALVES)):
                load_first(i)
            b, before = PANELS_1.at["OB"]
            sp.wait_ge(panel_done[b], before + 1)
            sp.dma_start(two("En").rearrange("p (h j) -> p h j", h=H), toeplitz(4 * H, 1, H)).then_inc(En_loaded, 16)

            for i in range(SLOTS):
                name = LAYER_HALVES[i][0]
                prev, p = FIRST_HALVES[len(FIRST_HALVES) - SLOTS + i]
                slot = HALVES_2.at[name][0]
                wait_used(part_1, prev, p, FIRST_HALVES)
                sp.dma_start(ring[:, slot, :], a["w_layers"][i]).then_inc(half_loaded[slot], 16)

            with sp.Fori(0, LAYERS) as l:
                part = layer(l)
                for i, (name, p) in enumerate(LAYER_HALVES):
                    if i >= SLOTS:
                        load_half(part, name, a["w_layers"][l * N_HALVES + i], LAYER_HALVES)
                b, before = part.turn("panel", "ff7")
                sp.wait_ge(panel_done[b], before + 1)
                sp.dma_start(par[:, :], a["par"][l + 1]).then_inc(par_loaded, 16)
                for i in range(SLOTS):
                    name = LAYER_HALVES[i][0]
                    prev, p = LAYER_HALVES[len(LAYER_HALVES) - SLOTS + i]
                    slot = HALVES_2.at[name][0]
                    wait_used(part, prev, p, LAYER_HALVES)
                    sp.dma_start(ring[:, slot, :], a["w_layers"][l * N_HALVES + (N_HALVES + i)]).then_inc(half_loaded[slot], 16)

            sp.dma_start(two("mgt")[:, 0:D], a["norm_final"].partition_broadcast(P)).then_inc(final_loaded, 16)
            for b in range(NB):
                sp.wait_ge(x_updated, X_UPDATES + b + 1)
                sp.dma_start(out.rearrange("(b p) d -> b p d", p=P)[b], tok[:, b, :]).then_inc(stored, 16)
            sp.wait_ge(stored, 32)
            sp.wait_ge(par_loaded, 16 * (LAYERS + 1))
            for s in range(SLOTS):
                sp.wait_ge(half_loaded[s], 16 * (HALVES_2.after[s] + (LAYERS - 1) * HALVES_2.each[s] + 1))

        @block.tensor
        def _(pe):
            def tile_for(part, name):
                b, before = part.turn("tile", name)
                if part.l is not None or before:
                    pe.wait_ge(tile_evicted[b], before)
                return tile[b], tile_done[b]

            def panel_for(part, name):
                b, before = part.turn("panel", name)
                if part.l is not None or before:
                    pe.wait_ge(panel_evicted[b], before * 2)
                return panel[b], panel_done[b]

            def wait_evicted(part, name):
                b, before = part.turn("tile", name)
                pe.wait_ge(tile_evicted[b], before + 1)

            def wait_half(part, name):
                slot, before = part.turn("half", name)
                pe.wait_ge(half_loaded[slot], before * 16 + 16)
                return slot

            def rows_out(part, name, lhs, halves, width=512, of=None):
                ps, done = panel_for(part, name)
                for i, half in enumerate(halves):
                    slot = wait_half(part, half)
                    w = ring[:, slot, 0:4 * width].rearrange("p (k n) -> p k n", k=4)
                    for k in range(4):
                        for b in range(NB):
                            last = i == len(halves) - 1 and k == 3
                            mm = pe.matmul(ps[:, b, 0:width], lhs(4 * i + k, b), w[:, k, :],
                                           start=(i == 0 and k == 0), stop=last)
                    if i < len(halves) - 1:
                        mm.then_inc(half_used, 1)
                mm.then_inc(done, 1)

            def columns_out(part, name):
                ps, done = panel_for(part, name)
                slots = [wait_half(part, f"{name}/{i}") for i in range(2)]
                for m in range(4):
                    for k in range(KC):
                        w = ring[:, slots[k // 4], (k % 4) * 512 + m * P:(k % 4) * 512 + (m + 1) * P]
                        mm = pe.matmul(ps[:, m // 2, (m % 2) * TOKENS:(m % 2 + 1) * TOKENS], w, hT[:, k, :],
                                       start=(k == 0), stop=(k == KC - 1))
                mm.then_inc(done, 1)

            def turn(part, name, source, n=4, rows=P):
                ps, done = tile_for(part, name)
                for i in range(n):
                    mm = pe.transpose(ps[0:rows, i * P:(i + 1) * P], source(i), ident[:, :])
                mm.then_inc(done, 1)

            def turn_rows(part, name, ready, base):
                for b in range(NB):
                    pe.wait_ge(ready, base + b + 1 if part.l is None else base + (b + 1))
                    for i in range(2):
                        turn(part, f"{name}{b}{i}", lambda c: tok[:, b, (4 * i + c) * P:(4 * i + c + 1) * P])

            def operand_ready(part, name):
                for b in range(NB):
                    for i in range(2):
                        wait_evicted(part, f"{name}{b}{i}")

            lhs_h = lambda k, b: hT[:, k, b * P:(b + 1) * P]
            two_halves = lambda n: [f"{n}/0", f"{n}/1"]

            part = part_1
            onehot = one("mgt")[0:33, 0:2560].rearrange("p (t j) -> p t j", t=5)
            tabs = one("mgt")[0:33, 2560:2600]
            pe.wait_ge(loaded, 16 * 7)
            pe.wait_ge(pad_ready, PADS)
            for t in range(5):
                ps, done = tile_for(part, f"bias{t}")
                pe.matmul(ps[0:H, :], tabs[:, t * H:(t + 1) * H], onehot[:, t, :], start=True, stop=True).then_inc(done, 1)
            turn_rows(part, "x", h_ready, 0)
            operand_ready(part, "x")
            staged = tok[:, :, :].rearrange("p b (s n) -> p b s n", s=2)

            def turn_heads(n):
                p = NORMED[n]
                for b in range(NB):
                    pe.wait_ge(head_normed, NB * n + b + 1)
                    turn(part, f"{p}{b}", lambda c: staged[:, b, n % 2, c * P:(c + 1) * P], n=1 if p == "kava" else 4)

            for n, p in enumerate(FIRST_PANELS[:17]):
                rows_out(part, p, lhs_h, two_halves(p), 256 if p == "kava" else 512)
                if 1 <= n <= len(NORMED):
                    turn_heads(n - 1)

            qaT, kaT = one("qaT").rearrange("p (c t) -> p c t", c=4), one("kaT")
            qbT = one("qbT").rearrange("p (g c t) -> p g c t", g=3, c=4)
            kbT = one("kbT").rearrange("p (g c t) -> p g c t", g=3, c=4)
            va = one("va").rearrange("p (b n) -> p b n", b=2)
            vb = one("vb").rearrange("p (g b n) -> p g b n", g=3, b=2)

            def head_rows(h):
                s = HD * (h // 4)
                return slice(s, s + HD), h % 4

            def scores_first(kind, h, g):
                ps, done = tile_for(part, f"S{kind}{h}{g}")
                for b in range(NB):
                    if kind == "A":
                        r, c = head_rows(h)
                        q, k = qaT[r, c, b * P:(b + 1) * P], kaT[r, :]
                    else:
                        r, c = slice(HD * (h % 2), HD * (h % 2) + HD), h // 2
                        q, k = qbT[r, g, c, b * P:(b + 1) * P], kbT[r, g, c, :]
                    mm = pe.matmul(ps[:, b * TOKENS:(b + 1) * TOKENS], q, k, start=True, stop=True)
                mm.then_inc(done, 1)

            units = units_first()
            opened = {}
            for i in range(len(units) + 1):
                if i == 0:
                    for p in NORMED:
                        for b in range(NB):
                            wait_evicted(part, f"{p}{b}")
                if i < len(units):
                    kind, h, n = units[i]
                    for g in range(n):
                        scores_first(kind, h, g)
                if i >= 1:
                    u = i - 1
                    kind, h, n = units[u]
                    if h == 0:
                        opened[kind] = panel_for(part, "O" + kind)
                        if kind == "A":
                            for p in ("kava", "vb0", "vb1", "vb2"):
                                bp, before = part.turn("panel", p)
                                pe.wait_ge(panel_evicted[bp], before * 2 + 2)
                    L = one("L").rearrange("p (s b j) -> p s b j", s=2, b=2)[:, u % 2]
                    PT = one("PT").rearrange("p (s g j) -> p s g j", s=2, g=3)[:, u % 2]
                    pe.wait_ge(probs, u + 1)
                    for g in range(n):
                        turn(part, f"T{kind}{h}{g}",
                             lambda c: L[:, c // 2, g * TOKENS + (c % 2) * P:g * TOKENS + (c % 2 + 1) * P])
                    ps, done = opened[kind]
                    for g in range(n):
                        wait_evicted(part, f"T{kind}{h}{g}")
                    for b in range(NB):
                        for g in range(n):
                            for k in range(2):
                                v = va[:, k, HD * (h // 4):HD * (h // 4) + HD] if kind == "A" else \
                                    vb[:, g, k, h * HD:(h + 1) * HD]
                                mm = pe.matmul(ps[:, b, h * HD:(h + 1) * HD], PT[:, g, (2 * b + k) * P:(2 * b + k + 1) * P], v,
                                               start=(g == 0 and k == 0), stop=(g == n - 1 and k == 1))
                    mm.then_inc(done if h == H - 1 else pv_done, 1)

            for t, name in enumerate(("yA", "yB")):
                for b in range(NB):
                    pe.wait_ge(y_ready, NB * t + b + 1)
                    turn(part, f"{name}{b}", lambda c: staged[:, b, t, c * P:(c + 1) * P])
            yT = one("yT").rearrange("p (i c t) -> p i c t", i=2, c=4)
            for t, name in enumerate(("yA", "yB")):
                for b in range(NB):
                    wait_evicted(part, f"{name}{b}")
                for c in range(2):
                    rows_out(part, f"br{t}{c}", lambda k, b: yT[:, t, k, b * P:(b + 1) * P], [f"br{t}{c}/0"])
            turn_rows(part, "m", merged, 0)
            operand_ready(part, "m")
            for c in range(2):
                rows_out(part, f"wo{c}", lhs_h, two_halves(f"wo{c}"))

            with pe.Fori(0, LAYERS) as l:
                part = layer(l)
                turn_rows(part, "x", h_ready, l * 4 + 2)
                operand_ready(part, "x")
                for p in ("cb", "ca", "q", "k4"):
                    columns_out(part, p)
                rows_out(part, "vsg", lhs_h, two_halves("vsg"), 280)

                ps, done = tile_for(part, "cmpH")
                pe.wait_ge(blocks_ready, l * 2 + 2)
                for i, half in enumerate(("w1k", "w1v")):
                    slot = wait_half(part, half)
                    blk = two("blk").rearrange("p (i j n) -> p i j n", i=2, j=16)[:, i]
                    for j in range(16):
                        mm = pe.matmul(ps[:, 32 * i:32 * i + 30], ring[:, slot, j * P:(j + 1) * P], blk[:, j, :],
                                       start=(j == 0), stop=(j == 15))
                mm.then_inc(done, 1)

                rows_out(part, "qkr", lhs_h, two_halves("qkr"))
                rows_out(part, "vr", lhs_h, two_halves("vr"))
                staged = tok[:, :, :].rearrange("p b (s n) -> p b s n", s=2)
                for b in range(NB):
                    pe.wait_ge(rot_ready, l * 2 + (b + 1))
                    turn(part, f"rot{b}", lambda c: staged[:, b, 0, c * P:(c + 1) * P])

                ps, done = tile_for(part, "cmp2")
                pe.wait_ge(hid_ready, l * 2 + 2)
                pe.matmul(ps[:, 0:30], pars("w2k"), two("hgk")[:, 0:30], start=True, stop=True)
                hgv = two("hgv").rearrange("p (g n) -> p g n", g=2)
                for g in range(2):
                    mm = pe.matmul(ps[:, 64 + g * HD:64 + (g + 1) * HD], hgv[:, g, :], pars("w2v"), start=True, stop=True)
                mm.then_inc(done, 1)
                rows_out(part, "gr", lhs_h, two_halves("gr"))

                wait_evicted(part, "cmp2")
                qT = two("qT").rearrange("p (c t) -> p c t", c=4)
                bq, before = part.turn("panel", "q")
                pe.wait_ge(panel_evicted[bq], before * 2 + 2)
                for g in range(2):
                    ps, done = tile_for(part, f"cmpS{g}")
                    for b in range(NB):
                        for i in range(4):
                            r, c = head_rows(4 * g + i)
                            s = (b * 4 + i) * N_CMP
                            mm = pe.matmul(ps[:, s:s + N_CMP], qT[r, c, b * P:(b + 1) * P],
                                           two("kcmpT")[r, g * N_CMP:(g + 1) * N_CMP], start=True, stop=True)
                    mm.then_inc(done, 1)
                rows_out(part, "mg0", lhs_h, two_halves("mg0"))

                pe.wait_ge(cmp_exp, l + 1)
                Pc = two("Pc").rearrange("p (s n) -> p s n", s=4)
                turn(part, "PcT", lambda c: Pc[:, c, :])
                for b in range(NB):
                    wait_evicted(part, f"rot{b}")
                rT = two("rT").rearrange("p (c t) -> p c t", c=4)

                def ret_scores(h):
                    ps, done = tile_for(part, f"R{h}")
                    r = slice(HD * (h % 2), HD * (h % 2) + HD)
                    pe.matmul(ps[:, 0:TOKENS], rT[r, 2 + h // 2, 0:P], rT[r, h // 2, :], start=True, stop=True)
                    pe.matmul(ps[:, TOKENS:TOKENS + P], rT[r, 2 + h // 2, P:TOKENS], rT[r, h // 2, P:TOKENS],
                              start=True, stop=True).then_inc(done, 1)

                ret_scores(0)
                ps_c, done_c = panel_for(part, "Oc")
                wait_evicted(part, "PcT")
                PcT = two("PcT").rearrange("p (s q) -> p s q", s=4)
                vblk = two("vblk").rearrange("p (g n) -> p g n", g=2)
                for b in range(NB):
                    for g in range(2):
                        mm = pe.matmul(ps_c[:, b, g * 4 * HD:(g + 1) * 4 * HD], PcT[:, 2 * b + g, :], vblk[:, g, :],
                                       start=True, stop=True)
                mm.then_inc(done_c, 1)

                vr = two("vr").rearrange("p (b n) -> p b n", b=2)
                ps_r, done_r = panel_for(part, "Or")
                bv, before = part.turn("panel", "vr")
                pe.wait_ge(panel_evicted[bv], before * 2 + 2)
                for h in range(RET_H):
                    if h + 1 < RET_H:
                        ret_scores(h + 1)
                    pe.wait_ge(kept_ready, l * RET_H + (h + 1))
                    PR = two("PR").rearrange("p (s n) -> p s n", s=2)[:, h % 2]
                    hv = slice(h * P, (h + 1) * P)
                    pe.matmul(ps_r[:, 0, hv], PR[:, 0:P], vr[:, 0, hv], start=True, stop=True)
                    pe.matmul(ps_r[:, 1, hv], PR[:, P:TOKENS], vr[:, 0, hv], start=True, stop=False)
                    mm = pe.matmul(ps_r[:, 1, hv], PR[:, TOKENS:TOKENS + P], vr[:, 1, hv], start=False, stop=True)
                    mm.then_inc(pv_done if h < RET_H - 1 else done_r, 1)
                for i in range(1, 4):
                    rows_out(part, f"mg{i}", lhs_h, two_halves(f"mg{i}"))
                for b in range(NB):
                    pe.wait_ge(ret_ready, l * 2 + (b + 1))
                    turn(part, f"oR{b}", lambda c: two("or").rearrange("p (b n) -> p b n", b=2)[:, b, c * P:(c + 1) * P])
                rows_out(part, "mg4", lhs_h, two_halves("mg4"))
                pe.wait_ge(conv_ready, l + 1)
                acc = two("acc").rearrange("p (c t) -> p c t", c=4)
                for b in range(NB):
                    turn(part, f"cv{b}", lambda c: acc[:, c, b * P:(b + 1) * P])
                rows_out(part, "mg5", lhs_h, two_halves("mg5"))
                for b in range(NB):
                    pe.wait_ge(conv_normed, l * 2 + (b + 1))
                    turn(part, f"cz{b}", lambda c: staged[:, b, 1, c * P:(c + 1) * P])

                kT = two("kT").rearrange("p (i t) -> p i t", i=2)
                vsw = two("vsw").rearrange("p (b n) -> p b n", b=2)
                units = units_layer()
                bk, before = part.turn("panel", "k4")
                pe.wait_ge(panel_evicted[bk], before * 2 + 2)
                bk, before = part.turn("panel", "vsg")
                pe.wait_ge(panel_evicted[bk], before * 2 + 2)
                for i in range(len(units) + 1):
                    if i < len(units):
                        kind, h, _ = units[i]
                        ps, done = tile_for(part, f"S{kind}{h}0")
                        r, c = head_rows(h)
                        w = 0 if kind == "s" else 1
                        pe.matmul(ps[:, 0:P], qT[r, c, 0:P], kT[r, w, 0:P], start=True, stop=True)
                        pe.matmul(ps[:, P:3 * P], qT[r, c, P:TOKENS], kT[r, w, :], start=True, stop=True).then_inc(done, 1)
                    if i >= 1:
                        u = i - 1
                        kind, h, _ = units[u]
                        w = 0 if kind == "s" else 1
                        if h == 0:
                            ps_o, done_o = panel_for(part, f"O{w}")
                        L = two("L").rearrange("p (s j) -> p s j", s=2)[:, u % 2]
                        PT = two("PT").rearrange("p (s j) -> p s j", s=2)[:, u % 2]
                        pe.wait_ge(probs, l * 16 + (16 + u + 1))
                        turn(part, f"T{kind}{h}0", lambda c: L[:, c * P:(c + 1) * P], n=3)
                        wait_evicted(part, f"T{kind}{h}0")
                        hd = slice(h * HD, (h + 1) * HD)
                        s = w * P + HD * (h // 4)
                        pe.matmul(ps_o[:, 0, hd], PT[:, 0:P], vsw[:, 0, s:s + HD], start=True, stop=True)
                        pe.matmul(ps_o[:, 1, hd], PT[:, P:2 * P], vsw[:, 0, s:s + HD], start=True, stop=False)
                        mm = pe.matmul(ps_o[:, 1, hd], PT[:, 2 * P:3 * P], vsw[:, 1, s:s + HD], start=False, stop=True)
                        mm.then_inc(done_o if h == H - 1 else pv_done, 1)

                for b in range(NB):
                    pe.wait_ge(y_ready, l * 2 + (4 + b + 1))
                    turn(part, f"y{b}", lambda c: two("y").rearrange("p (b n) -> p b n", b=2)[:, b, c * P:(c + 1) * P])
                for b in range(NB):
                    wait_evicted(part, f"y{b}")
                    wait_evicted(part, f"oR{b}")
                pe.wait_ge(branch_ready, l + 1)
                brT = two("brT").rearrange("p (i c t) -> p i c t", i=3, c=4)
                for i in range(3):
                    for c in range(2):
                        rows_out(part, f"br{i}{c}", lambda k, b: brT[:, i, k, b * P:(b + 1) * P], [f"br{i}{c}/0"])
                turn_rows(part, "m", merged, l * 2 + 2)
                operand_ready(part, "m")
                for c in range(2):
                    rows_out(part, f"wo{c}", lhs_h, two_halves(f"wo{c}"))
                turn_rows(part, "z", h_ready, l * 4 + 4)
                operand_ready(part, "z")
                for i in range(FF_PANELS):
                    columns_out(part, f"ff{i}")
                ffT = area[:, AREA_2["mgt"][0]:AREA_2["mgt"][0] + 8192].rearrange("p (k t) -> p k t", k=32)
                pe.wait_ge(squared, l * 16 + 16)
                for c in range(2):
                    rows_out(part, f"down{c}", lambda k, b: ffT[:, k, b * P:(b + 1) * P], [f"down{c}/{i}" for i in range(8)])

        @block.scalar
        def _(act):
            def row_squares(b, n):
                return act.activation(tok[:, b, :], x[:, b, :], ACT.Square, accum_out=ss[:, b:b + 1]).then_inc(squares, 1)

            part = part_1
            act.wait_ge(x_loaded, 16)
            for b in range(NB):
                row_squares(b, b)
            rows = area[:, AREA_1["E"][0]:AREA_1["E"][0] + 2560].rearrange("p (t j) -> p t j", t=5)
            for t in range(5):
                ps = tile_of(act, part, f"bias{t}")
                act.activation(rows[0:H, t, :], ps[0:H, :], ACT.Copy).then_inc(tile_sem(part, f"bias{t}"), 1)
            for t in range(5):
                b, before = part.turn("tile", f"bias{t}")
                act.wait_ge(tile_evicted[b], before + 1)
                act.dma_start(bias_rows[t], rows[0:H, t, :]).then_inc(rows_stored, 16)

            squares_of = one("L").rearrange("p (b n) -> p b n", b=6)
            gain = dict(qa=0, kava=1, qb0=2, qb1=2, qb2=2, kb0=3, kb1=3, kb2=3)

            def evict_heads(n):
                p = NORMED[n]
                col = 8 + gain[p]
                for b in range(NB):
                    ps = tile_of(act, part, f"{p}{b}")
                    if n == 0 and b == 0:
                        act.wait_ge(cw_ready, 1)
                    if p == "kava":
                        to, w = one("kaT")[:, b * P:(b + 1) * P], P
                        src = ps[:, 0:P]
                    else:
                        g = int(p[2]) if len(p) == 3 else 0
                        region = "qaT" if p == "qa" else p[0:2] + "T"
                        base = AREA_1[region][0] + g * 1024
                        to = area[:, base:base + 1024].rearrange("p (c t) -> p c t", c=4)[:, :, b * P:(b + 1) * P]
                        src = ps[:, :].rearrange("p (c t) -> p c t", c=4)
                    act.activation(to, src, ACT.Identity, scale=first[:, col:col + 1])\
                       .then_inc(tile_sem(part, f"{p}{b}"), 1)

            act.wait_ge(pad_ready, PADS)
            for n, p in enumerate(FIRST_PANELS[:17]):
                ps = panel_of(act, part, p)
                if n < len(NORMED):
                    for b in range(NB):
                        w = P if p == "kava" else 512
                        if n >= 1:
                            act.wait_ge(head_sum, NB * (n - 1) + b + 1)
                        act.activation(squares_of[:, b, 0:w], ps[:, b, 0:w], ACT.Square).then_inc(head_sq, 1)
                elif p in ("vb0", "vb1", "vb2"):
                    g = int(p[2])
                    to = one("vb").rearrange("p (g b n) -> p g b n", g=3, b=2)
                    for b in range(NB):
                        act.activation(to[:, g, b, :], ps[:, b, :], ACT.Copy).then_inc(panel_sem(part, p), 1)
                elif p in ("ga", "gb"):
                    to = one("mgt").rearrange("p (b n) -> p b n", b=8)
                    for b in range(NB):
                        act.activation(to[:, b + 2 * (p == "gb"), :], ps[:, b, :], ACT.Tanh, scale=0.5).then_inc(gate_tanh, 1)
                else:
                    c = int(p[2])
                    to = one("mgt").rearrange("p (b n) -> p b n", b=2)
                    src = tok[:, :, :].rearrange("p b (s n) -> p b s n", s=2)
                    if c == 0:
                        bg, before = part.turn("panel", "gb")
                        act.wait_ge(panel_evicted[bg], before * 2 + 2)
                    for b in range(NB):
                        act.wait_ge(merge_sum, NB * c + b + 1)
                        act.activation(to[:, b, c * 512:(c + 1) * 512], src[:, b, c % 2, :], ACT.Tanh, scale=0.5)\
                           .then_inc(merge_tanh, 1)
                if 1 <= n <= len(NORMED):
                    evict_heads(n - 1)

            units = units_first()

            def exp_first(u):
                kind, h, n = units[u]
                L = one("L").rearrange("p (s b j) -> p s b j", s=2, b=2)[:, u % 2]
                act.wait_ge(logits, u + 1)
                for b in range(NB):
                    e = act.activation(L[:, b, 0:n * TOKENS], L[:, b, 0:n * TOKENS], ACT.Exp, bias=negmax[:, b, u:u + 1],
                                       accum_out=den[:, b, u:u + 1])
                e.then_inc(probs, 1)

            exp_first(0)
            for u in range(len(units)):
                kind, h, n = units[u]
                if u + 1 < len(units):
                    exp_first(u + 1)
                PT = one("PT").rearrange("p (s g j) -> p s g j", s=2, g=3)[:, u % 2]
                if u >= 2:
                    wait_products(act, part, u - 2)
                for g in (0, 2)[:n]:
                    if g < n:
                        ps = tile_of(act, part, f"T{kind}{h}{g}")
                        act.activation(PT[:, g, :], ps[:, :], ACT.Copy).then_inc(tile_sem(part, f"T{kind}{h}{g}"), 1)
                if u == H:
                    act.wait_ge(sink_diff, 1)
                    act.activation(sinks[:, :, :], sinks[:, :, :], ACT.Exp).then_inc(sink_exp, 1)

            yT = one("yT").rearrange("p (i c t) -> p i c t", i=2, c=4)
            for t, name in enumerate(("yA", "yB")):
                for b in range(NB):
                    ps = tile_of(act, part, f"{name}{b}")
                    act.activation(yT[:, t, :, b * P:(b + 1) * P], ps[:, :].rearrange("p (c t) -> p c t", c=4), ACT.Copy)\
                       .then_inc(tile_sem(part, f"{name}{b}"), 1)

            def evict_merged(part):
                for b in range(NB):
                    for i in range(2):
                        ps = tile_of(act, part, f"m{b}{i}")
                        act.activation(hT[:, 4 * i:4 * i + 4, b * P:(b + 1) * P], ps[:, :].rearrange("p (c t) -> p c t", c=4),
                                       ACT.Copy, scale=0.5).then_inc(tile_sem(part, f"m{b}{i}"), 1)

            evict_merged(part)

            with act.Fori(0, LAYERS) as l:
                part = layer(l)
                act.wait_ge(x_updated, l * 2 + 1)
                for b in range(NB):
                    row_squares(b, 0)
                tz = two("tz").rearrange("p (b n) -> p b n", b=2)
                ps = panel_of(act, part, "cb")
                for b in range(NB):
                    act.activation(tz[:, b, :], ps[:, b, :], ACT.Tanh, scale=0.5).then_inc(panel_sem(part, "cb"), 1)
                qT = two("qT").rearrange("p (b n) -> p b n", b=2)
                ps = panel_of(act, part, "q")
                for b in range(NB):
                    act.activation(qT[:, b, :], ps[:, b, :], ACT.Copy, scale=HD ** -0.5).then_inc(panel_sem(part, "q"), 1)
                ps = panel_of(act, part, "k4")
                act.activation(two("kT"), ps[:, 1, :], ACT.Copy).then_inc(panel_sem(part, "k4"), 1)
                ps = panel_of(act, part, "vsg")
                vsw = two("vsw").rearrange("p (b n) -> p b n", b=2)
                gt = two("gt").rearrange("p (b n) -> p b n", b=2)
                for b in range(NB):
                    act.activation(vsw[:, b, :], ps[:, b, 0:256], ACT.Copy)
                    act.activation(gt[:, b, :], ps[:, b, 256:280], ACT.Tanh, scale=0.5).then_inc(panel_sem(part, "vsg"), 1)
                act.wait_ge(hid_in, l + 1)
                act.activation(two("ht"), two("hy"), ACT.Tanh, scale=GELU_C).then_inc(hid_tanh, 1)
                ps = panel_of(act, part, "vr")
                vr = two("vr").rearrange("p (b n) -> p b n", b=2)
                for b in range(NB):
                    act.activation(vr[:, b, :], ps[:, b, :], ACT.Copy).then_inc(panel_sem(part, "vr"), 1)
                rT = two("rT").rearrange("p (c t) -> p c t", c=4)
                for b in range(NB):
                    ps = tile_of(act, part, f"rot{b}")
                    act.activation(rT[:, :, b * P:(b + 1) * P], ps[:, :].rearrange("p (c t) -> p c t", c=4), ACT.Copy)\
                       .then_inc(tile_sem(part, f"rot{b}"), 1)
                ps = tile_of(act, part, "cmp2")
                act.activation(two("kcmpT")[:, 0:30], ps[:, 0:30], ACT.Copy, scale=0.5)
                vblk = two("vblk").rearrange("p (g i d) -> p g i d", g=2, i=4)
                for i in range(4):
                    r = slice(32 * i, 32 * i + 32)
                    e = act.activation(vblk[r, :, i, :], ps[r, 64:64 + 2 * HD].rearrange("p (g d) -> p g d", g=2),
                                       ACT.Copy, scale=0.5)
                e.then_inc(tile_sem(part, "cmp2"), 1)
                ps = panel_of(act, part, "gr")
                tg = two("tg").rearrange("p (b n) -> p b n", b=2)
                for b in range(NB):
                    act.activation(tg[:, b, :], ps[:, b, :], ACT.Tanh, scale=0.5).then_inc(gr_tanh, 1)
                act.wait_ge(cmp_logits, l + 1)
                Pc = two("Pc").rearrange("p (s n) -> p s n", s=16)[:, :, 0:N_CMP]
                act.activation(Pc, two("Lc").rearrange("p (s n) -> p s n", s=16), ACT.Exp).then_inc(cmp_exp, 1)
                mgt = two("mgt").rearrange("p (b n) -> p b n", b=2)

                def gates(i):
                    ps = panel_of(act, part, f"mg{i}")
                    for b in range(NB):
                        act.activation(mgt[:, b, i * 512:(i + 1) * 512], ps[:, b, :], ACT.Tanh, scale=0.5)\
                           .then_inc(panel_sem(part, f"mg{i}"), 1)

                gates(0)
                ps = tile_of(act, part, "PcT")
                act.activation(two("PcT"), ps[:, :], ACT.Copy).then_inc(tile_sem(part, "PcT"), 1)
                for i in range(1, 6):
                    gates(i)
                z = two("z").rearrange("p (c t) -> p c t", c=4)
                for b in range(NB):
                    ps = tile_of(act, part, f"cz{b}")
                    for c in range(4):
                        e = act.activation(z[:, c, b * P:(b + 1) * P], ps[:, c * P:(c + 1) * P], ACT.Identity,
                                           scale=lnh[:, 0, c:c + 1], bias=lnh[:, 1, c:c + 1])
                    e.then_inc(tile_sem(part, f"cz{b}"), 1)
                for b in range(NB):
                    bz, before = part.turn("tile", f"cz{b}")
                    act.wait_ge(tile_evicted[bz], before + 1)
                act.activation(two("tz"), two("z"), ACT.Tanh).then_inc(conv_z, 1)

                units = units_layer()

                def exp_layer(u):
                    L = two("L").rearrange("p (s j) -> p s j", s=2)[:, u % 2]
                    act.wait_ge(logits, l * 16 + (16 + u + 1))
                    act.activation(L[:, 0:P], L[:, 0:P], ACT.Exp, bias=negmax[:, 0, u:u + 1], accum_out=den[:, 0, u:u + 1])
                    act.activation(L[:, P:3 * P], L[:, P:3 * P], ACT.Exp, bias=negmax[:, 1, u:u + 1],
                                   accum_out=den[:, 1, u:u + 1]).then_inc(probs, 1)

                exp_layer(0)
                for u in range(len(units)):
                    kind, h, _ = units[u]
                    if u + 1 < len(units):
                        exp_layer(u + 1)
                    PT = two("PT").rearrange("p (s j) -> p s j", s=2)[:, u % 2]
                    if u >= 2:
                        wait_products(act, part, u - 2)
                    ps = tile_of(act, part, f"T{kind}{h}0")
                    act.activation(PT, ps[:, 0:3 * P], ACT.Copy).then_inc(tile_sem(part, f"T{kind}{h}0"), 1)
                brT = two("brT").rearrange("p (i c t) -> p i c t", i=3, c=4)
                for b in range(NB):
                    ps = tile_of(act, part, f"y{b}")
                    act.activation(brT[:, 0, :, b * P:(b + 1) * P], ps[:, :].rearrange("p (c t) -> p c t", c=4),
                                   ACT.Copy, scale=0.5).then_inc(tile_sem(part, f"y{b}"), 1)
                evict_merged(part)
                act.wait_ge(x_updated, l * 2 + 2)
                for b in range(NB):
                    row_squares(b, 0)
                ffT = area[:, AREA_2["mgt"][0]:AREA_2["mgt"][0] + 8192].rearrange("p (k t) -> p k t", k=16)
                rr = two("y")
                for i in range(FF_PANELS):
                    s = (i % 2) * 512
                    ps = panel_of(act, part, f"ff{i}")
                    act.activation(rr[:, s:s + 512], ps[:, 0, :], ACT.Relu).then_inc(panel_sem(part, f"ff{i}"), 1)
                    act.drain()
                    act.activation(ffT[:, 2 * i, :], rr[:, s:s + 512], ACT.Square).then_inc(squared, 1)
            act.wait_ge(x_updated, X_UPDATES)
            for b in range(NB):
                row_squares(b, 0)

        @block.vector
        def _(v):
            part = part_1
            v.memset(one("mgt")[32:33, 2560:2600], 1.0).then_inc(pad_ready, 1)
            v.memset(zero, 0.0).then_inc(pad_ready, 1)
            v.memset(low, -3.0e38).then_inc(pad_ready, 1)
            v.memset(half_power, -0.5).then_inc(pad_ready, 1)
            v.wait_ge(loaded, 16 * 7)
            for c in (8, 10):
                e = v.tensor_scalar(first[:, c:c + 1], first[:, c:c + 1], HD ** -0.5, None, ALU.mult)
            e.then_inc(cw_ready, 1)

            def rows_normed(part, base, tiles, gain):
                for b in range(NB):
                    v.wait_ge(rstd_ready, base + 1)
                    v.tensor_scalar(tok[:, b, :], x[:, b, :], rstd[:, b:b + 1], None, ALU.mult).then_inc(h_ready, 1)
                for b in range(NB):
                    for i in range(2):
                        ps = tile_of(v, part, f"{tiles}{b}{i}")
                        v.tensor_tensor(hT[:, 4 * i:4 * i + 4, b * P:(b + 1) * P], ps[:, :].rearrange("p (c t) -> p c t", c=4),
                                        gain[:, 4 * i:4 * i + 4].unsqueeze(2).broadcast_to([P, 4, P]), ALU.mult)\
                         .then_inc(tile_sem(part, f"{tiles}{b}{i}"), 1)

            rows_normed(part, 0, "x", first[:, 0:8])
            squares_of = one("L").rearrange("p (b n) -> p b n", b=6)
            staged = tok[:, :, :].rearrange("p b (s n) -> p b s n", s=2)
            for n, p in enumerate(FIRST_PANELS[:17]):
                if n < len(NORMED):
                    nh = 2 if p == "kava" else 8
                    for b in range(NB):
                        v.wait_ge(head_sq, NB * n + b + 1)
                        if n >= 1:
                            v.wait_ge(head_rstd, n)
                        v.tensor_reduce(hs[:, b, 0:nh], squares_of[:, b, 0:nh * HD].rearrange("p (h d) -> p h d", d=HD),
                                        AX.X, ALU.add).then_inc(head_sum, 1)
                    ps = panel_of(v, part, p)
                    v.wait_ge(head_rstd, n + 1)
                    for b in range(NB):
                        if n >= 2:
                            tile_of(v, part, f"{NORMED[n - 2]}{b}")
                        e = v.tensor_tensor(staged[:, b, n % 2, 0:nh * HD].rearrange("p (h d) -> p h d", d=HD),
                                            ps[:, b, 0:nh * HD].rearrange("p (h d) -> p h d", d=HD),
                                            hr[:, b, 0:nh].unsqueeze(2).broadcast_to([P, nh, HD]), ALU.mult)
                        e.then_inc(head_normed, 1)
                        if p == "kava":
                            va = one("va").rearrange("p (b n) -> p b n", b=2)
                            v.tensor_copy(va[:, b, :], ps[:, b, P:2 * P])\
                             .then_inc(panel_sem(part, p), 1)
                    if p != "kava":
                        for b in range(NB):
                            v.wait_ge(head_normed, NB * n + b + 1)
                            v.sem_inc(panel_sem(part, p), 1)
                elif p in ("ga", "gb"):
                    ps = panel_of(v, part, p)
                    i = int(p == "gb")
                    t = one("mgt").rearrange("p (b n) -> p b n", b=8)
                    to = one("sga" if p == "ga" else "sgb").rearrange("p (b n) -> p b n", b=2)
                    for b in range(NB):
                        v.wait_ge(gate_tanh, NB * i + b + 1)
                        v.scalar_tensor_tensor(to[:, b, :], t[:, b + 2 * i, :], 1.0, ps[:, b, :], ALU.add, ALU.mult)\
                         .then_inc(panel_sem(part, p), 1)
                elif p.startswith("mg"):
                    ps = panel_of(v, part, p)
                    c = int(p[2])
                    bm = one("PT")[:, c * 512:(c + 1) * 512]
                    v.wait_ge(bmerge_loaded, 16)
                    if c == 0:
                        for b in range(NB):
                            tile_of(v, part, f"kb2{b}")
                            tile_of(v, part, f"kb1{b}")
                    for b in range(NB):
                        if c >= 2:
                            v.wait_ge(merge_tanh, NB * (c - 2) + b + 1)
                        v.tensor_tensor(staged[:, b, c % 2, :], ps[:, b, :], bm, ALU.add).then_inc(merge_sum, 1)
                    for b in range(NB):
                        v.wait_ge(merge_sum, NB * c + b + 1)
                        v.sem_inc(panel_sem(part, p), 1)
            units = units_first()
            Es = one("E").rearrange("p (s t j) -> p s t j", s=2, t=3)

            def logits_first(u):
                kind, h, n = units[u]
                L = one("L").rearrange("p (s b j) -> p s b j", s=2, b=2)[:, u % 2]
                mx = mxs[u % 2]
                load = h // 2 if kind == "A" else 4 + h
                v.wait_ge(E_loaded[load % 2], 16 * (load // 2 + 1))
                if u >= 2:
                    k2, h2, n2 = units[u - 2]
                    for g in range(n2):
                        tile_of(v, part, f"T{k2}{h2}{g}")
                for g in range(n):
                    ps = tile_of(v, part, f"S{kind}{h}{g}")
                    E = Es[:, load % 2, h % 2 if kind == "A" else g, :]
                    for b in range(NB):
                        init = first[:, 12 + h:13 + h] if kind == "A" else low
                        e = v.tensor_tensor_reduce(L[:, b, g * TOKENS:(g + 1) * TOKENS], ps[:, b * TOKENS:(b + 1) * TOKENS],
                                                   E[:, P * (1 - b):P * (1 - b) + TOKENS], 1.0, init, ALU.add, ALU.max,
                                                   mx[:, b, g:g + 1])
                    e.then_inc(tile_sem(part, f"S{kind}{h}{g}"), 1)
                v.drain()
                v.tensor_reduce(negmax[:, :, u:u + 1], mx[:, :, 0:n], AX.X, ALU.max, negate=True).then_inc(logits, 1)
                if kind == "B" or h % 2 == 1:
                    v.sem_inc(E_used, 1)

            v.wait_ge(merge_tanh, 2 * 4)
            logits_first(0)
            for u in range(len(units)):
                kind, h, n = units[u]
                if u + 1 < len(units):
                    logits_first(u + 1)
                if n == 3:
                    if u >= 2:
                        wait_products(v, part, u - 2)
                    PT = one("PT").rearrange("p (s g j) -> p s g j", s=2, g=3)[:, u % 2]
                    ps = tile_of(v, part, f"T{kind}{h}1")
                    v.tensor_copy(PT[:, 1, :], ps[:, :]).then_inc(tile_sem(part, f"T{kind}{h}1"), 1)
                if u == H:
                    v.tensor_tensor(sinks[:, :, :], negmax[:, :, 0:H], first[:, 12:20].unsqueeze(1).broadcast_to([P, 2, H]),
                                    ALU.add).then_inc(sink_diff, 1)
                    v.wait_ge(sink_exp, 1)
                    v.tensor_tensor(den[:, :, 0:H], den[:, :, 0:H], sinks[:, :, :], ALU.add)
                    v.drain()
                    normed_out(v, part, 0)
            v.wait_ge(probs, 16)
            normed_out(v, part, 1)

            def merge(part, branches, mgt, width, updates):
                for i in range(branches):
                    for c in range(2):
                        ps = panel_of(v, part, f"br{i}{c}")
                        cs = slice(c * 512, (c + 1) * 512)
                        for b in range(NB):
                            g = mgt[:, b, i * D + c * 512:i * D + (c + 1) * 512]
                            if i == 0:
                                v.scalar_tensor_tensor(tok[:, b, cs], g, 1.0, ps[:, b, :], ALU.add, ALU.mult)\
                                 .then_inc(panel_sem(part, f"br{i}{c}"), 1)
                            else:
                                v.scalar_tensor_tensor(g, g, 1.0, ps[:, b, :], ALU.add, ALU.mult)\
                                 .then_inc(panel_sem(part, f"br{i}{c}"), 1)
                        if i:
                            v.drain()
                            for b in range(NB):
                                g = mgt[:, b, i * D + c * 512:i * D + (c + 1) * 512]
                                e = v.tensor_tensor(tok[:, b, cs], tok[:, b, cs], g, ALU.add)
                                if i == branches - 1 and c == 1:
                                    e.then_inc(merged, 1)

            def residual(part, names):
                for c, name in enumerate(names):
                    ps = panel_of(v, part, name)
                    cs = slice(c * 512, (c + 1) * 512)
                    for b in range(NB):
                        v.tensor_tensor(x[:, b, cs], x[:, b, cs], ps[:, b, :], ALU.add).then_inc(panel_sem(part, name), 1)
                v.drain().then_inc(x_updated, 1)

            for name in ("yA", "yB"):
                for b in range(NB):
                    tile_of(v, part, f"{name}{b}")
            merge(part, 2, one("mgt").rearrange("p (b n) -> p b n", b=2), 2 * D, 0)
            residual(part, ("wo0", "wo1"))
            u_all = two("u").rearrange("p (c t) -> p c t", c=4)
            hgv = two("hgv").rearrange("p (g q n) -> p g q n", g=2, q=4)
            v.memset(u_all[:, :, 0:32], 0.0)
            v.memset(two("hgv"), 0.0)
            v.memset(two("Pc"), 0.0)
            v.memset(two("hx"), 0.0)
            v.memset(two("vblk"), 0.0)
            v.drain()

            with v.Fori(0, LAYERS) as l:
                part = layer(l)
                v.wait_ge(par_loaded, l * 16 + 16)
                v.tensor_scalar(cw[:, :, :], pars("conv_w").rearrange("p (c j) -> p c j", c=4), 0.5, None, ALU.mult)
                for i, name in enumerate(("ln_g", "ln_b", "gn")):
                    v.tensor_scalar(lnh[:, i, :], pars(name), 0.5, None, ALU.mult)
                v.drain().then_inc(cw_ready, 1)
                rows_normed(part, l * 2 + 1, "x", pars("mix"))
                tz = two("tz").rearrange("p (b n) -> p b n", b=2)
                bc, before = part.turn("panel", "cb")
                v.wait_ge(panel_evicted[bc], before * 2 + 2)
                ps = panel_of(v, part, "ca")
                for b in range(NB):
                    v.scalar_tensor_tensor(u_all[:, 2 * b:2 * b + 2, 32:288], tz[:, b, :].rearrange("p (c t) -> p c t", c=2), 1.0,
                                           ps[:, b, :].rearrange("p (c t) -> p c t", c=2), ALU.add, ALU.mult)\
                     .then_inc(panel_sem(part, "ca"), 1)
                v.drain()
                acc = two("acc").rearrange("p (c t) -> p c t", c=4)
                cb_ = pars("conv_b")

                def taps(first_tap, last_tap):
                    for j in range(first_tap, last_tap):
                        for c in range(4):
                            src = u_all[:, c, 2 + j:2 + j + TOKENS]
                            if j == 0:
                                v.tensor_scalar(acc[:, c, :], src, cw[:, c, 0:1], cb_[:, c:c + 1], ALU.mult, ALU.add)
                            else:
                                v.scalar_tensor_tensor(acc[:, c, :], src, cw[:, c, j:j + 1], acc[:, c, :], ALU.mult, ALU.add)
                        v.drain()

                taps(0, 4)
                ps = panel_of(v, part, "k4")
                kcP = two("kcP").rearrange("p (i g t) -> p i g t", i=2, g=2)
                for i in range(2):
                    for g in range(2):
                        s = i * TOKENS
                        rows = slice(HD * g, HD * g + HD)
                        v.tensor_copy(kcP[0:HD, i, g, :], ps[rows, 0, s:s + TOKENS])
                        e = v.tensor_copy(kcP[HD:P, i, g, 0:TOKENS - 1], ps[rows, 0, s + 1:s + TOKENS])
                e.then_inc(panel_sem(part, "k4"), 1)
                v.drain()
                blk = two("blk").rearrange("p (i j n) -> p i j n", i=2, j=16)
                pe_ = pars("pe").rearrange("p (i j) -> p i j", i=2)
                for i in range(2):
                    for g in range(2):
                        lo = kcP[:, i, g, :].rearrange("p (n j s) -> p j n s", j=8, s=2)
                        for half in range(2):
                            src = lo[:, :, half:half + N_CMP, 0]
                            e = v.tensor_tensor(blk[:, i, 8 * half:8 * half + 8, g * N_CMP:(g + 1) * N_CMP], src,
                                                pe_[:, i, 8 * half:8 * half + 8].unsqueeze(2).broadcast_to([P, 8, N_CMP]), ALU.add)
                    e.then_inc(blocks_ready, 1)
                taps(4, 8)
                ps = tile_of(v, part, "cmpH")
                hx, hy, ht = two("hx"), two("hy"), two("ht")
                v.tensor_copy(hx[:, 0:30], ps[:, 0:30])
                v.tensor_copy(hx[:, 32:62], ps[:, 32:62]).then_inc(tile_sem(part, "cmpH"), 1)
                v.drain()
                v.tensor_tensor(hy, hx, hx, ALU.mult)
                v.drain()
                v.tensor_scalar(hy, hy, GELU_A, 1.0, ALU.mult, ALU.add)
                v.drain()
                v.tensor_tensor(hy, hy, hx, ALU.mult).then_inc(hid_in, 1)
                v.wait_ge(hid_tanh, l + 1)
                v.scalar_tensor_tensor(two("hgk"), ht[:, 0:32], 1.0, hx[:, 0:32], ALU.add, ALU.mult).then_inc(hid_ready, 1)
                for g in range(2):
                    s = 32 + g * N_CMP
                    e = v.scalar_tensor_tensor(hgv[:, g, :, 0:N_CMP], ht[:, s:s + N_CMP].unsqueeze(1).broadcast_to([P, 4, N_CMP]), 1.0,
                                               hx[:, s:s + N_CMP].unsqueeze(1).broadcast_to([P, 4, N_CMP]), ALU.add, ALU.mult)
                e.then_inc(hid_ready, 1)
                ps = panel_of(v, part, "qkr")
                t4 = two("or").rearrange("p (i h d) -> p i h d", i=4, h=8)
                for b in range(NB):
                    src = ps[:, b, :].rearrange("p (h s d) -> p h s d", h=8, s=2)
                    dst = staged[:, b, 0, :].rearrange("p (h s d) -> p h s d", h=8, s=2)
                    cos, sin = (rope[:, b, i, :].unsqueeze(1).broadcast_to([P, 8, 32]) for i in range(2))
                    v.tensor_tensor(t4[:, 0], src[:, :, 0, :], cos, ALU.mult)
                    v.tensor_tensor(t4[:, 1], src[:, :, 1, :], sin, ALU.mult)
                    v.tensor_tensor(t4[:, 2], src[:, :, 0, :], sin, ALU.mult)
                    v.tensor_tensor(t4[:, 3], src[:, :, 1, :], cos, ALU.mult).then_inc(panel_sem(part, "qkr"), 1)
                    v.drain()
                    v.tensor_tensor(dst[:, :, 0, :], t4[:, 0], t4[:, 1], ALU.subtract)
                    v.tensor_tensor(dst[:, :, 1, :], t4[:, 2], t4[:, 3], ALU.add).then_inc(rot_ready, 1)
                    v.drain()
                taps(8, 13)
                ps = panel_of(v, part, "gr")
                tg = two("tg").rearrange("p (b n) -> p b n", b=2)
                sgr = two("sgr").rearrange("p (b n) -> p b n", b=2)
                for b in range(NB):
                    v.wait_ge(gr_tanh, l * 2 + (b + 1))
                    v.scalar_tensor_tensor(sgr[:, b, :], tg[:, b, :], 1.0, ps[:, b, :], ALU.add, ALU.mult)\
                     .then_inc(panel_sem(part, "gr"), 1)
                v.wait_ge(En_loaded, 16)
                En = two("En").rearrange("p (h j) -> p h j", h=H)
                Lc = two("Lc").rearrange("p (b h n) -> p b h n", b=2, h=H)
                for g in range(2):
                    ps = tile_of(v, part, f"cmpS{g}")
                    for b in range(NB):
                        s = 31 + P * (1 - b)
                        src = ps[:, b * 4 * N_CMP:(b + 1) * 4 * N_CMP].rearrange("p (h n) -> p h n", h=4)
                        hg = slice(4 * g, 4 * g + 4)
                        e = v.tensor_tensor(Lc[:, b, hg], src, En[:, hg, s:s + (N_CMP - 1) * CMP_STRIDE + 1:CMP_STRIDE], ALU.add)
                    e.then_inc(tile_sem(part, f"cmpS{g}"), 1)
                v.drain()
                v.tensor_reduce(cmx[:, :, :], Lc[:, :, :, :], AX.X, ALU.max)
                v.drain()
                v.tensor_scalar(cmx[:, :, :], cmx[:, :, :], -1.0e29, None, ALU.max)
                v.drain()
                v.tensor_tensor(Lc[:, :, :, :], Lc[:, :, :, :], cmx[:, :, :].unsqueeze(3).broadcast_to([P, 2, H, N_CMP]),
                                ALU.subtract).then_inc(cmp_logits, 1)
                taps(13, 15)
                v.wait_ge(cmp_exp, l + 1)
                Pc = two("Pc").rearrange("p (b h n) -> p b h n", b=2, h=H)
                v.tensor_reduce(cden[:, :, :], Pc[:, :, :, 0:N_CMP], AX.X, ALU.add)
                v.drain()
                v.tensor_scalar(cden[:, :, :], cden[:, :, :], 1e-30, None, ALU.max)
                v.drain()
                v.reciprocal(cden[:, :, :], cden[:, :, :])
                v.drain()
                gt = two("gt").rearrange("p (b h i) -> p b h i", b=2, h=H)
                v.scalar_tensor_tensor(coef_c[:, :, :], gt[:, :, :, 0], 1.0, cden[:, :, :], ALU.add, ALU.mult)
                v.drain()
                PR = two("PR").rearrange("p (s n) -> p s n", s=2)

                def decayed(h):
                    ps = tile_of(v, part, f"R{h}")
                    if h >= 2:
                        v.wait_ge(pv_done, l * (2 * (H - 1) + RET_H - 1) + (2 * (H - 1) + h - 1))
                    v.tensor_tensor(PR[:, h % 2, 0:TOKENS], ps[:, 0:TOKENS], decay[:, h, :], ALU.mult)
                    v.tensor_tensor(PR[:, h % 2, TOKENS:TOKENS + P], ps[:, TOKENS:TOKENS + P], decay[:, h, 0:P], ALU.mult)
                    v.drain().then_inc(kept_ready, 1)
                    v.sem_inc(tile_sem(part, f"R{h}"), 1)

                decayed(0)
                y = two("y").rearrange("p (b n) -> p b n", b=2)
                tmp = two("tmp").rearrange("p (b n) -> p b n", b=2)

                def scaled(to, ps, b, by):
                    return v.tensor_tensor(to[:, b, :].rearrange("p (h d) -> p h d", h=H), ps[:, b, :].rearrange("p (h d) -> p h d", h=H),
                                           by.unsqueeze(2).broadcast_to([P, H, HD]), ALU.mult)

                ps = panel_of(v, part, "Oc")
                for b in range(NB):
                    scaled(y, ps, b, coef_c[:, b, :]).then_inc(panel_sem(part, "Oc"), 1)
                for h in range(1, RET_H):
                    decayed(h)
                ps = panel_of(v, part, "Or")
                for b in range(NB):
                    for h in range(RET_H):
                        v.bn_stats(bns[:, 4 * b + h, :], ps[:, b, h * P:(h + 1) * P])
                v.drain()
                for i in range(8):
                    v.bn_aggr(bna[:, i, :], bns[:, i, :])
                v.drain().then_inc(ret_stats, 1)
                v.wait_ge(ret_rstd, l + 1)
                o_r = two("or").rearrange("p (b n) -> p b n", b=2)
                for b in range(NB):
                    for h in range(RET_H):
                        hv = slice(h * P, (h + 1) * P)
                        v.tensor_scalar(o_r[:, b, hv], ps[:, b, hv], bna[:, 4 * b + h, 0:1], brs[:, b, h:h + 1],
                                        ALU.subtract, ALU.mult)
                    v.drain().then_inc(panel_sem(part, "Or"), 1)
                    v.tensor_tensor(o_r[:, b, :], o_r[:, b, :], sgr[:, b, :], ALU.mult).then_inc(ret_ready, 1)
                taps(15, 26)
                brT = two("brT").rearrange("p (i c t) -> p i c t", i=3, c=4)
                for b in range(NB):
                    ps = tile_of(v, part, f"oR{b}")
                    v.tensor_tensor(brT[:, 1, :, b * P:(b + 1) * P], ps[:, :].rearrange("p (c t) -> p c t", c=4),
                                    lnh[:, 2, :].unsqueeze(2).broadcast_to([P, 4, P]), ALU.mult).then_inc(tile_sem(part, f"oR{b}"), 1)
                taps(26, TAPS)
                v.sem_inc(conv_ready, 1)
                pss = [tile_of(v, part, f"cv{b}") for b in range(NB)]
                for b in range(NB):
                    v.bn_stats(cns[:, b, :], pss[b][:, :])
                v.drain()
                for b in range(NB):
                    v.bn_aggr(cna[:, b, :], cns[:, b, :])
                v.drain().then_inc(conv_stats, 1)
                v.wait_ge(conv_rstd, l + 1)
                for b in range(NB):
                    v.tensor_scalar(staged[:, b, 1, :], pss[b][:, :], cna[:, b, 0:1], crs[:, b:b + 1], ALU.subtract, ALU.mult)
                    v.drain().then_inc(tile_sem(part, f"cv{b}"), 1)
                    v.sem_inc(conv_normed, 1)
                units = units_layer()

                def logits_layer(u):
                    kind, h, _ = units[u]
                    mx = mxs[u % 2]
                    L = two("L").rearrange("p (s j) -> p s j", s=2)[:, u % 2]
                    if u >= 2:
                        k2, h2, _ = units[u - 2]
                        tile_of(v, part, f"T{k2}{h2}0")
                    ps = tile_of(v, part, f"S{kind}{h}0")
                    v.sem_inc(taken, 1)
                    v.tensor_tensor_reduce(L[:, 0:P], ps[:, 0:P], En[:, h, P:2 * P], 1.0, -3.0e38, ALU.add, ALU.max, mx[:, 0, 0:1])
                    v.tensor_tensor_reduce(L[:, P:3 * P], ps[:, P:3 * P], En[:, h, 0:TOKENS], 1.0, -3.0e38, ALU.add, ALU.max,
                                           mx[:, 1, 0:1]).then_inc(tile_sem(part, f"S{kind}{h}0"), 1)
                    v.drain()
                    v.tensor_scalar(negmax[:, :, u:u + 1], mx[:, :, 0:1], -1.0, None, ALU.mult).then_inc(logits, 1)

                logits_layer(0)
                v.wait_ge(conv_z, l + 1)
                v.scalar_tensor_tensor(brT[:, 2].rearrange("p c t -> p (c t)"), two("tz"), 1.0, two("z"), ALU.add, ALU.mult).then_inc(branch_ready, 1)
                for u in range(1, len(units)):
                    logits_layer(u)
                    if u == H + 1:
                        sum_out(v, part, l, 0)
                sum_out(v, part, l, 1)
                merge(part, 3, two("mgt").rearrange("p (b n) -> p b n", b=2), 3 * D, 0)
                residual(part, ("wo0", "wo1"))
                rows_normed(part, l * 2 + 2, "z", pars("mlp"))
                ffT = area[:, AREA_2["mgt"][0]:AREA_2["mgt"][0] + 8192].rearrange("p (k t) -> p k t", k=16)
                rr = two("tmp")
                for i in range(FF_PANELS):
                    s = (i % 2) * 512
                    ps = panel_of(v, part, f"ff{i}")
                    v.tensor_scalar(rr[:, s:s + 512], ps[:, 1, :], 0.0, None, ALU.max).then_inc(panel_sem(part, f"ff{i}"), 1)
                    v.drain()
                    v.tensor_tensor(ffT[:, 2 * i + 1, :], rr[:, s:s + 512], rr[:, s:s + 512], ALU.mult).then_inc(squared, 1)
                residual(part, ("down0", "down1"))
            v.wait_ge(rstd_ready, 2 * LAYERS + 2)
            v.wait_ge(final_loaded, 16)
            for b in range(NB):
                v.scalar_tensor_tensor(tok[:, b, :], x[:, b, :], rstd[:, b:b + 1], two("mgt")[:, 0:D], ALU.mult, ALU.mult)\
                 .then_inc(x_updated, 1)

        @block.gpsimd
        def _(g):
            def inverse_root(to, of, scale, out_sem, shape_power):
                g.sem_inc(taken, 1)
                g.tensor_scalar(to, of, scale, EPS, ALU.mult, ALU.add)
                g.drain()
                g.tensor_tensor(to, to, shape_power, ALU.pow).then_inc(out_sem, 1)

            g.wait_ge(pad_ready, PADS)
            g.wait_ge(squares, 2)
            inverse_root(rstd, ss, 1.0 / D, rstd_ready, half_power[:, 0:2])
            for n, p in enumerate(NORMED):
                nh = 2 if p == "kava" else 8
                g.wait_ge(head_sum, NB * (n + 1))
                if n >= 1:
                    g.wait_ge(head_normed, NB * n)
                inverse_root(hr[:, :, 0:nh], hs[:, :, 0:nh], 1.0 / HD, head_rstd,
                             half_power[:, 0:nh].unsqueeze(1).broadcast_to([P, 2, nh]))
            with g.Fori(0, LAYERS) as l:
                g.wait_ge(squares, l * 4 + 4)
                inverse_root(rstd, ss, 1.0 / D, rstd_ready, half_power[:, 0:2])
                g.wait_ge(ret_stats, l + 1)
                inverse_root(brs[:, :, :], bna[:, :, 1:2].rearrange("p (b h) o -> p b (h o)", b=2), 1.0, ret_rstd,
                             half_power[:, 0:4].unsqueeze(1).broadcast_to([P, 2, 4]))
                g.wait_ge(conv_stats, l + 1)
                inverse_root(crs, cna[:, :, 1], 1.0, conv_rstd, half_power[:, 0:2])
                g.wait_ge(squares, l * 4 + 6)
                inverse_root(rstd, ss, 1.0 / D, rstd_ready, half_power[:, 0:2])
            g.wait_ge(squares, 4 * LAYERS + 4)
            inverse_root(rstd, ss, 1.0 / D, rstd_ready, half_power[:, 0:2])


PAIRS = [0, 4, 1, 5, 2, 6, 3, 7]


def t5_bucket(rel):
    n = np.abs(rel)
    nf = np.maximum(n, 8).astype(np.float32)
    large = 8 + (np.log(nf / np.float32(8)) / np.float32(np.log(1024 / 8)) * np.float32(8)).astype(np.int32)
    return (rel > 0) * 16 + np.where(n < 8, n, np.minimum(large, 15))


def causal_bucket(dist):
    n = np.maximum(dist, 0)
    nf = np.maximum(n, 1).astype(np.float32)
    large = 16 + (np.log(nf / np.float32(16)) / np.float32(np.log(128 / 16)) * np.float32(16)).astype(np.int32)
    return np.where(n < 16, n, np.minimum(large, 31))


def position_table():
    t = np.zeros((33, 5, 512), np.float32)
    rel = np.arange(512) - 255
    kinds = [(np.abs(rel) <= P, t5_bucket(rel))]
    for window, dilation in GROUPS:
        reach = window // (2 * dilation) * dilation
        kinds.append(((rel % dilation == 0) & (np.abs(rel) <= reach), t5_bucket(rel)))
    kinds.append((rel <= 0, causal_bucket(-rel)))
    for i, (valid, bucket) in enumerate(kinds):
        for j in range(512):
            if valid[j]:
                t[bucket[j], i, j] = 1.0
            else:
                t[32, i, j] = MASKED
    return t.reshape(33, -1)


def decay_table():
    log_g = np.log1p(-np.exp2(-5.0 - np.arange(RET_H)))
    d = np.arange(TOKENS)[None, None, :] - np.arange(P)[:, None, None]
    return (np.where(d >= 0, np.exp(log_g[None, :, None] * np.maximum(d, 0)), 0.0) * HD ** -0.5).astype(np.float32)


def rope_table():
    half = HD // 2
    inv = np.float32(10000.0) ** (-np.arange(half, dtype=np.float32) / np.float32(half))
    ang = (np.arange(TOKENS, dtype=np.float32)[:, None] * inv[None, :]).astype(np.float32)
    t = np.stack([np.cos(ang), np.sin(ang)], 1).astype(np.float32)
    return np.ascontiguousarray(t.reshape(NB, P, 2, half).transpose(1, 0, 2, 3))


def chunks(w):
    k, n = w.shape
    return [np.ascontiguousarray(w[i * 512:(i + 1) * 512].reshape(4, P, n).transpose(1, 0, 2)).reshape(P, 4 * n)
            for i in range(k // 512)]


def pad_half(h):
    return np.pad(h, ((0, 0), (0, HALF - h.shape[1])))


def by_partition(v):
    return v.reshape(-1, P).T


def pack(inputs):
    f = {k: np.asarray(v) for k, v in inputs.items()}
    w = f["w_in"][0]
    cols = {"qa": w[:, 0:512].reshape(D, H, HD)[:, PAIRS].reshape(D, 512), "kava": w[:, 512:768]}
    for g in range(3):
        for i, n in enumerate(("qb", "kb", "vb")):
            s = 768 + i * 1536 + g * 512
            cols[f"{n}{g}"] = w[:, s:s + 512]
    cols["ga"], cols["gb"] = w[:, 5376:5888], w[:, 5888:6400]
    for i in range(4):
        cols[f"mg{i}"] = w[:, 6400 + 512 * i:6912 + 512 * i]
    for c in range(2):
        cs = slice(512 * c, 512 * c + 512)
        cols[f"br0{c}"], cols[f"br1{c}"] = f["w_branch_a"][0][:, cs], f["w_branch_b"][0][:, cs]
        cols[f"wo{c}"] = f["w_out"][0][:, cs]
    halves = {p: chunks(c) for p, c in cols.items()}
    w_first = np.stack([pad_half(halves[p][int(n.split("/")[1])]) for n, p in FIRST_HALVES])

    w_layers, par = [], []
    for l in range(LAYERS):
        w = f["w_in_2"][l]
        at = dict(kc=512, vc=640, ks=768, vs=896, kw=1024, vw=1152)
        k = {n: w[:, s:s + P] for n, s in at.items()}
        cols = {"q": w[:, 0:512].reshape(D, H, HD)[:, PAIRS].reshape(D, 512),
                "k4": np.concatenate([k["kc"], k["vc"], k["ks"], k["kw"]], 1),
                "vsg": np.concatenate([k["vs"], k["vw"], w[:, 1280:1304]], 1),
                "qkr": w[:, 1304:1816], "vr": w[:, 1816:2328], "gr": w[:, 2328:2840],
                "ca": w[:, 2840:3352], "cb": w[:, 3352:3864]}
        for i in range(6):
            cols[f"mg{i}"] = w[:, 3864 + 512 * i:4376 + 512 * i]
        for c in range(2):
            cs = slice(512 * c, 512 * c + 512)
            for i in range(3):
                cols[f"br{i}{c}"] = f["w_branch_2"][l, i][:, cs]
            cols[f"wo{c}"] = f["w_out_2"][l][:, cs]
            cols[f"down{c}"] = f["w_ff2_2"][l][:, cs]
        for i in range(FF_PANELS):
            cols[f"ff{i}"] = f["w_ff1_2"][l][:, 512 * i:512 * i + 512]
        halves = {p: chunks(c) for p, c in cols.items()}
        for n, p in LAYER_HALVES:
            if p == "cmpH":
                w1 = f["cmp_w1_" + n[2] + "_2"][l]
                w_layers.append(w1.reshape(16, 2 * HD, P).transpose(1, 0, 2).reshape(P, HALF))
            else:
                w_layers.append(pad_half(halves[p][int(n.split("/")[1])]))
        pe = [f[f"cmp_pe_{n}_2"][l].reshape(16, 2 * HD).T for n in "kv"]
        par.append(np.concatenate(
            [by_partition(f["norm_mix_2"][l]), by_partition(f["norm_mlp_2"][l]), by_partition(f["ret_gn_2"][l]),
             by_partition(f["conv_ln_g_2"][l]), by_partition(f["conv_ln_b_2"][l]), by_partition(f["conv_b_2"][l]),
             f["conv_w_2"][l].T.reshape(4, P, TAPS).transpose(1, 0, 2).reshape(P, 4 * TAPS), *pe,
             f["cmp_w2_k_2"][l], f["cmp_w2_k_2"][l], f["cmp_w2_v_2"][l]], 1))
    w_layers += [np.zeros((P, HALF), np.float32)] * SLOTS
    par.append(np.zeros((P, PAR), np.float32))
    gains = np.stack([np.concatenate([f[n][0], f[n][0]]) for n in ("q_norm_a", "k_norm_a", "q_norm_b", "k_norm_b")], 1)
    return dict(
        x=f["x"][0], w_first=w_first, w_layers=np.stack(w_layers), par=np.stack(par),
        first=np.concatenate([by_partition(f["norm_gain"][0]), gains, np.tile(f["sink_a"][0:1], (P, 1))], 1),
        rel_bias=f["rel_bias"], rel_table=f["rel_table_2"], b_merge=f["b_merge"][0].reshape(-1),
        norm_final=f["norm_final_2"], ident=np.eye(P, dtype=np.float32), onehot=position_table(),
        decay=decay_table(), rope=rope_table())


def kernel(**inputs):
    import concourse.bacc as bacc
    from concourse.bass_utils import run_bass_kernel_spmd

    nc = bacc.Bacc("TRN2", target_bir_lowering=False, num_devices=1)
    arrays, args = {}, {}
    for name, v in pack(inputs).items():
        v = np.ascontiguousarray(v)
        arrays[f"in_{name}_dram"] = v
        args[name] = nc.dram_tensor(f"in_{name}_dram", v.shape, mybir.dt.from_np(v.dtype), kind="ExternalInput").ap()
    out = nc.dram_tensor("out_0_dram", (TOKENS, D), F32, kind="ExternalOutput").ap()
    block_kernel(nc, args, out)
    r = run_bass_kernel_spmd(nc, [arrays], core_ids=[0])
    return r.results[0]["out_0_dram"].reshape(1, TOKENS, D)
```

```python
from contextlib import ExitStack

import numpy as np

import concourse.bass as bass
from concourse import mybir

F32 = mybir.dt.float32
ALU = mybir.AluOpType
ACT = mybir.ActivationFunctionType
AX = mybir.AxisListType

P = 128
TOKENS, D = 256, 1024
NB = TOKENS // P
KC = D // P
HD = 64
H = 8
HALF = 4 * 512
SLOTS = 6
EPS = 1e-6
MASKED = -1e30
LAYERS = 2
GROUPS = ((128, 1), (512, 4), (2048, 16))
N_CMP, CMP_STRIDE, CMP_LEN = 15, 16, 32
TAPS = 31
RET_H = 4
FF_PANELS = 8
TOEP = 3 * P
GELU_C, GELU_A = 0.7978845608028654, 0.044715

PAR_SIZES = dict(mix=KC, mlp=KC, gn=4, ln_g=4, ln_b=4, conv_b=4, conv_w=4 * TAPS, pe=32, w2k=P, w2v=HD)
PAR_AT, PAR = {}, 0
for _name, _size in PAR_SIZES.items():
    PAR_AT[_name] = (PAR, PAR + _size)
    PAR += _size
FIRST_AT = dict(norm=(0, 8), gains=(8, 12), sink=(12, 20))
FIRST = 20

FIRST_PANELS = ["qa", "kava", "qb0", "qb1", "qb2", "kb0", "kb1", "kb2", "vb0", "vb1", "vb2", "ga", "gb",
                "mg0", "mg1", "mg2", "mg3", "br00", "br01", "br10", "br11", "wo0", "wo1"]
NORMED = ["qa", "kava", "qb0", "qb1", "qb2", "kb0", "kb1", "kb2"]
LAYER_PANELS = (["cb", "ca", "q", "k4", "vsg", "qkr", "vr", "gr", "mg0", "Oc", "mg1", "Or", "mg2", "mg3",
                 "mg4", "mg5"] + [f"br{i}{c}" for i in range(3) for c in range(2)]
                + ["wo0", "wo1"] + [f"ff{i}" for i in range(FF_PANELS)] + ["down0", "down1"])
FIRST_WIDE = ["ga", "gb", "mg0", "mg1", "mg2", "mg3"]
LAYER_WIDE = ["qkr", "vr", "gr", "mg0", "mg1", "mg2", "mg3", "mg4", "mg5"]


def halves_of(panels, skip):
    out = []
    for p in panels:
        if p in skip:
            continue
        n = 1 if p.startswith("br") else 8 if p.startswith("down") else 2
        out += [(f"{p}/{i}", p) for i in range(n)]
        if p == "vsg":
            out += [("w1k", "cmpH"), ("w1v", "cmpH")]
    return out


FIRST_HALVES = halves_of(FIRST_PANELS, ())
LAYER_HALVES = halves_of(LAYER_PANELS, ("Oc", "Or"))
N_HALVES = len(LAYER_HALVES)
ONE_BY_ONE = ("cb", "ca", "q", "k4", "cmpH", *[f"ff{i}" for i in range(FF_PANELS)])


def transposed(name):
    return [f"{name}{b}" for b in range(NB)]


def units_first():
    return [("A", h, 1) for h in range(H)] + [("B", h, 3) for h in range(H)]


def units_layer():
    return [("s", h, 1) for h in range(H)] + [("w", h, 1) for h in range(H)]


GROUP = 4
TILES = 3


def unit_steps(n):
    out = [("S", 0)]
    for u in range(n):
        if u + 1 < n:
            out.append(("S", u + 1))
        out += [("T", u), ("V", u)]
    return out


def make_plan(panels, steps, slots, extra):
    steps = list(steps)
    plan = {}
    for p in panels:
        for s in range(KC):
            at = []
            if s in slots and steps:
                at.append(steps.pop(0))
            plan[p, s] = at + [(e, 0) for e in extra.get((p, s), [])]
    assert not steps
    return plan


FIRST_PLAN = make_plan(FIRST_WIDE, unit_steps(2 * H), range(KC), {})
LAYER_PLAN = make_plan(LAYER_WIDE, unit_steps(2 * H), (0, 1, 3, 4, 5, 7), {
    ("qkr", 6): ["cmpH"], ("vr", 2): ["rot"], ("vr", 6): ["cmp2"], ("gr", 2): ["cmpS"], ("mg0", 2): ["PcT"],
    ("mg0", 6): ["R0"], ("mg1", 0): ["R1"], ("mg1", 2): ["R2"], ("mg1", 5): ["R3"], ("mg4", 2): ["oR"], ("mg5", 1): ["cv"],
    ("mg5", 4): ["y"], ("mg5", 7): ["cz"]})


def plan_tiles(plan, units):
    out = []
    for steps in plan.values():
        for e, u in steps:
            if e in "ST":
                out += [f"{e}{units[u][0]}{units[u][1]}{g}" for g in range(units[u][2])]
            elif e == "cmpS":
                out += ["cmpS0", "cmpS1"]
            elif e in ("rot", "oR", "cv", "cz", "y"):
                out += transposed(e)
            elif e != "V":
                out.append(e)
    return out


FIRST_TILES = (["bias0", "bias1", "bias2", "bias3", "bias4"] + [f"x{b}{i}" for b in range(NB) for i in range(2)]
               + [t for p in NORMED for t in transposed(p)] + plan_tiles(FIRST_PLAN, units_first())
               + transposed("yA") + transposed("yB") + [f"m{b}{i}" for b in range(NB) for i in range(2)])
LAYER_TILES = ([f"x{b}{i}" for b in range(NB) for i in range(2)] + plan_tiles(LAYER_PLAN, units_layer())
               + [f"m{b}{i}" for b in range(NB) for i in range(2)]
               + [f"z{b}{i}" for b in range(NB) for i in range(2)])


def last_half(name, p, halves):
    i = [h for h, _ in halves].index(name)
    return p in ONE_BY_ONE or i + 1 == len(halves) or halves[i + 1][1] != p


def used_before(name, halves):
    i = [h for h, _ in halves].index(name)
    return sum(not last_half(h, p, halves) for h, p in halves[:i])


PADS = 4
X_UPDATES = 1 + 2 * LAYERS


class Turns:

    def __init__(self, names, buffers, before=None):
        self.before = before or [0] * buffers
        self.at, count = {}, list(self.before)
        start = sum(self.before)
        for i, n in enumerate(names):
            b = (start + i) % buffers
            self.at[n] = (b, count[b])
            count[b] += 1
        self.after = count
        self.each = [c - b for c, b in zip(count, self.before)]


class Part:

    def __init__(self, tiles, panels, halves, l):
        self.turns = dict(tile=tiles, panel=panels, half=halves)
        self.l = l

    def turn(self, kind, name):
        t = self.turns[kind]
        b, before = t.at[name]
        return b, before if self.l is None else self.l * t.each[b] + before


TILES_1 = Turns(FIRST_TILES, TILES)
PANELS_1 = Turns(FIRST_PANELS, 2)
HALVES_1 = Turns([h for h, _ in FIRST_HALVES], SLOTS)
TILES_2 = Turns(LAYER_TILES, TILES, TILES_1.after)
PANELS_2 = Turns(LAYER_PANELS, 2, PANELS_1.after)
HALVES_2 = Turns([h for h, _ in LAYER_HALVES], SLOTS, HALVES_1.after)
assert sum(PANELS_2.each) % 2 == 0 and sum(HALVES_2.each) % SLOTS == 0


def area_map(sizes):
    at, end = {}, 0
    for name, size in sizes:
        at[name] = (end, end + size)
        end += size
    return at, end


AREA_1, END_1 = area_map([
    ("qaT", 1024), ("kaT", 256), ("va", 256), ("qbT", 3072), ("kbT", 3072), ("vb", 3072), ("sga", 1024),
    ("sgb", 1024), ("mgt", 4096), ("L", 2 * 1536), ("PT", 2 * 1536), ("E", 2 * 3 * TOEP), ("yT", 2048), ("bm", 2048),
    ("ys", 2048)])
AREA_2, END_2 = area_map([
    ("En", H * TOEP), ("qT", 1024), ("kT", 512), ("vsw", 512), ("gt", 48), ("kcP", 1024), ("blk", 960),
    ("hx", 64), ("hy", 64), ("ht", 64), ("hgk", 32), ("hgv", 256), ("kcmpT", 32), ("vblk", 512), ("Lc", 240),
    ("Pc", 512), ("PcT", 512), ("u", 4 * 288), ("tz", 1024), ("acc", 1024), ("rT", 1024),
    ("vr", 1024), ("sgr", 1024), ("PR", 4 * 384), ("or", 1024), ("mgt", 6144), ("brT", 3072), ("L", 768),
    ("PT", 768), ("y", 1024), ("tmp", 1024), ("yc", 1024)])
AREA_2["z"] = AREA_2["kcP"]
AREA = max(END_1, END_2)


def block_kernel(nc, a, out):
    ctx = ExitStack()
    with ctx:
        def sb(name, *shape):
            return ctx.enter_context(nc.sbuf_tensor(name, [P, *shape], F32))

        def sem(name):
            return ctx.enter_context(nc.semaphore(name))

        ring = sb("ring", SLOTS, HALF)
        x = sb("x", NB, D)
        hT = sb("hT", KC, TOKENS)
        tok = sb("tok", NB, D)
        ident = sb("ident", P)
        decay = sb("decay", RET_H, TOKENS)
        rope = sb("rope", NB, 2, HD // 2)
        par = sb("par", PAR)
        first = sb("first", FIRST)
        cw = sb("cw", 4, TAPS)
        lnh = sb("lnh", 3, 4)
        stat = sb("stat", 256)
        area = sb("area", AREA)
        tile = [ctx.enter_context(nc.psum_tensor(f"tile{i}", [P, 512], F32)) for i in range(TILES)]
        panel = [ctx.enter_context(nc.psum_tensor(f"panel{i}", [P, 2, 512], F32)) for i in range(2)]
        heads_out = ctx.enter_context(nc.psum_tensor("heads_out", [P, NB, GROUP * HD], F32))
        bias_rows = nc.dram_tensor("bias_rows", (5, H, 512), F32, kind="Internal").ap()
        bias_copies = nc.dram_tensor("bias_copies", (5, H, P, 512), F32, kind="Internal").ap()

        def toeplitz(head, step, n):
            return bass.AP(tensor=bias_copies.tensor, offset=head * P * 512 + 127,
                           ap=[[511, P], [step * P * 512, n], [1, TOEP]])


        def one(name):
            s, e = AREA_1[name]
            return area[:, s:e]

        def two(name):
            s, e = AREA_2[name]
            return area[:, s:e]

        def pars(name):
            s, e = PAR_AT[name]
            return par[:, s:e]

        def st(s, *shape):
            n = int(np.prod(shape))
            v = stat[:, s:s + n]
            if len(shape) == 2:
                v = v.rearrange("p (a b) -> p a b", a=shape[0])
            return v

        ss, rstd = st(0, 2), st(2, 2)
        hs, hr = st(4, 2, 8), st(20, 2, 8)
        mxs = [st(36, 2, 3), st(224, 2, 3)]
        negmax = stat[:, 42:74].rearrange("p (b u) -> p b u", b=2)
        den = stat[:, 74:106].rearrange("p (b u) -> p b u", b=2)
        sinks = stat[:, 106:122].rearrange("p (b u) -> p b u", b=2)
        cmx, cden, coef_c = st(122, 2, 8), st(138, 2, 8), st(154, 2, 8)
        half_power = stat[:, 170:178]
        bns, bna = sb("bns", 8, 6), sb("bna", 8, 2)
        brs = st(178, 2, 4)
        cns, cna, crs = sb("cns", 2, 6), sb("cna", 2, 2), st(186, 2)
        coef = stat[:, 190:222].rearrange("p (b u) -> p b u", b=2)
        zero = stat[:, 222:223]
        low = stat[:, 223:224]

        loaded = sem("constants_loaded")
        x_loaded = sem("x_loaded")
        par_loaded = sem("layer_parameters_loaded")
        bmerge_loaded = sem("merge_bias_loaded")
        final_loaded = sem("final_gain_loaded")
        En_loaded = sem("layer_bias_loaded")
        E_loaded = [sem(f"head_bias{i}_loaded") for i in range(2)]
        E_used = sem("head_bias_used")
        half_loaded = [sem(f"half{i}_loaded") for i in range(SLOTS)]
        half_used = sem("half_used")
        tile_done = [sem(f"tile{i}_done") for i in range(TILES)]
        tile_evicted = [sem(f"tile{i}_evicted") for i in range(TILES)]
        panel_done = [sem(f"panel{i}_done") for i in range(2)]
        panel_evicted = [sem(f"panel{i}_evicted") for i in range(2)]
        pad_ready = sem("constant_fill_ready")
        rows_ready = sem("bias_rows_ready")
        rows_stored = sem("bias_rows_stored")
        copies_stored = sem("bias_copies_stored")
        squares = sem("row_squares_ready")
        rstd_ready = sem("row_rstd_ready")
        h_ready = sem("h_ready")
        head_sq = sem("head_squares_ready")
        head_sum = sem("head_sums_ready")
        head_rstd = sem("head_rstd_ready")
        head_normed = sem("heads_normed")
        gate_tanh = sem("gate_tanh_ready")
        merge_sum = sem("merge_bias_added")
        merge_tanh = sem("merge_tanh_ready")
        logits = sem("logits_ready")
        probs = sem("probs_ready")
        pv_done = sem("pv_done")
        group_done = sem("head_group_done")
        group_evicted = sem("head_group_evicted")
        y_ready = sem("y_ready")
        merged = sem("merged_ready")
        x_updated = sem("x_updated")
        cw_ready = sem("half_weights_ready")
        conv_tanh = sem("conv_tanh_ready")
        u_ready = sem("conv_input_ready")
        conv_ready = sem("conv_sum_ready")
        conv_stats = sem("conv_stats_ready")
        conv_rstd = sem("conv_rstd_ready")
        conv_normed = sem("conv_normed")
        conv_z = sem("conv_z_tanh_ready")
        pairs_ready = sem("token_pairs_ready")
        blocks_ready = sem("blocks_ready")
        hid_in = sem("gelu_argument_ready")
        hid_tanh = sem("gelu_tanh_ready")
        hid_ready = sem("hidden_ready")
        cmp_logits = sem("compressed_logits_ready")
        cmp_exp = sem("compressed_exp_ready")
        rot_ready = sem("rotated_ready")
        gr_tanh = sem("retention_gate_tanh_ready")
        kept_ready = sem("decayed_scores_ready")
        ret_stats = sem("retention_stats_ready")
        ret_rstd = sem("retention_rstd_ready")
        ret_ready = sem("retention_output_ready")
        branch_ready = sem("conv_branch_ready")
        relu_done = sem("relu_done")
        squared = sem("squares_of_relu_ready")
        stored = sem("output_stored")
        taken = sem("operands_taken")

        block = ctx.enter_context(nc.Block())
        part_1 = Part(TILES_1, PANELS_1, HALVES_1, None)

        def layer(l):
            return Part(TILES_2, PANELS_2, HALVES_2, l)

        def count(part, first_block, each, n):
            return n if part.l is None else part.l * each + (first_block + n)

        PER = dict(half_used=(len([1 for h, p in FIRST_HALVES if not last_half(h, p, FIRST_HALVES)]),
                              len([1 for h, p in LAYER_HALVES if not last_half(h, p, LAYER_HALVES)])))

        def wait_done(eng, sems, part, kind, name):
            b, before = part.turn(kind, name)
            eng.wait_ge(sems[b], before + 1)
            return b

        def tile_of(eng, part, name):
            return tile[wait_done(eng, tile_done, part, "tile", name)]

        def panel_of(eng, part, name):
            return panel[wait_done(eng, panel_done, part, "panel", name)]

        def tile_sem(part, name):
            return tile_evicted[part.turn("tile", name)[0]]

        def panel_sem(part, name):
            return panel_evicted[part.turn("panel", name)[0]]

        def wait_products(eng, part, u):
            if u % GROUP == GROUP - 1:
                eng.wait_ge(group_done, count(part, 4, 4, u // GROUP + 1))
            else:
                eng.wait_ge(pv_done, count(part, 12, 12, u - u // GROUP + 1))

        def normed_out(v, part, i):
            us = slice(GROUP * i, GROUP * (i + 1))
            c = coef[:, :, us]
            v.wait_ge(probs, GROUP * (i + 1))
            if i < 2:
                v.tensor_tensor(den[:, :, us], den[:, :, us], sinks[:, :, us], ALU.add)
                v.drain()
            v.reciprocal(c, den[:, :, us])
            v.drain()
            v.tensor_scalar(c, c, 0.5, None, ALU.mult)
            v.drain()
            v.wait_ge(group_done, i + 1)
            hs_ = slice(GROUP * HD * (i % 2), GROUP * HD * (i % 2 + 1))
            to = one("ys").rearrange("p (t b n) -> p t b n", t=2, b=2)[:, i // 2, :, hs_]
            gate = one(("sga", "sgb")[i // 2]).rearrange("p (b n) -> p b n", b=2)[:, :, hs_]
            for b in range(NB):
                v.tensor_tensor(to[:, b, :].rearrange("p (h d) -> p h d", h=GROUP),
                                heads_out[:, b, :].rearrange("p (h d) -> p h d", h=GROUP),
                                c[:, b, :].unsqueeze(2).broadcast_to([P, GROUP, HD]), ALU.mult)
            v.drain().then_inc(group_evicted, 1)
            for b in range(NB):
                e = v.tensor_tensor(to[:, b, :], to[:, b, :], gate[:, b, :], ALU.mult)
            e.then_inc(y_ready, 1)

        def sum_out(v, part, l, i):
            w = i // 2
            us = slice(GROUP * i, GROUP * (i + 1))
            c = coef[:, :, us]
            gt = two("gt").rearrange("p (b h i) -> p b h i", b=2, h=H)[:, :, GROUP * (i % 2):GROUP * (i % 2 + 1)]
            hs_ = slice(GROUP * HD * (i % 2), GROUP * HD * (i % 2 + 1))
            y = two("y").rearrange("p (b n) -> p b n", b=2)[:, :, hs_]
            tmp = two("tmp").rearrange("p (s b n) -> p s b n", s=2, b=2)[:, i % 2]
            v.wait_ge(probs, l * 16 + (16 + GROUP * (i + 1)))
            v.reciprocal(c, den[:, :, us])
            v.drain()
            v.scalar_tensor_tensor(c, gt[:, :, :, 1 + w], 1.0, c, ALU.add, ALU.mult)
            v.drain()
            v.wait_ge(group_done, l * 4 + (4 + i + 1))
            to = y if i < 2 else tmp
            for b in range(NB):
                v.tensor_tensor(to[:, b, :].rearrange("p (h d) -> p h d", h=GROUP),
                                heads_out[:, b, :].rearrange("p (h d) -> p h d", h=GROUP),
                                c[:, b, :].unsqueeze(2).broadcast_to([P, GROUP, HD]), ALU.mult)
            v.drain().then_inc(group_evicted, 1)
            if i >= 2:
                for b in range(NB):
                    e = v.tensor_tensor(y[:, b, :], y[:, b, :], tmp[:, b, :], ALU.add)
                v.drain()
                e = v.tensor_tensor(y, y, two("yc").rearrange("p (b n) -> p b n", b=2)[:, :, hs_], ALU.add)
                e.then_inc(y_ready, 1)

        @block.sync
        def _(sp):
            sp.dma_start(x[:, :, :], a["x"].rearrange("(b p) d -> p b d", p=P)).then_inc(x_loaded, 16)
            for name, to in (("ident", ident[:, :]), ("first", first[:, :]), ("decay", decay[:, :, :]),
                             ("rope", rope[:, :, :, :])):
                sp.dma_start(to, a[name]).then_inc(loaded, 16)
            onehot = one("mgt")[0:33, 0:2560]
            sp.dma_start(onehot[0:33, :], a["onehot"]).then_inc(loaded, 16)
            tabs = one("mgt")[0:32, 2560:2600]
            sp.dma_start(tabs[:, 0:32], a["rel_bias"]).then_inc(loaded, 16)
            sp.dma_start(tabs[:, 32:40], a["rel_table"]).then_inc(loaded, 16)
            sp.dma_start(par[:, :], a["par"][0]).then_inc(par_loaded, 16)

            def load_half(part, name, source, halves):
                i = [h for h, _ in halves].index(name)
                slot = part.turn("half", name)[0]
                if i >= SLOTS:
                    wait_used(part, *halves[i - SLOTS], halves)
                w = 4 * 280 if name.startswith("vsg") else 4 * 256 if name.startswith("kava") else HALF
                sp.dma_start(ring[:, slot, 0:w], source[:, 0:w]).then_inc(half_loaded[slot], 16)

            def wait_used(part, prev, p, halves):
                if p == "cmpH":
                    b, before = part.turn("tile", "cmpH")
                    sp.wait_ge(tile_done[b], before + 1)
                elif last_half(prev, p, halves):
                    b, before = part.turn("panel", p)
                    sp.wait_ge(panel_done[b], before + 1)
                else:
                    n = used_before(prev, halves)
                    sp.wait_ge(half_used, count(part, PER["half_used"][0], PER["half_used"][1], n + 1))

            def load_first(i):
                name = FIRST_HALVES[i][0]
                load_half(part_1, name, a["w_first"][i], FIRST_HALVES)
                if name == "mg0/0":
                    sp.dma_start(one("bm"), a["b_merge"].partition_broadcast(P)).then_inc(bmerge_loaded, 16)

            for i in range(8):
                load_first(i)
            for t in range(5):
                sp.wait_ge(rows_stored, 16 * 5)
                src = bass.AP(tensor=bias_rows.tensor, offset=t * H * 512, ap=[[512, H], [0, P], [1, 512]])
                sp.dma_start(bias_copies[t], src).then_inc(copies_stored, 16)
            sp.wait_ge(copies_stored, 16 * 5)
            Es = one("E").rearrange("p (s t j) -> p s t j", s=2, t=3)

            def load_bias(n):
                if n >= 2:
                    sp.wait_ge(E_used, n - 1)
                if n < 4:
                    sp.dma_start(Es[:, n % 2, 0:2, :], toeplitz(2 * n, 1, 2)).then_inc(E_loaded[n % 2], 16)
                else:
                    sp.dma_start(Es[:, n % 2, :, :], toeplitz(H + n - 4, H, 3)).then_inc(E_loaded[n % 2], 16)

            names = [h for h, _ in FIRST_HALVES]
            first_wide = names.index("ga/0")
            bias_at = {}
            for n in range(2):
                load_bias(n)
            for n in range(2, 4 + H):
                unit = 2 * n if n < 4 else n + 4
                before_step = max(0, 3 * unit - 9)
                bias_at.setdefault(first_wide + SLOTS - 1 + before_step // 4, []).append(n)
            for i in range(8, len(FIRST_HALVES)):
                load_first(i)
                for n in bias_at.pop(i, []):
                    load_bias(n)
            for ns in bias_at.values():
                for n in ns:
                    load_bias(n)
            sp.wait_ge(group_done, 4)
            sp.dma_start(two("En").rearrange("p (h j) -> p h j", h=H), toeplitz(4 * H, 1, H)).then_inc(En_loaded, 16)

            for i in range(SLOTS):
                name = LAYER_HALVES[i][0]
                prev, p = FIRST_HALVES[len(FIRST_HALVES) - SLOTS + i]
                slot = HALVES_2.at[name][0]
                wait_used(part_1, prev, p, FIRST_HALVES)
                sp.dma_start(ring[:, slot, :], a["w_layers"][i]).then_inc(half_loaded[slot], 16)

            with sp.Fori(0, LAYERS) as l:
                part = layer(l)
                for i, (name, p) in enumerate(LAYER_HALVES):
                    if i >= SLOTS:
                        load_half(part, name, a["w_layers"][l * N_HALVES + i], LAYER_HALVES)
                b, before = part.turn("panel", "ff7")
                sp.wait_ge(panel_done[b], before + 1)
                sp.dma_start(par[:, :], a["par"][l + 1]).then_inc(par_loaded, 16)
                for i in range(SLOTS):
                    name = LAYER_HALVES[i][0]
                    prev, p = LAYER_HALVES[len(LAYER_HALVES) - SLOTS + i]
                    slot = HALVES_2.at[name][0]
                    wait_used(part, prev, p, LAYER_HALVES)
                    sp.dma_start(ring[:, slot, :], a["w_layers"][l * N_HALVES + (N_HALVES + i)]).then_inc(half_loaded[slot], 16)

            sp.dma_start(two("mgt")[:, 0:D], a["norm_final"].partition_broadcast(P)).then_inc(final_loaded, 16)
            for b in range(NB):
                sp.wait_ge(x_updated, X_UPDATES + b + 1)
                sp.dma_start(out.rearrange("(b p) d -> b p d", p=P)[b], tok[:, b, :]).then_inc(stored, 16)
            sp.wait_ge(stored, 32)
            sp.wait_ge(par_loaded, 16 * (LAYERS + 1))
            for s in range(SLOTS):
                sp.wait_ge(half_loaded[s], 16 * (HALVES_2.after[s] + (LAYERS - 1) * HALVES_2.each[s] + 1))

        @block.tensor
        def _(pe):
            def tile_for(part, name):
                b, before = part.turn("tile", name)
                if part.l is not None or before:
                    pe.wait_ge(tile_evicted[b], before)
                return tile[b], tile_done[b]

            def panel_for(part, name):
                b, before = part.turn("panel", name)
                if part.l is not None or before:
                    pe.wait_ge(panel_evicted[b], before * 2)
                return panel[b], panel_done[b]

            def wait_evicted(part, name):
                b, before = part.turn("tile", name)
                pe.wait_ge(tile_evicted[b], before + 1)

            def tile_after(part, name, names):
                for n in names:
                    if part.turn("tile", n)[0] != part.turn("tile", name)[0]:
                        wait_evicted(part, n)
                return tile_for(part, name)

            def wait_half(part, name):
                slot, before = part.turn("half", name)
                pe.wait_ge(half_loaded[slot], before * 16 + 16)
                return slot

            def rows_out(part, name, lhs, halves, width=512, plan=None, step=None):
                ps, done = panel_for(part, name)
                for i, half in enumerate(halves):
                    slot = wait_half(part, half)
                    w = ring[:, slot, 0:4 * width].rearrange("p (k n) -> p k n", k=4)
                    for k in range(4):
                        for b in range(NB):
                            last = i == len(halves) - 1 and k == 3
                            mm = pe.matmul(ps[:, b, 0:width], lhs(4 * i + k, b), w[:, k, :],
                                           start=(i == 0 and k == 0), stop=last)
                        if last:
                            mm.then_inc(done, 1)
                        elif k == 3:
                            mm.then_inc(half_used, 1)
                        if plan:
                            for e, u in plan[name, 4 * i + k]:
                                step(e, u)

            def columns_out(part, name):
                ps, done = panel_for(part, name)
                slots = [wait_half(part, f"{name}/{i}") for i in range(2)]
                for m in range(4):
                    for k in range(KC):
                        w = ring[:, slots[k // 4], (k % 4) * 512 + m * P:(k % 4) * 512 + (m + 1) * P]
                        mm = pe.matmul(ps[:, m // 2, (m % 2) * TOKENS:(m % 2 + 1) * TOKENS], w, hT[:, k, :],
                                       start=(k == 0), stop=(k == KC - 1))
                mm.then_inc(done, 1)

            def turn(part, name, source, n=4, rows=P):
                ps, done = tile_for(part, name)
                for i in range(n):
                    mm = pe.transpose(ps[0:rows, i * P:(i + 1) * P], source(i), ident[:, :])
                mm.then_inc(done, 1)

            def turn_rows(part, name, ready, base):
                for b in range(NB):
                    pe.wait_ge(ready, base + b + 1 if part.l is None else base + (b + 1))
                    for i in range(2):
                        turn(part, f"{name}{b}{i}", lambda c: tok[:, b, (4 * i + c) * P:(4 * i + c + 1) * P])

            def operand_ready(part, name):
                for b in range(NB):
                    for i in range(2):
                        wait_evicted(part, f"{name}{b}{i}")

            lhs_h = lambda k, b: hT[:, k, b * P:(b + 1) * P]
            two_halves = lambda n: [f"{n}/0", f"{n}/1"]

            part = part_1
            onehot = one("mgt")[0:33, 0:2560].rearrange("p (t j) -> p t j", t=5)
            tabs = one("mgt")[0:33, 2560:2600]
            pe.wait_ge(loaded, 16 * 7)
            pe.wait_ge(pad_ready, PADS)
            for t in range(5):
                ps, done = tile_for(part, f"bias{t}")
                pe.matmul(ps[0:H, :], tabs[:, t * H:(t + 1) * H], onehot[:, t, :], start=True, stop=True).then_inc(done, 1)
            turn_rows(part, "x", h_ready, 0)
            operand_ready(part, "x")
            staged = tok[:, :, :].rearrange("p b (s n) -> p b s n", s=2)

            def turn_heads(n):
                p = NORMED[n]
                for b in range(NB):
                    pe.wait_ge(head_normed, NB * n + b + 1)
                    turn(part, f"{p}{b}", lambda c: staged[:, b, n % 2, c * P:(c + 1) * P], n=1 if p == "kava" else 4)

            for n, p in enumerate(FIRST_PANELS[:11]):
                rows_out(part, p, lhs_h, two_halves(p), 256 if p == "kava" else 512)
                if 1 <= n <= len(NORMED):
                    turn_heads(n - 1)

            qaT, kaT = one("qaT").rearrange("p (c t) -> p c t", c=4), one("kaT")
            qbT = one("qbT").rearrange("p (g c t) -> p g c t", g=3, c=4)
            kbT = one("kbT").rearrange("p (g c t) -> p g c t", g=3, c=4)
            va = one("va").rearrange("p (b n) -> p b n", b=2)
            vb = one("vb").rearrange("p (g b n) -> p g b n", g=3, b=2)

            def head_rows(h):
                s = HD * (h // 4)
                return slice(s, s + HD), h % 4

            def scores_first(kind, h, g):
                ps, done = tile_for(part, f"S{kind}{h}{g}")
                for b in range(NB):
                    if kind == "A":
                        r, c = head_rows(h)
                        q, k = qaT[r, c, b * P:(b + 1) * P], kaT[r, :]
                    else:
                        r, c = slice(HD * (h % 2), HD * (h % 2) + HD), h // 2
                        q, k = qbT[r, g, c, b * P:(b + 1) * P], kbT[r, g, c, :]
                    mm = pe.matmul(ps[:, b * TOKENS:(b + 1) * TOKENS], q, k, start=True, stop=True)
                mm.then_inc(done, 1)

            units = units_first()
            ys = one("ys").rearrange("p (t b n) -> p t b n", t=2, b=2)

            def open_group(u, base):
                if u % GROUP == 0 and (base is not None or u):
                    pe.wait_ge(group_evicted, u // GROUP if base is None else base + u // GROUP)

            def step_first(e, u):
                kind, h, n = units[u]
                L = one("L").rearrange("p (s b j) -> p s b j", s=2, b=2)[:, u % 2]
                PT = one("PT").rearrange("p (s g j) -> p s g j", s=2, g=3)[:, u % 2]
                if e == "S":
                    if u == 0:
                        for p in NORMED:
                            for b in range(NB):
                                wait_evicted(part, f"{p}{b}")
                    for g in range(n):
                        scores_first(kind, h, g)
                elif e == "T":
                    pe.wait_ge(probs, u + 1)
                    for g in range(n):
                        turn(part, f"T{kind}{h}{g}",
                             lambda c: L[:, c // 2, g * TOKENS + (c % 2) * P:g * TOKENS + (c % 2 + 1) * P])
                else:
                    if u == 0:
                        for p in ("kava", "vb0", "vb1", "vb2"):
                            bp, before = part.turn("panel", p)
                            pe.wait_ge(panel_evicted[bp], before * 2 + 2)
                    open_group(u, None)
                    for g in range(n):
                        wait_evicted(part, f"T{kind}{h}{g}")
                    hd = slice((h % GROUP) * HD, (h % GROUP + 1) * HD)
                    for b in range(NB):
                        for g in range(n):
                            for k in range(2):
                                val = va[:, k, HD * (h // 4):HD * (h // 4) + HD] if kind == "A" else \
                                    vb[:, g, k, h * HD:(h + 1) * HD]
                                mm = pe.matmul(heads_out[:, b, hd], PT[:, g, (2 * b + k) * P:(2 * b + k + 1) * P], val,
                                               start=(g == 0 and k == 0), stop=(g == n - 1 and k == 1))
                    mm.then_inc(group_done if u % GROUP == GROUP - 1 else pv_done, 1)

            for p in FIRST_WIDE:
                rows_out(part, p, lhs_h, two_halves(p), 512, FIRST_PLAN, step_first)

            for t, name in enumerate(("yA", "yB")):
                for b in range(NB):
                    pe.wait_ge(y_ready, 2 * t + 2)
                    turn(part, f"{name}{b}", lambda c: ys[:, t, b, c * P:(c + 1) * P])
            yT = one("yT").rearrange("p (i c t) -> p i c t", i=2, c=4)
            for t, name in enumerate(("yA", "yB")):
                for b in range(NB):
                    wait_evicted(part, f"{name}{b}")
                for c in range(2):
                    rows_out(part, f"br{t}{c}", lambda k, b: yT[:, t, k, b * P:(b + 1) * P], [f"br{t}{c}/0"])
            turn_rows(part, "m", merged, 0)
            operand_ready(part, "m")
            for c in range(2):
                rows_out(part, f"wo{c}", lhs_h, two_halves(f"wo{c}"))

            with pe.Fori(0, LAYERS) as l:
                part = layer(l)
                turn_rows(part, "x", h_ready, l * 4 + 2)
                operand_ready(part, "x")
                for p in ("cb", "ca", "q", "k4"):
                    columns_out(part, p)
                rows_out(part, "vsg", lhs_h, two_halves("vsg"), 280)

                staged = tok[:, :, :].rearrange("p b (s n) -> p b s n", s=2)
                qT = two("qT").rearrange("p (c t) -> p c t", c=4)
                kT = two("kT").rearrange("p (i t) -> p i t", i=2)
                vsw = two("vsw").rearrange("p (b n) -> p b n", b=2)
                rT = two("rT").rearrange("p (c t) -> p c t", c=4)
                PR = two("PR").rearrange("p (h n) -> p h n", h=RET_H)
                PcT = two("PcT").rearrange("p (s q) -> p s q", s=4)
                Pc = two("Pc").rearrange("p (s n) -> p s n", s=4)
                acc = two("acc").rearrange("p (c t) -> p c t", c=4)
                units = units_layer()

                def compress():
                    ps, done = tile_for(part, "cmpH")
                    pe.wait_ge(blocks_ready, l * 2 + 2)
                    for i, half in enumerate(("w1k", "w1v")):
                        slot = wait_half(part, half)
                        blk = two("blk").rearrange("p (i j n) -> p i j n", i=2, j=16)[:, i]
                        for j in range(16):
                            mm = pe.matmul(ps[:, 32 * i:32 * i + 30], ring[:, slot, j * P:(j + 1) * P], blk[:, j, :],
                                           start=(j == 0), stop=(j == 15))
                    mm.then_inc(done, 1)

                def compress_2():
                    ps, done = tile_for(part, "cmp2")
                    pe.wait_ge(hid_ready, l * 2 + 2)
                    pe.matmul(ps[:, 0:30], pars("w2k"), two("hgk")[:, 0:30], start=True, stop=True)
                    hgv = two("hgv").rearrange("p (g n) -> p g n", g=2)
                    for g in range(2):
                        mm = pe.matmul(ps[:, 64 + g * HD:64 + (g + 1) * HD], hgv[:, g, :], pars("w2v"), start=True, stop=True)
                    mm.then_inc(done, 1)

                def compressed_scores():
                    for g in range(2):
                        ps, done = tile_after(part, f"cmpS{g}", ["cmp2"] if g == 0 else [])
                        for b in range(NB):
                            for i in range(4):
                                r, c = head_rows(4 * g + i)
                                s = (b * 4 + i) * N_CMP
                                mm = pe.matmul(ps[:, s:s + N_CMP], qT[r, c, b * P:(b + 1) * P],
                                               two("kcmpT")[r, g * N_CMP:(g + 1) * N_CMP], start=True, stop=True)
                        mm.then_inc(done, 1)

                def compressed_out():
                    ps, done = panel_for(part, "Oc")
                    wait_evicted(part, "PcT")
                    vblk = two("vblk").rearrange("p (g n) -> p g n", g=2)
                    for b in range(NB):
                        for g in range(2):
                            mm = pe.matmul(ps[:, b, g * 4 * HD:(g + 1) * 4 * HD], PcT[:, 2 * b + g, :], vblk[:, g, :],
                                           start=True, stop=True)
                    mm.then_inc(done, 1)

                def ret_scores(h):
                    ps, done = tile_after(part, f"R{h}", transposed("rot") if h == 0 else [])
                    r = slice(HD * (h % 2), HD * (h % 2) + HD)
                    pe.matmul(ps[:, 0:TOKENS], rT[r, 2 + h // 2, 0:P], rT[r, h // 2, :], start=True, stop=True)
                    pe.matmul(ps[:, TOKENS:TOKENS + P], rT[r, 2 + h // 2, P:TOKENS], rT[r, h // 2, P:TOKENS],
                              start=True, stop=True).then_inc(done, 1)

                def retention_out():
                    vr = two("vr").rearrange("p (b n) -> p b n", b=2)
                    ps, done = panel_for(part, "Or")
                    bv, before = part.turn("panel", "vr")
                    pe.wait_ge(panel_evicted[bv], before * 2 + 2)
                    for h in range(RET_H):
                        wait_evicted(part, f"R{h}")
                        hv = slice(h * P, (h + 1) * P)
                        pe.matmul(ps[:, 0, hv], PR[:, h, 0:P], vr[:, 0, hv], start=True, stop=True)
                        pe.matmul(ps[:, 1, hv], PR[:, h, P:TOKENS], vr[:, 0, hv], start=True, stop=False)
                        mm = pe.matmul(ps[:, 1, hv], PR[:, h, TOKENS:TOKENS + P], vr[:, 1, hv], start=False, stop=True)
                    mm.then_inc(done, 1)

                def step_layer(e, u):
                    kind, h, _ = units[u]
                    w = 0 if kind == "s" else 1
                    r, c = head_rows(h)
                    L = two("L").rearrange("p (s j) -> p s j", s=2)[:, u % 2]
                    PT = two("PT").rearrange("p (s j) -> p s j", s=2)[:, u % 2]
                    if e == "S":
                        if u == 0:
                            for p in ("q", "k4"):
                                bp, before = part.turn("panel", p)
                                pe.wait_ge(panel_evicted[bp], before * 2 + 2)
                        ps, done = tile_for(part, f"S{kind}{h}0")
                        pe.matmul(ps[:, 0:P], qT[r, c, 0:P], kT[r, w, 0:P], start=True, stop=True)
                        pe.matmul(ps[:, P:3 * P], qT[r, c, P:TOKENS], kT[r, w, :], start=True, stop=True).then_inc(done, 1)
                    elif e == "T":
                        pe.wait_ge(probs, l * 16 + (16 + u + 1))
                        turn(part, f"T{kind}{h}0", lambda c: L[:, c * P:(c + 1) * P], n=3)
                    elif e == "V":
                        if u == 0:
                            bp, before = part.turn("panel", "vsg")
                            pe.wait_ge(panel_evicted[bp], before * 2 + 2)
                        open_group(u, l * 4 + 4)
                        wait_evicted(part, f"T{kind}{h}0")
                        hd = slice((h % GROUP) * HD, (h % GROUP + 1) * HD)
                        s = w * P + HD * (h // 4)
                        pe.matmul(heads_out[:, 0, hd], PT[:, 0:P], vsw[:, 0, s:s + HD], start=True, stop=True)
                        pe.matmul(heads_out[:, 1, hd], PT[:, P:2 * P], vsw[:, 0, s:s + HD], start=True, stop=False)
                        mm = pe.matmul(heads_out[:, 1, hd], PT[:, 2 * P:3 * P], vsw[:, 1, s:s + HD], start=False, stop=True)
                        mm.then_inc(group_done if u % GROUP == GROUP - 1 else pv_done, 1)
                    elif e == "cmpH":
                        compress()
                    elif e == "cmp2":
                        compress_2()
                    elif e == "cmpS":
                        compressed_scores()
                    elif e == "PcT":
                        pe.wait_ge(cmp_exp, l + 1)
                        turn(part, "PcT", lambda c: Pc[:, c, :])
                    elif e[0] == "R":
                        ret_scores(int(e[1]))
                    elif e == "rot":
                        for b in range(NB):
                            pe.wait_ge(rot_ready, l * 2 + (b + 1))
                            turn(part, f"rot{b}", lambda c: staged[:, b, 0, c * P:(c + 1) * P])
                    elif e == "oR":
                        for b in range(NB):
                            pe.wait_ge(ret_ready, l * 2 + (b + 1))
                            turn(part, f"oR{b}", lambda c: two("or").rearrange("p (b n) -> p b n", b=2)[:, b, c * P:(c + 1) * P])
                    elif e == "cv":
                        pe.wait_ge(conv_ready, l + 1)
                        for b in range(NB):
                            turn(part, f"cv{b}", lambda c: acc[:, c, b * P:(b + 1) * P])
                    elif e == "cz":
                        for b in range(NB):
                            pe.wait_ge(conv_normed, l * 2 + (b + 1))
                            turn(part, f"cz{b}", lambda c: staged[:, b, 1, c * P:(c + 1) * P])
                    elif e == "y":
                        for b in range(NB):
                            pe.wait_ge(y_ready, l * 2 + (4 + 2))
                            turn(part, f"y{b}", lambda c: two("y").rearrange("p (b n) -> p b n", b=2)[:, b, c * P:(c + 1) * P])

                for p in LAYER_WIDE:
                    rows_out(part, p, lhs_h, two_halves(p), 512, LAYER_PLAN, step_layer)
                    if p == "mg0":
                        compressed_out()
                    elif p == "mg1":
                        retention_out()
                last = {}
                for name in transposed("oR") + transposed("y"):
                    last[part.turn("tile", name)[0]] = name
                for name in last.values():
                    wait_evicted(part, name)
                brT = two("brT").rearrange("p (i c t) -> p i c t", i=3, c=4)
                for i in range(3):
                    if i == 2:
                        pe.wait_ge(branch_ready, l + 1)
                    for c in range(2):
                        rows_out(part, f"br{i}{c}", lambda k, b: brT[:, i, k, b * P:(b + 1) * P], [f"br{i}{c}/0"])
                turn_rows(part, "m", merged, l * 2 + 2)
                operand_ready(part, "m")
                for c in range(2):
                    rows_out(part, f"wo{c}", lhs_h, two_halves(f"wo{c}"))
                turn_rows(part, "z", h_ready, l * 4 + 4)
                operand_ready(part, "z")
                for i in range(FF_PANELS):
                    columns_out(part, f"ff{i}")
                ffT = area[:, AREA_2["mgt"][0]:AREA_2["mgt"][0] + 8192].rearrange("p (k t) -> p k t", k=32)
                pe.wait_ge(squared, l * 16 + 16)
                for c in range(2):
                    rows_out(part, f"down{c}", lambda k, b: ffT[:, k, b * P:(b + 1) * P], [f"down{c}/{i}" for i in range(8)])

        @block.scalar
        def _(act):
            def row_squares(b, n):
                return act.activation(tok[:, b, :], x[:, b, :], ACT.Square, accum_out=ss[:, b:b + 1]).then_inc(squares, 1)

            part = part_1
            act.wait_ge(x_loaded, 16)
            for b in range(NB):
                row_squares(b, b)
            rows = area[:, AREA_1["E"][0]:AREA_1["E"][0] + 2560].rearrange("p (t j) -> p t j", t=5)
            for t in range(5):
                ps = tile_of(act, part, f"bias{t}")
                act.activation(rows[0:H, t, :], ps[0:H, :], ACT.Copy).then_inc(tile_sem(part, f"bias{t}"), 1)
            for t in range(5):
                b, before = part.turn("tile", f"bias{t}")
                act.wait_ge(tile_evicted[b], before + 1)
                act.dma_start(bias_rows[t], rows[0:H, t, :]).then_inc(rows_stored, 16)

            squares_of = one("L").rearrange("p (b n) -> p b n", b=6)
            gain = dict(qa=0, kava=1, qb0=2, qb1=2, qb2=2, kb0=3, kb1=3, kb2=3)

            def evict_heads(n):
                p = NORMED[n]
                col = 8 + gain[p]
                for b in range(NB):
                    ps = tile_of(act, part, f"{p}{b}")
                    if n == 0 and b == 0:
                        act.wait_ge(cw_ready, 1)
                    if p == "kava":
                        to, w = one("kaT")[:, b * P:(b + 1) * P], P
                        src = ps[:, 0:P]
                    else:
                        g = int(p[2]) if len(p) == 3 else 0
                        region = "qaT" if p == "qa" else p[0:2] + "T"
                        base = AREA_1[region][0] + g * 1024
                        to = area[:, base:base + 1024].rearrange("p (c t) -> p c t", c=4)[:, :, b * P:(b + 1) * P]
                        src = ps[:, :].rearrange("p (c t) -> p c t", c=4)
                    act.activation(to, src, ACT.Identity, scale=first[:, col:col + 1])\
                       .then_inc(tile_sem(part, f"{p}{b}"), 1)

            act.wait_ge(pad_ready, PADS)
            units = units_first()

            def exp_first(u):
                kind, h, n = units[u]
                L = one("L").rearrange("p (s b j) -> p s b j", s=2, b=2)[:, u % 2]
                act.wait_ge(logits, u + 1)
                if kind == "A":
                    act.activation(sinks[:, :, u:u + 1], sinks[:, :, u:u + 1], ACT.Exp)
                for b in range(NB):
                    e = act.activation(L[:, b, 0:n * TOKENS], L[:, b, 0:n * TOKENS], ACT.Exp, bias=negmax[:, b, u:u + 1],
                                       accum_out=den[:, b, u:u + 1])
                e.then_inc(probs, 1)

            def step_first(e, u):
                kind, h, n = units[u]
                if e == "S" and u == 0:
                    exp_first(0)
                elif e == "T":
                    PT = one("PT").rearrange("p (s g j) -> p s g j", s=2, g=3)[:, u % 2]
                    if u >= 2:
                        wait_products(act, part, u - 2)
                    for g in (0, 2)[:n]:
                        ps = tile_of(act, part, f"T{kind}{h}{g}")
                        act.activation(PT[:, g, :], ps[:, :], ACT.Copy).then_inc(tile_sem(part, f"T{kind}{h}{g}"), 1)
                elif e == "V" and u + 1 < len(units):
                    exp_first(u + 1)

            for n, p in enumerate(FIRST_PANELS[:17]):
                for s in range(KC):
                    for e, u in FIRST_PLAN.get((p, s), []):
                        step_first(e, u)
                ps = panel_of(act, part, p)
                if n < len(NORMED):
                    for b in range(NB):
                        w = P if p == "kava" else 512
                        if n >= 1:
                            act.wait_ge(head_sum, NB * (n - 1) + b + 1)
                        act.activation(squares_of[:, b, 0:w], ps[:, b, 0:w], ACT.Square).then_inc(head_sq, 1)
                elif p in ("vb0", "vb1", "vb2"):
                    g = int(p[2])
                    to = one("vb").rearrange("p (g b n) -> p g b n", g=3, b=2)
                    for b in range(NB):
                        act.activation(to[:, g, b, :], ps[:, b, :], ACT.Copy).then_inc(panel_sem(part, p), 1)
                elif p in ("ga", "gb"):
                    to = one("mgt").rearrange("p (b n) -> p b n", b=8)
                    for b in range(NB):
                        act.activation(to[:, b + 2 * (p == "gb"), :], ps[:, b, :], ACT.Tanh, scale=0.5).then_inc(gate_tanh, 1)
                else:
                    c = int(p[2])
                    to = one("mgt").rearrange("p (b n) -> p b n", b=2)
                    src = tok[:, :, :].rearrange("p b (s n) -> p b s n", s=2)
                    if c == 0:
                        bg, before = part.turn("panel", "gb")
                        act.wait_ge(panel_evicted[bg], before * 2 + 2)
                    for b in range(NB):
                        act.wait_ge(merge_sum, NB * c + b + 1)
                        act.activation(to[:, b, c * 512:(c + 1) * 512], src[:, b, c % 2, :], ACT.Tanh, scale=0.5)\
                           .then_inc(merge_tanh, 1)
                if 1 <= n <= len(NORMED):
                    evict_heads(n - 1)

            yT = one("yT").rearrange("p (i c t) -> p i c t", i=2, c=4)
            for t, name in enumerate(("yA", "yB")):
                for b in range(NB):
                    ps = tile_of(act, part, f"{name}{b}")
                    act.activation(yT[:, t, :, b * P:(b + 1) * P], ps[:, :].rearrange("p (c t) -> p c t", c=4), ACT.Copy)\
                       .then_inc(tile_sem(part, f"{name}{b}"), 1)

            def evict_merged(part):
                for b in range(NB):
                    for i in range(2):
                        ps = tile_of(act, part, f"m{b}{i}")
                        act.activation(hT[:, 4 * i:4 * i + 4, b * P:(b + 1) * P], ps[:, :].rearrange("p (c t) -> p c t", c=4),
                                       ACT.Copy, scale=0.5).then_inc(tile_sem(part, f"m{b}{i}"), 1)

            evict_merged(part)

            with act.Fori(0, LAYERS) as l:
                part = layer(l)
                act.wait_ge(x_updated, l * 2 + 1)
                for b in range(NB):
                    row_squares(b, 0)
                tz = two("tz").rearrange("p (b n) -> p b n", b=2)
                ps = panel_of(act, part, "cb")
                for b in range(NB):
                    act.activation(tz[:, b, :], ps[:, b, :], ACT.Tanh, scale=0.5).then_inc(panel_sem(part, "cb"), 1)
                qT = two("qT").rearrange("p (b n) -> p b n", b=2)
                ps = panel_of(act, part, "q")
                for b in range(NB):
                    act.activation(qT[:, b, :], ps[:, b, :], ACT.Copy, scale=HD ** -0.5).then_inc(panel_sem(part, "q"), 1)
                ps = panel_of(act, part, "k4")
                act.activation(two("kT"), ps[:, 1, :], ACT.Copy).then_inc(panel_sem(part, "k4"), 1)
                ps = panel_of(act, part, "vsg")
                vsw = two("vsw").rearrange("p (b n) -> p b n", b=2)
                gt = two("gt").rearrange("p (b n) -> p b n", b=2)
                for b in range(NB):
                    act.activation(vsw[:, b, :], ps[:, b, 0:256], ACT.Copy)
                    act.activation(gt[:, b, :], ps[:, b, 256:280], ACT.Tanh, scale=0.5).then_inc(panel_sem(part, "vsg"), 1)
                rT = two("rT").rearrange("p (c t) -> p c t", c=4)
                mgt = two("mgt").rearrange("p (b n) -> p b n", b=2)
                z = two("z").rearrange("p (c t) -> p c t", c=4)
                brT = two("brT").rearrange("p (i c t) -> p i c t", i=3, c=4)
                units = units_layer()

                def exp_layer(u):
                    L = two("L").rearrange("p (s j) -> p s j", s=2)[:, u % 2]
                    act.wait_ge(logits, l * 16 + (16 + u + 1))
                    act.activation(L[:, 0:P], L[:, 0:P], ACT.Exp, bias=negmax[:, 0, u:u + 1], accum_out=den[:, 0, u:u + 1])
                    act.activation(L[:, P:3 * P], L[:, P:3 * P], ACT.Exp, bias=negmax[:, 1, u:u + 1],
                                   accum_out=den[:, 1, u:u + 1]).then_inc(probs, 1)

                def step_layer(e, u):
                    kind, h, _ = units[u]
                    if e == "S" and u == 0:
                        exp_layer(0)
                    elif e == "T":
                        PT = two("PT").rearrange("p (s j) -> p s j", s=2)[:, u % 2]
                        if u >= 2:
                            wait_products(act, part, u - 2)
                        ps = tile_of(act, part, f"T{kind}{h}0")
                        act.activation(PT, ps[:, 0:3 * P], ACT.Copy).then_inc(tile_sem(part, f"T{kind}{h}0"), 1)
                    elif e == "V" and u + 1 < len(units):
                        exp_layer(u + 1)
                    elif e == "cmpH":
                        act.wait_ge(hid_in, l + 1)
                        act.activation(two("ht"), two("hy"), ACT.Tanh, scale=GELU_C).then_inc(hid_tanh, 1)
                    elif e == "rot":
                        for b in range(NB):
                            ps = tile_of(act, part, f"rot{b}")
                            act.activation(rT[:, :, b * P:(b + 1) * P], ps[:, :].rearrange("p (c t) -> p c t", c=4), ACT.Copy)\
                               .then_inc(tile_sem(part, f"rot{b}"), 1)
                    elif e == "cmp2":
                        ps = tile_of(act, part, "cmp2")
                        act.activation(two("kcmpT")[:, 0:30], ps[:, 0:30], ACT.Copy, scale=0.5)
                        vblk = two("vblk").rearrange("p (g i d) -> p g i d", g=2, i=4)
                        for i in range(4):
                            r = slice(32 * i, 32 * i + 32)
                            c = act.activation(vblk[r, :, i, :], ps[r, 64:64 + 2 * HD].rearrange("p (g d) -> p g d", g=2),
                                               ACT.Copy, scale=0.5)
                        c.then_inc(tile_sem(part, "cmp2"), 1)
                    elif e == "cmpS":
                        act.wait_ge(cmp_logits, l + 1)
                        Pc = two("Pc").rearrange("p (s n) -> p s n", s=16)[:, :, 0:N_CMP]
                        act.activation(Pc, two("Lc").rearrange("p (s n) -> p s n", s=16), ACT.Exp).then_inc(cmp_exp, 1)
                    elif e == "PcT":
                        ps = tile_of(act, part, "PcT")
                        act.activation(two("PcT"), ps[:, :], ACT.Copy).then_inc(tile_sem(part, "PcT"), 1)
                    elif e == "y":
                        for b in range(NB):
                            ps = tile_of(act, part, f"y{b}")
                            act.activation(brT[:, 0, :, b * P:(b + 1) * P], ps[:, :].rearrange("p (c t) -> p c t", c=4),
                                           ACT.Copy, scale=0.5).then_inc(tile_sem(part, f"y{b}"), 1)
                    elif e == "cz":
                        for b in range(NB):
                            ps = tile_of(act, part, f"cz{b}")
                            for c in range(4):
                                i = act.activation(z[:, c, b * P:(b + 1) * P], ps[:, c * P:(c + 1) * P], ACT.Identity,
                                                   scale=lnh[:, 0, c:c + 1], bias=lnh[:, 1, c:c + 1])
                            i.then_inc(tile_sem(part, f"cz{b}"), 1)
                        act.drain()
                        act.activation(two("tz"), two("z"), ACT.Tanh).then_inc(conv_z, 1)

                for p in LAYER_WIDE:
                    for s in range(KC):
                        for e, u in LAYER_PLAN[p, s]:
                            step_layer(e, u)
                    if p == "qkr":
                        continue
                    ps = panel_of(act, part, p)
                    for b in range(NB):
                        if p == "vr":
                            act.activation(two("vr").rearrange("p (b n) -> p b n", b=2)[:, b, :], ps[:, b, :], ACT.Copy)\
                               .then_inc(panel_sem(part, p), 1)
                        elif p == "gr":
                            act.activation(two("tz").rearrange("p (b n) -> p b n", b=2)[:, b, :], ps[:, b, :],
                                           ACT.Tanh, scale=0.5).then_inc(gr_tanh, 1)
                        else:
                            i = int(p[2])
                            act.activation(mgt[:, b, i * 512:(i + 1) * 512], ps[:, b, :], ACT.Tanh, scale=0.5)\
                               .then_inc(panel_sem(part, p), 1)
                evict_merged(part)
                act.wait_ge(x_updated, l * 2 + 2)
                for b in range(NB):
                    row_squares(b, 0)
                ffT = area[:, AREA_2["mgt"][0]:AREA_2["mgt"][0] + 8192].rearrange("p (k t) -> p k t", k=16)
                rr = two("y")
                for i in range(FF_PANELS):
                    s = (i % 2) * 512
                    ps = panel_of(act, part, f"ff{i}")
                    act.activation(rr[:, s:s + 512], ps[:, 0, :], ACT.Relu).then_inc(panel_sem(part, f"ff{i}"), 1)
                    act.drain()
                    act.activation(ffT[:, 2 * i, :], rr[:, s:s + 512], ACT.Square).then_inc(squared, 1)
            act.wait_ge(x_updated, X_UPDATES)
            for b in range(NB):
                row_squares(b, 0)

        @block.vector
        def _(v):
            part = part_1
            v.memset(one("mgt")[32:33, 2560:2600], 1.0).then_inc(pad_ready, 1)
            v.memset(zero, 0.0).then_inc(pad_ready, 1)
            v.memset(low, -3.0e38).then_inc(pad_ready, 1)
            v.memset(half_power, -0.5).then_inc(pad_ready, 1)
            v.wait_ge(loaded, 16 * 7)
            for c in (8, 10):
                e = v.tensor_scalar(first[:, c:c + 1], first[:, c:c + 1], HD ** -0.5, None, ALU.mult)
            e.then_inc(cw_ready, 1)

            def rows_normed(part, base, tiles, gain):
                for b in range(NB):
                    v.wait_ge(rstd_ready, base + 1)
                    v.tensor_scalar(tok[:, b, :], x[:, b, :], rstd[:, b:b + 1], None, ALU.mult).then_inc(h_ready, 1)
                for b in range(NB):
                    for i in range(2):
                        ps = tile_of(v, part, f"{tiles}{b}{i}")
                        v.tensor_tensor(hT[:, 4 * i:4 * i + 4, b * P:(b + 1) * P], ps[:, :].rearrange("p (c t) -> p c t", c=4),
                                        gain[:, 4 * i:4 * i + 4].unsqueeze(2).broadcast_to([P, 4, P]), ALU.mult)\
                         .then_inc(tile_sem(part, f"{tiles}{b}{i}"), 1)

            rows_normed(part, 0, "x", first[:, 0:8])
            squares_of = one("L").rearrange("p (b n) -> p b n", b=6)
            staged = tok[:, :, :].rearrange("p b (s n) -> p b s n", s=2)
            units = units_first()
            Es = one("E").rearrange("p (s t j) -> p s t j", s=2, t=3)

            def logits_first(u):
                kind, h, n = units[u]
                L = one("L").rearrange("p (s b j) -> p s b j", s=2, b=2)[:, u % 2]
                mx = mxs[u % 2]
                load = h // 2 if kind == "A" else 4 + h
                v.wait_ge(E_loaded[load % 2], 16 * (load // 2 + 1))
                if u >= 2:
                    k2, h2, n2 = units[u - 2]
                    for g in range(n2):
                        tile_of(v, part, f"T{k2}{h2}{g}")
                for g in range(n):
                    ps = tile_of(v, part, f"S{kind}{h}{g}")
                    E = Es[:, load % 2, h % 2 if kind == "A" else g, :]
                    for b in range(NB):
                        init = first[:, 12 + h:13 + h] if kind == "A" else low
                        e = v.tensor_tensor_reduce(L[:, b, g * TOKENS:(g + 1) * TOKENS], ps[:, b * TOKENS:(b + 1) * TOKENS],
                                                   E[:, P * (1 - b):P * (1 - b) + TOKENS], 1.0, init, ALU.add, ALU.max,
                                                   mx[:, b, g:g + 1])
                    e.then_inc(tile_sem(part, f"S{kind}{h}{g}"), 1)
                v.drain()
                r = v.tensor_reduce(negmax[:, :, u:u + 1], mx[:, :, 0:n], AX.X, ALU.max, negate=True)
                if kind == "A":
                    v.drain()
                    r = v.tensor_scalar(sinks[:, :, u:u + 1], negmax[:, :, u:u + 1], first[:, 12 + h:13 + h], None, ALU.add)
                r.then_inc(logits, 1)
                if kind == "B" or h % 2 == 1:
                    v.sem_inc(E_used, 1)

            def step_first(e, u):
                kind, h, n = units[u]
                if e == "S":
                    logits_first(u)
                elif e == "T" and n == 3:
                    if u >= 2:
                        wait_products(v, part, u - 2)
                    PT = one("PT").rearrange("p (s g j) -> p s g j", s=2, g=3)[:, u % 2]
                    ps = tile_of(v, part, f"T{kind}{h}1")
                    v.tensor_copy(PT[:, 1, :], ps[:, :]).then_inc(tile_sem(part, f"T{kind}{h}1"), 1)
                elif e == "V" and u % GROUP == GROUP - 1:
                    normed_out(v, part, u // GROUP)

            for n, p in enumerate(FIRST_PANELS[:17]):
                for s in range(KC):
                    for e, u in FIRST_PLAN.get((p, s), []):
                        step_first(e, u)
                if n < len(NORMED):
                    nh = 2 if p == "kava" else 8
                    for b in range(NB):
                        v.wait_ge(head_sq, NB * n + b + 1)
                        if n >= 1:
                            v.wait_ge(head_rstd, n)
                        v.tensor_reduce(hs[:, b, 0:nh], squares_of[:, b, 0:nh * HD].rearrange("p (h d) -> p h d", d=HD),
                                        AX.X, ALU.add).then_inc(head_sum, 1)
                    ps = panel_of(v, part, p)
                    v.wait_ge(head_rstd, n + 1)
                    for b in range(NB):
                        if n >= 2:
                            tile_of(v, part, f"{NORMED[n - 2]}{b}")
                        e = v.tensor_tensor(staged[:, b, n % 2, 0:nh * HD].rearrange("p (h d) -> p h d", d=HD),
                                            ps[:, b, 0:nh * HD].rearrange("p (h d) -> p h d", d=HD),
                                            hr[:, b, 0:nh].unsqueeze(2).broadcast_to([P, nh, HD]), ALU.mult)
                        e.then_inc(head_normed, 1)
                        if p == "kava":
                            va = one("va").rearrange("p (b n) -> p b n", b=2)
                            v.tensor_copy(va[:, b, :], ps[:, b, P:2 * P])\
                             .then_inc(panel_sem(part, p), 1)
                    if p != "kava":
                        for b in range(NB):
                            v.wait_ge(head_normed, NB * n + b + 1)
                            v.sem_inc(panel_sem(part, p), 1)
                elif p in ("ga", "gb"):
                    ps = panel_of(v, part, p)
                    i = int(p == "gb")
                    t = one("mgt").rearrange("p (b n) -> p b n", b=8)
                    to = one("sga" if p == "ga" else "sgb").rearrange("p (b n) -> p b n", b=2)
                    for b in range(NB):
                        v.wait_ge(gate_tanh, NB * i + b + 1)
                        v.scalar_tensor_tensor(to[:, b, :], t[:, b + 2 * i, :], 1.0, ps[:, b, :], ALU.add, ALU.mult)\
                         .then_inc(panel_sem(part, p), 1)
                elif p.startswith("mg"):
                    ps = panel_of(v, part, p)
                    c = int(p[2])
                    bm = one("bm")[:, c * 512:(c + 1) * 512]
                    v.wait_ge(bmerge_loaded, 16)
                    if c == 0:
                        for b in range(NB):
                            tile_of(v, part, f"kb2{b}")
                            tile_of(v, part, f"kb1{b}")
                    for b in range(NB):
                        if c >= 2:
                            v.wait_ge(merge_tanh, NB * (c - 2) + b + 1)
                        v.tensor_tensor(staged[:, b, c % 2, :], ps[:, b, :], bm, ALU.add).then_inc(merge_sum, 1)
                    for b in range(NB):
                        v.wait_ge(merge_sum, NB * c + b + 1)
                        v.sem_inc(panel_sem(part, p), 1)
            def merge(part, branches, mgt, width, updates):
                for i in range(branches):
                    for c in range(2):
                        ps = panel_of(v, part, f"br{i}{c}")
                        cs = slice(c * 512, (c + 1) * 512)
                        for b in range(NB):
                            g = mgt[:, b, i * D + c * 512:i * D + (c + 1) * 512]
                            if i == 0:
                                v.scalar_tensor_tensor(tok[:, b, cs], g, 1.0, ps[:, b, :], ALU.add, ALU.mult)\
                                 .then_inc(panel_sem(part, f"br{i}{c}"), 1)
                            else:
                                v.scalar_tensor_tensor(g, g, 1.0, ps[:, b, :], ALU.add, ALU.mult)\
                                 .then_inc(panel_sem(part, f"br{i}{c}"), 1)
                        if i:
                            v.drain()
                            for b in range(NB):
                                g = mgt[:, b, i * D + c * 512:i * D + (c + 1) * 512]
                                e = v.tensor_tensor(tok[:, b, cs], tok[:, b, cs], g, ALU.add)
                                if i == branches - 1 and c == 1:
                                    e.then_inc(merged, 1)

            def residual(part, names):
                for c, name in enumerate(names):
                    ps = panel_of(v, part, name)
                    cs = slice(c * 512, (c + 1) * 512)
                    for b in range(NB):
                        v.tensor_tensor(x[:, b, cs], x[:, b, cs], ps[:, b, :], ALU.add).then_inc(panel_sem(part, name), 1)
                v.drain().then_inc(x_updated, 1)

            v.wait_ge(merge_tanh, NB * 4)
            merge(part, 2, one("mgt").rearrange("p (b n) -> p b n", b=2), 2 * D, 0)
            residual(part, ("wo0", "wo1"))
            u_all = two("u").rearrange("p (c t) -> p c t", c=4)
            hgv = two("hgv").rearrange("p (g q n) -> p g q n", g=2, q=4)
            v.memset(u_all[:, :, 0:32], 0.0)
            v.memset(two("hgv"), 0.0)
            v.memset(two("Pc"), 0.0)
            v.memset(two("hx"), 0.0)
            v.memset(two("vblk"), 0.0)
            v.drain()

            with v.Fori(0, LAYERS) as l:
                part = layer(l)
                v.wait_ge(par_loaded, l * 16 + 16)
                v.tensor_scalar(cw[:, :, :], pars("conv_w").rearrange("p (c j) -> p c j", c=4), 0.5, None, ALU.mult)
                for i, name in enumerate(("ln_g", "ln_b", "gn")):
                    v.tensor_scalar(lnh[:, i, :], pars(name), 0.5, None, ALU.mult)
                v.drain().then_inc(cw_ready, 1)
                rows_normed(part, l * 2 + 1, "x", pars("mix"))
                tz = two("tz").rearrange("p (b n) -> p b n", b=2)
                bc, before = part.turn("panel", "cb")
                v.wait_ge(panel_evicted[bc], before * 2 + 2)
                ps = panel_of(v, part, "ca")
                for b in range(NB):
                    v.scalar_tensor_tensor(u_all[:, 2 * b:2 * b + 2, 32:288], tz[:, b, :].rearrange("p (c t) -> p c t", c=2), 1.0,
                                           ps[:, b, :].rearrange("p (c t) -> p c t", c=2), ALU.add, ALU.mult)\
                     .then_inc(panel_sem(part, "ca"), 1)
                v.drain()
                acc = two("acc").rearrange("p (c t) -> p c t", c=4)
                cb_ = pars("conv_b")

                def taps(first_tap, last_tap):
                    for j in range(first_tap, last_tap):
                        for c in range(4):
                            src = u_all[:, c, 2 + j:2 + j + TOKENS]
                            if j == 0:
                                v.tensor_scalar(acc[:, c, :], src, cw[:, c, 0:1], cb_[:, c:c + 1], ALU.mult, ALU.add)
                            else:
                                v.scalar_tensor_tensor(acc[:, c, :], src, cw[:, c, j:j + 1], acc[:, c, :], ALU.mult, ALU.add)
                        v.drain()

                ps = panel_of(v, part, "k4")
                kcP = two("kcP").rearrange("p (i g t) -> p i g t", i=2, g=2)
                for i in range(2):
                    for g in range(2):
                        s = i * TOKENS
                        rows = slice(HD * g, HD * g + HD)
                        v.tensor_copy(kcP[0:HD, i, g, :], ps[rows, 0, s:s + TOKENS])
                        e = v.tensor_copy(kcP[HD:P, i, g, 0:TOKENS - 1], ps[rows, 0, s + 1:s + TOKENS])
                e.then_inc(panel_sem(part, "k4"), 1)
                v.drain()
                blk = two("blk").rearrange("p (i j n) -> p i j n", i=2, j=16)
                pe_ = pars("pe").rearrange("p (i j) -> p i j", i=2)
                for i in range(2):
                    for g in range(2):
                        lo = kcP[:, i, g, :].rearrange("p (n j s) -> p j n s", j=8, s=2)
                        for half in range(2):
                            src = lo[:, :, half:half + N_CMP, 0]
                            e = v.tensor_tensor(blk[:, i, 8 * half:8 * half + 8, g * N_CMP:(g + 1) * N_CMP], src,
                                                pe_[:, i, 8 * half:8 * half + 8].unsqueeze(2).broadcast_to([P, 8, N_CMP]), ALU.add)
                    e.then_inc(blocks_ready, 1)
                units = units_layer()
                En = two("En").rearrange("p (h j) -> p h j", h=H)
                Lc = two("Lc").rearrange("p (b h n) -> p b h n", b=2, h=H)
                PR = two("PR").rearrange("p (h n) -> p h n", h=RET_H)
                hx, hy, ht = two("hx"), two("hy"), two("ht")
                gt = two("gt").rearrange("p (b h i) -> p b h i", b=2, h=H)
                brT = two("brT").rearrange("p (i c t) -> p i c t", i=3, c=4)
                sgr = two("sgr").rearrange("p (b n) -> p b n", b=2)
                o_r = two("or").rearrange("p (b n) -> p b n", b=2)

                def logits_layer(u):
                    kind, h, _ = units[u]
                    mx = mxs[u % 2]
                    L = two("L").rearrange("p (s j) -> p s j", s=2)[:, u % 2]
                    if u >= 2:
                        k2, h2, _ = units[u - 2]
                        tile_of(v, part, f"T{k2}{h2}0")
                        v.sem_inc(taken, 1)
                    elif u == 0:
                        v.wait_ge(En_loaded, 16)
                    ps = tile_of(v, part, f"S{kind}{h}0")
                    v.sem_inc(taken, 1)
                    v.tensor_tensor_reduce(L[:, 0:P], ps[:, 0:P], En[:, h, P:2 * P], 1.0, -3.0e38, ALU.add, ALU.max, mx[:, 0, 0:1])
                    v.tensor_tensor_reduce(L[:, P:3 * P], ps[:, P:3 * P], En[:, h, 0:TOKENS], 1.0, -3.0e38, ALU.add, ALU.max,
                                           mx[:, 1, 0:1]).then_inc(tile_sem(part, f"S{kind}{h}0"), 1)
                    v.drain()
                    v.tensor_scalar(negmax[:, :, u:u + 1], mx[:, :, 0:1], -1.0, None, ALU.mult).then_inc(logits, 1)

                def gelu():
                    ps = tile_of(v, part, "cmpH")
                    v.tensor_copy(hx[:, 0:30], ps[:, 0:30])
                    v.tensor_copy(hx[:, 32:62], ps[:, 32:62]).then_inc(tile_sem(part, "cmpH"), 1)
                    v.drain()
                    v.tensor_tensor(hy, hx, hx, ALU.mult)
                    v.drain()
                    v.tensor_scalar(hy, hy, GELU_A, 1.0, ALU.mult, ALU.add)
                    v.drain()
                    v.tensor_tensor(hy, hy, hx, ALU.mult).then_inc(hid_in, 1)
                    v.wait_ge(hid_tanh, l + 1)
                    v.scalar_tensor_tensor(two("hgk"), ht[:, 0:32], 1.0, hx[:, 0:32], ALU.add, ALU.mult).then_inc(hid_ready, 1)
                    for g in range(2):
                        s = 32 + g * N_CMP
                        e = v.scalar_tensor_tensor(hgv[:, g, :, 0:N_CMP], ht[:, s:s + N_CMP].unsqueeze(1).broadcast_to([P, 4, N_CMP]),
                                                   1.0, hx[:, s:s + N_CMP].unsqueeze(1).broadcast_to([P, 4, N_CMP]), ALU.add, ALU.mult)
                    e.then_inc(hid_ready, 1)

                def rotate():
                    ps = panel_of(v, part, "qkr")
                    t4 = two("or").rearrange("p (i h d) -> p i h d", i=4, h=8)
                    for b in range(NB):
                        src = ps[:, b, :].rearrange("p (h s d) -> p h s d", h=8, s=2)
                        dst = staged[:, b, 0, :].rearrange("p (h s d) -> p h s d", h=8, s=2)
                        cos, sin = (rope[:, b, i, :].unsqueeze(1).broadcast_to([P, 8, 32]) for i in range(2))
                        v.tensor_tensor(t4[:, 0], src[:, :, 0, :], cos, ALU.mult)
                        v.tensor_tensor(t4[:, 1], src[:, :, 1, :], sin, ALU.mult)
                        v.tensor_tensor(t4[:, 2], src[:, :, 0, :], sin, ALU.mult)
                        v.tensor_tensor(t4[:, 3], src[:, :, 1, :], cos, ALU.mult).then_inc(panel_sem(part, "qkr"), 1)
                        v.drain()
                        v.tensor_tensor(dst[:, :, 0, :], t4[:, 0], t4[:, 1], ALU.subtract)
                        v.tensor_tensor(dst[:, :, 1, :], t4[:, 2], t4[:, 3], ALU.add).then_inc(rot_ready, 1)
                        v.drain()

                def compressed_logits():
                    for g in range(2):
                        ps = tile_of(v, part, f"cmpS{g}")
                        for b in range(NB):
                            s = 31 + P * (1 - b)
                            src = ps[:, b * 4 * N_CMP:(b + 1) * 4 * N_CMP].rearrange("p (h n) -> p h n", h=4)
                            hg = slice(4 * g, 4 * g + 4)
                            e = v.tensor_tensor(Lc[:, b, hg], src, En[:, hg, s:s + (N_CMP - 1) * CMP_STRIDE + 1:CMP_STRIDE], ALU.add)
                        e.then_inc(tile_sem(part, f"cmpS{g}"), 1)
                    v.drain()
                    v.tensor_reduce(cmx[:, :, :], Lc[:, :, :, :], AX.X, ALU.max)
                    v.drain()
                    v.tensor_scalar(cmx[:, :, :], cmx[:, :, :], -1.0e29, None, ALU.max)
                    v.drain()
                    v.tensor_tensor(Lc[:, :, :, :], Lc[:, :, :, :], cmx[:, :, :].unsqueeze(3).broadcast_to([P, 2, H, N_CMP]),
                                    ALU.subtract).then_inc(cmp_logits, 1)

                def compressed_coefficients():
                    v.wait_ge(cmp_exp, l + 1)
                    Pc = two("Pc").rearrange("p (b h n) -> p b h n", b=2, h=H)
                    v.tensor_reduce(cden[:, :, :], Pc[:, :, :, 0:N_CMP], AX.X, ALU.add)
                    v.drain()
                    v.tensor_scalar(cden[:, :, :], cden[:, :, :], 1e-30, None, ALU.max)
                    v.drain()
                    v.reciprocal(cden[:, :, :], cden[:, :, :])
                    v.drain()
                    v.scalar_tensor_tensor(coef_c[:, :, :], gt[:, :, :, 0], 1.0, cden[:, :, :], ALU.add, ALU.mult)

                def decayed(h):
                    ps = tile_of(v, part, f"R{h}")
                    v.tensor_tensor(PR[:, h, 0:TOKENS], ps[:, 0:TOKENS], decay[:, h, :], ALU.mult)
                    v.tensor_tensor(PR[:, h, TOKENS:TOKENS + P], ps[:, TOKENS:TOKENS + P], decay[:, h, 0:P], ALU.mult)\
                     .then_inc(tile_sem(part, f"R{h}"), 1)

                def compressed_out():
                    yc = two("yc").rearrange("p (b n) -> p b n", b=2)
                    ps = panel_of(v, part, "Oc")
                    for b in range(NB):
                        v.tensor_tensor(yc[:, b, :].rearrange("p (h d) -> p h d", h=H), ps[:, b, :].rearrange("p (h d) -> p h d", h=H),
                                        coef_c[:, b, :].unsqueeze(2).broadcast_to([P, H, HD]), ALU.mult)\
                         .then_inc(panel_sem(part, "Oc"), 1)

                def retention_norm():
                    ps = panel_of(v, part, "Or")
                    for b in range(NB):
                        for h in range(RET_H):
                            v.bn_stats(bns[:, 4 * b + h, :], ps[:, b, h * P:(h + 1) * P])
                    v.drain()
                    for i in range(8):
                        v.bn_aggr(bna[:, i, :], bns[:, i, :])
                    v.drain().then_inc(ret_stats, 1)
                    v.wait_ge(ret_rstd, l + 1)
                    for b in range(NB):
                        for h in range(RET_H):
                            hv = slice(h * P, (h + 1) * P)
                            v.tensor_scalar(o_r[:, b, hv], ps[:, b, hv], bna[:, 4 * b + h, 0:1], brs[:, b, h:h + 1],
                                            ALU.subtract, ALU.mult)
                        v.drain().then_inc(panel_sem(part, "Or"), 1)
                        v.tensor_tensor(o_r[:, b, :], o_r[:, b, :], sgr[:, b, :], ALU.mult).then_inc(ret_ready, 1)

                def step_layer(e, u):
                    if e == "S":
                        logits_layer(u)
                    elif e in ("T", "V"):
                        taps(2 * u + (e == "V"), min(2 * u + (e == "V") + 1, TAPS))
                        if e == "V" and u % GROUP == GROUP - 1:
                            sum_out(v, part, l, u // GROUP)
                        if 2 * u + (e == "V") == TAPS - 1:
                            v.sem_inc(conv_ready, 1)
                    elif e == "cmpH":
                        gelu()
                    elif e == "rot":
                        pass
                    elif e == "cmpS":
                        compressed_logits()
                    elif e == "PcT":
                        compressed_coefficients()
                    elif e[0] == "R":
                        decayed(int(e[1]))
                    elif e == "oR":
                        for b in range(NB):
                            ps = tile_of(v, part, f"oR{b}")
                            v.tensor_tensor(brT[:, 1, :, b * P:(b + 1) * P], ps[:, :].rearrange("p (c t) -> p c t", c=4),
                                            lnh[:, 2, :].unsqueeze(2).broadcast_to([P, 4, P]), ALU.mult)\
                             .then_inc(tile_sem(part, f"oR{b}"), 1)
                    elif e == "cv":
                        pss = [tile_of(v, part, f"cv{b}") for b in range(NB)]
                        for b in range(NB):
                            v.bn_stats(cns[:, b, :], pss[b][:, :])
                        v.drain()
                        for b in range(NB):
                            v.bn_aggr(cna[:, b, :], cns[:, b, :])
                        v.drain().then_inc(conv_stats, 1)
                        v.wait_ge(conv_rstd, l + 1)
                        for b in range(NB):
                            v.tensor_scalar(staged[:, b, 1, :], pss[b][:, :], cna[:, b, 0:1], crs[:, b:b + 1], ALU.subtract, ALU.mult)
                            v.drain().then_inc(tile_sem(part, f"cv{b}"), 1)
                            v.sem_inc(conv_normed, 1)

                for p in LAYER_WIDE:
                    for s in range(KC):
                        for e, u in LAYER_PLAN[p, s]:
                            step_layer(e, u)
                    if p == "qkr":
                        rotate()
                    elif p == "gr":
                        ps = panel_of(v, part, "gr")
                        tg = two("tz").rearrange("p (b n) -> p b n", b=2)
                        for b in range(NB):
                            v.wait_ge(gr_tanh, l * 2 + (b + 1))
                            v.scalar_tensor_tensor(sgr[:, b, :], tg[:, b, :], 1.0, ps[:, b, :], ALU.add, ALU.mult)\
                             .then_inc(panel_sem(part, "gr"), 1)
                    elif p == "mg0":
                        compressed_out()
                    elif p == "mg1":
                        retention_norm()
                v.wait_ge(conv_z, l + 1)
                v.scalar_tensor_tensor(brT[:, 2].rearrange("p c t -> p (c t)"), two("tz"), 1.0, two("z"), ALU.add, ALU.mult).then_inc(branch_ready, 1)
                merge(part, 3, two("mgt").rearrange("p (b n) -> p b n", b=2), 3 * D, 0)
                residual(part, ("wo0", "wo1"))
                rows_normed(part, l * 2 + 2, "z", pars("mlp"))
                ffT = area[:, AREA_2["mgt"][0]:AREA_2["mgt"][0] + 8192].rearrange("p (k t) -> p k t", k=16)
                rr = two("tmp")
                for i in range(FF_PANELS):
                    s = (i % 2) * 512
                    ps = panel_of(v, part, f"ff{i}")
                    v.tensor_scalar(rr[:, s:s + 512], ps[:, 1, :], 0.0, None, ALU.max).then_inc(panel_sem(part, f"ff{i}"), 1)
                    v.drain()
                    v.tensor_tensor(ffT[:, 2 * i + 1, :], rr[:, s:s + 512], rr[:, s:s + 512], ALU.mult).then_inc(squared, 1)
                residual(part, ("down0", "down1"))
            v.wait_ge(rstd_ready, 2 * LAYERS + 2)
            v.wait_ge(final_loaded, 16)
            for b in range(NB):
                v.scalar_tensor_tensor(tok[:, b, :], x[:, b, :], rstd[:, b:b + 1], two("mgt")[:, 0:D], ALU.mult, ALU.mult)\
                 .then_inc(x_updated, 1)

        @block.gpsimd
        def _(g):
            def inverse_root(to, of, scale, out_sem, shape_power):
                g.sem_inc(taken, 1)
                g.tensor_scalar(to, of, scale, EPS, ALU.mult, ALU.add)
                g.drain()
                g.tensor_tensor(to, to, shape_power, ALU.pow).then_inc(out_sem, 1)

            g.wait_ge(pad_ready, PADS)
            g.wait_ge(squares, 2)
            inverse_root(rstd, ss, 1.0 / D, rstd_ready, half_power[:, 0:2])
            for n, p in enumerate(NORMED):
                nh = 2 if p == "kava" else 8
                g.wait_ge(head_sum, NB * (n + 1))
                if n >= 1:
                    g.wait_ge(head_normed, NB * n)
                inverse_root(hr[:, :, 0:nh], hs[:, :, 0:nh], 1.0 / HD, head_rstd,
                             half_power[:, 0:nh].unsqueeze(1).broadcast_to([P, 2, nh]))
            with g.Fori(0, LAYERS) as l:
                g.wait_ge(squares, l * 4 + 4)
                inverse_root(rstd, ss, 1.0 / D, rstd_ready, half_power[:, 0:2])
                g.wait_ge(ret_stats, l + 1)
                inverse_root(brs[:, :, :], bna[:, :, 1:2].rearrange("p (b h) o -> p b (h o)", b=2), 1.0, ret_rstd,
                             half_power[:, 0:4].unsqueeze(1).broadcast_to([P, 2, 4]))
                g.wait_ge(conv_stats, l + 1)
                inverse_root(crs, cna[:, :, 1], 1.0, conv_rstd, half_power[:, 0:2])
                g.wait_ge(squares, l * 4 + 6)
                inverse_root(rstd, ss, 1.0 / D, rstd_ready, half_power[:, 0:2])
            g.wait_ge(squares, 4 * LAYERS + 4)
            inverse_root(rstd, ss, 1.0 / D, rstd_ready, half_power[:, 0:2])


PAIRS = [0, 4, 1, 5, 2, 6, 3, 7]


def t5_bucket(rel):
    n = np.abs(rel)
    nf = np.maximum(n, 8).astype(np.float32)
    large = 8 + (np.log(nf / np.float32(8)) / np.float32(np.log(1024 / 8)) * np.float32(8)).astype(np.int32)
    return (rel > 0) * 16 + np.where(n < 8, n, np.minimum(large, 15))


def causal_bucket(dist):
    n = np.maximum(dist, 0)
    nf = np.maximum(n, 1).astype(np.float32)
    large = 16 + (np.log(nf / np.float32(16)) / np.float32(np.log(128 / 16)) * np.float32(16)).astype(np.int32)
    return np.where(n < 16, n, np.minimum(large, 31))


def position_table():
    t = np.zeros((33, 5, 512), np.float32)
    rel = np.arange(512) - 255
    kinds = [(np.abs(rel) <= P, t5_bucket(rel))]
    for window, dilation in GROUPS:
        reach = window // (2 * dilation) * dilation
        kinds.append(((rel % dilation == 0) & (np.abs(rel) <= reach), t5_bucket(rel)))
    kinds.append((rel <= 0, causal_bucket(-rel)))
    for i, (valid, bucket) in enumerate(kinds):
        for j in range(512):
            if valid[j]:
                t[bucket[j], i, j] = 1.0
            else:
                t[32, i, j] = MASKED
    return t.reshape(33, -1)


def decay_table():
    log_g = np.log1p(-np.exp2(-5.0 - np.arange(RET_H)))
    d = np.arange(TOKENS)[None, None, :] - np.arange(P)[:, None, None]
    return (np.where(d >= 0, np.exp(log_g[None, :, None] * np.maximum(d, 0)), 0.0) * HD ** -0.5).astype(np.float32)


def rope_table():
    half = HD // 2
    inv = np.float32(10000.0) ** (-np.arange(half, dtype=np.float32) / np.float32(half))
    ang = (np.arange(TOKENS, dtype=np.float32)[:, None] * inv[None, :]).astype(np.float32)
    t = np.stack([np.cos(ang), np.sin(ang)], 1).astype(np.float32)
    return np.ascontiguousarray(t.reshape(NB, P, 2, half).transpose(1, 0, 2, 3))


def chunks(w):
    k, n = w.shape
    return [np.ascontiguousarray(w[i * 512:(i + 1) * 512].reshape(4, P, n).transpose(1, 0, 2)).reshape(P, 4 * n)
            for i in range(k // 512)]


def pad_half(h):
    return np.pad(h, ((0, 0), (0, HALF - h.shape[1])))


def by_partition(v):
    return v.reshape(-1, P).T


def pack(inputs):
    f = {k: np.asarray(v) for k, v in inputs.items()}
    w = f["w_in"][0]
    cols = {"qa": w[:, 0:512].reshape(D, H, HD)[:, PAIRS].reshape(D, 512), "kava": w[:, 512:768]}
    for g in range(3):
        for i, n in enumerate(("qb", "kb", "vb")):
            s = 768 + i * 1536 + g * 512
            cols[f"{n}{g}"] = w[:, s:s + 512]
    cols["ga"], cols["gb"] = w[:, 5376:5888], w[:, 5888:6400]
    for i in range(4):
        cols[f"mg{i}"] = w[:, 6400 + 512 * i:6912 + 512 * i]
    for c in range(2):
        cs = slice(512 * c, 512 * c + 512)
        cols[f"br0{c}"], cols[f"br1{c}"] = f["w_branch_a"][0][:, cs], f["w_branch_b"][0][:, cs]
        cols[f"wo{c}"] = f["w_out"][0][:, cs]
    halves = {p: chunks(c) for p, c in cols.items()}
    w_first = np.stack([pad_half(halves[p][int(n.split("/")[1])]) for n, p in FIRST_HALVES])

    w_layers, par = [], []
    for l in range(LAYERS):
        w = f["w_in_2"][l]
        at = dict(kc=512, vc=640, ks=768, vs=896, kw=1024, vw=1152)
        k = {n: w[:, s:s + P] for n, s in at.items()}
        cols = {"q": w[:, 0:512].reshape(D, H, HD)[:, PAIRS].reshape(D, 512),
                "k4": np.concatenate([k["kc"], k["vc"], k["ks"], k["kw"]], 1),
                "vsg": np.concatenate([k["vs"], k["vw"], w[:, 1280:1304]], 1),
                "qkr": w[:, 1304:1816], "vr": w[:, 1816:2328], "gr": w[:, 2328:2840],
                "ca": w[:, 2840:3352], "cb": w[:, 3352:3864]}
        for i in range(6):
            cols[f"mg{i}"] = w[:, 3864 + 512 * i:4376 + 512 * i]
        for c in range(2):
            cs = slice(512 * c, 512 * c + 512)
            for i in range(3):
                cols[f"br{i}{c}"] = f["w_branch_2"][l, i][:, cs]
            cols[f"wo{c}"] = f["w_out_2"][l][:, cs]
            cols[f"down{c}"] = f["w_ff2_2"][l][:, cs]
        for i in range(FF_PANELS):
            cols[f"ff{i}"] = f["w_ff1_2"][l][:, 512 * i:512 * i + 512]
        halves = {p: chunks(c) for p, c in cols.items()}
        for n, p in LAYER_HALVES:
            if p == "cmpH":
                w1 = f["cmp_w1_" + n[2] + "_2"][l]
                w_layers.append(w1.reshape(16, 2 * HD, P).transpose(1, 0, 2).reshape(P, HALF))
            else:
                w_layers.append(pad_half(halves[p][int(n.split("/")[1])]))
        pe = [f[f"cmp_pe_{n}_2"][l].reshape(16, 2 * HD).T for n in "kv"]
        par.append(np.concatenate(
            [by_partition(f["norm_mix_2"][l]), by_partition(f["norm_mlp_2"][l]), by_partition(f["ret_gn_2"][l]),
             by_partition(f["conv_ln_g_2"][l]), by_partition(f["conv_ln_b_2"][l]), by_partition(f["conv_b_2"][l]),
             f["conv_w_2"][l].T.reshape(4, P, TAPS).transpose(1, 0, 2).reshape(P, 4 * TAPS), *pe,
             f["cmp_w2_k_2"][l], f["cmp_w2_k_2"][l], f["cmp_w2_v_2"][l]], 1))
    w_layers += [np.zeros((P, HALF), np.float32)] * SLOTS
    par.append(np.zeros((P, PAR), np.float32))
    gains = np.stack([np.concatenate([f[n][0], f[n][0]]) for n in ("q_norm_a", "k_norm_a", "q_norm_b", "k_norm_b")], 1)
    return dict(
        x=f["x"][0], w_first=w_first, w_layers=np.stack(w_layers), par=np.stack(par),
        first=np.concatenate([by_partition(f["norm_gain"][0]), gains, np.tile(f["sink_a"][0:1], (P, 1))], 1),
        rel_bias=f["rel_bias"], rel_table=f["rel_table_2"], b_merge=f["b_merge"][0].reshape(-1),
        norm_final=f["norm_final_2"], ident=np.eye(P, dtype=np.float32), onehot=position_table(),
        decay=decay_table(), rope=rope_table())


def kernel(**inputs):
    import concourse.bacc as bacc
    from concourse.bass_utils import run_bass_kernel_spmd

    nc = bacc.Bacc("TRN2", target_bir_lowering=False, num_devices=1)
    arrays, args = {}, {}
    for name, v in pack(inputs).items():
        v = np.ascontiguousarray(v)
        arrays[f"in_{name}_dram"] = v
        args[name] = nc.dram_tensor(f"in_{name}_dram", v.shape, mybir.dt.from_np(v.dtype), kind="ExternalInput").ap()
    out = nc.dram_tensor("out_0_dram", (TOKENS, D), F32, kind="ExternalOutput").ap()
    block_kernel(nc, args, out)
    r = run_bass_kernel_spmd(nc, [arrays], core_ids=[0])
    return r.results[0]["out_0_dram"].reshape(1, TOKENS, D)
```

```python
from contextlib import ExitStack

import numpy as np

import concourse.bass as bass
from concourse import mybir

F32 = mybir.dt.float32
F32R = mybir.dt.float32r
ALU = mybir.AluOpType
ACT = mybir.ActivationFunctionType
AX = mybir.AxisListType

P = 128
TOKENS, D = 256, 1024
NB = TOKENS // P
KC = D // P
HD = 64
H = 8
HALF = 4 * 512
SLOTS = 6
HI_SLOTS = 3
EPS = 1e-6
MASKED = -1e30
LAYERS = 2
GROUPS = ((128, 1), (512, 4), (2048, 16))
N_CMP, CMP_STRIDE, CMP_LEN = 15, 16, 32
TAPS = 31
RET_H = 4
FF_PANELS = 8
TOEP = 3 * P
GELU_C, GELU_A = 0.7978845608028654, 0.044715

PAR_SIZES = dict(mlp=KC, gn=4, ln_g=4, ln_b=4, conv_b=4, conv_w=4 * TAPS, pe=32, w2k=P, w2v=HD)
PAR_AT, PAR = {}, 0
for _name, _size in PAR_SIZES.items():
    PAR_AT[_name] = (PAR, PAR + _size)
    PAR += _size
FIRST_AT = dict(norm=(0, 8), gains=(8, 12), sink=(12, 20))
FIRST = 20

FIRST_PANELS = ["qa", "kava", "qb0", "qb1", "qb2", "kb0", "kb1", "kb2", "vb0", "vb1", "vb2", "ga", "gb",
                "mg0", "mg1", "mg2", "mg3", "br00", "br01", "br10", "br11", "wo0", "wo1"]
NORMED = ["qa", "kava", "qb0", "qb1", "qb2", "kb0", "kb1", "kb2"]
LAYER_PANELS = (["cb", "ca", "q", "k4", "vsg", "qkr", "vr", "gr", "mg0", "Oc", "mg1", "Or", "mg2", "mg3",
                 "mg4", "mg5"] + [f"br{i}{c}" for i in range(3) for c in range(2)]
                + ["wo0", "wo1"] + [f"ff{i}" for i in range(FF_PANELS)] + ["down0", "down1"])
FIRST_WIDE = ["ga", "gb", "mg0", "mg1", "mg2", "mg3"]
LAYER_WIDE = ["qkr", "vr", "gr", "mg0", "mg1", "mg2", "mg3", "mg4", "mg5"]


def halves_of(panels, skip):
    out = []
    for p in panels:
        if p in skip:
            continue
        n = 1 if p.startswith("br") else 8 if p.startswith("down") else 2
        out += [(f"{p}/{i}", p) for i in range(n)]
        if p == "qkr":
            out += [("w1k", "cmpHk")]
        if p == "vr":
            out[-1:-1] = [("w1v", "cmpHv")]
    return out


FIRST_HALVES = halves_of(FIRST_PANELS, ())
LAYER_HALVES = halves_of(LAYER_PANELS, ("Oc", "Or"))
N_HALVES = len(LAYER_HALVES)
BY_COLUMNS = ("cb", "ca", "q", "k4", *[f"ff{i}" for i in range(FF_PANELS)])



def transposed(name):
    return [f"{name}{b}" for b in range(NB)]


def by_columns(name):
    return [f"{name}{b}{i}" for i in range(2) for b in range(NB)]


def units_first():
    return [("A", h, 1) for h in range(H)] + [("B", h, 3) for h in range(H)]


def units_layer():
    return [("s", h, 1) for h in range(H)] + [("w", h, 1) for h in range(H)]


GROUP = 4
TILES = 3


def unit_steps(n):
    out = [("S", 0)]
    for u in range(n):
        if u + 1 < n:
            out.append(("S", u + 1))
        out += [("T", u), ("V", u)]
    return out


def make_plan(panels, steps, slots, extra):
    steps = list(steps)
    plan = {}
    for p in panels:
        for s in range(KC):
            at = []
            if s in slots and steps:
                at.append(steps.pop(0))
            plan[p, s] = at + [(e, 0) for e in extra.get((p, s), [])]
    assert not steps
    return plan


FIRST_PLAN = make_plan(FIRST_WIDE, unit_steps(2 * H), range(KC), {("mg2", 3): ["yA"]})
LAYER_PLAN = make_plan(LAYER_WIDE, unit_steps(2 * H), (0, 1, 3, 4, 5, 7), {
    ("qkr", 7): ["cmpHk"], ("vr", 1): ["ro0"], ("vr", 2): ["ro1"], ("vr", 3): ["cmpHv"], ("vr", 6): ["rot"],
    ("gr", 0): ["cmp2"], ("gr", 3): ["cmpS"], ("mg0", 2): ["PcT"],
    ("mg0", 6): ["R0"], ("mg1", 0): ["R1"], ("mg1", 2): ["R2"], ("mg1", 5): ["R3"], ("mg4", 2): ["oR"], ("mg5", 1): ["cv"],
    ("mg5", 4): ["y"], ("mg5", 7): ["cz"]})


def plan_tiles(plan, units):
    out = []
    for steps in plan.values():
        for e, u in steps:
            if e in "ST":
                out += [f"{e}{units[u][0]}{units[u][1]}{g}" for g in range(units[u][2])]
            elif e == "cmpS":
                out += ["cmpS0", "cmpS1"]
            elif e in ("rot", "oR", "cv", "cz", "y", "yA"):
                out += transposed(e)
            elif e not in ("V", "ro0", "ro1"):
                out.append(e)
    return out


FIRST_TILES = (["bias0", "bias1", "bias2", "bias3", "bias4"] + [f"x{b}{i}" for b in range(NB) for i in range(2)]
               + [t for p in NORMED for t in transposed(p)] + plan_tiles(FIRST_PLAN, units_first())
               + transposed("yB") + by_columns("m"))
LAYER_TILES = ([f"x{b}{i}" for b in range(NB) for i in range(2)] + plan_tiles(LAYER_PLAN, units_layer())
               + by_columns("m") + by_columns("z"))


def last_half(name, p, halves):
    i = [h for h, _ in halves].index(name)
    return p.startswith("cmpH") or all(q != p for _, q in halves[i + 1:])


def used_before(name, halves):
    i = [h for h, _ in halves].index(name)
    return sum(not last_half(h, p, halves) for h, p in halves[:i])


PADS = 4
X_UPDATES = 2 * (1 + 2 * LAYERS)


class Turns:

    def __init__(self, names, buffers, before=None):
        self.before = before or [0] * buffers
        self.at, count = {}, list(self.before)
        start = sum(self.before)
        for i, n in enumerate(names):
            b = (start + i) % buffers
            self.at[n] = (b, count[b])
            count[b] += 1
        self.after = count
        self.each = [c - b for c, b in zip(count, self.before)]


class Part:

    def __init__(self, tiles, panels, halves, high, names, l):
        self.turns = dict(tile=tiles, panel=panels, half=halves, high=high)
        self.halves = names
        self.l = l

    def turn(self, kind, name):
        t = self.turns[kind]
        b, before = t.at[name]
        return b, before if self.l is None else self.l * t.each[b] + before


TILES_1 = Turns(FIRST_TILES, TILES)
PANELS_1 = Turns(FIRST_PANELS, 2)
HALVES_1 = Turns([h for h, _ in FIRST_HALVES], SLOTS)
TILES_2 = Turns(LAYER_TILES, TILES, TILES_1.after)
PANELS_2 = Turns(LAYER_PANELS, 2, PANELS_1.after)
HALVES_2 = Turns([h for h, _ in LAYER_HALVES], SLOTS, HALVES_1.after)
HIGH_1 = Turns([h for h, _ in FIRST_HALVES], HI_SLOTS)
HIGH_2 = Turns([h for h, _ in LAYER_HALVES], HI_SLOTS, HIGH_1.after)
assert N_HALVES % HI_SLOTS == 0
assert sum(PANELS_2.each) % 2 == 0 and sum(HALVES_2.each) % SLOTS == 0


def area_map(sizes):
    at, end = {}, 0
    for name, size in sizes:
        at[name] = (end, end + size)
        end += size
    return at, end


AREA_1, END_1 = area_map([
    ("kbT", 3072), ("qbT", 3072), ("qaT", 1024), ("kaT", 256), ("va", 256), ("vb", 3072), ("sgb", 1024),
    ("mgt", 4096), ("L", 2 * 1536), ("PT", 2 * 1536), ("E", 2 * 3 * TOEP)])
AREA_2, END_2 = area_map([
    ("En", H * TOEP), ("hx", 64), ("hgv", 256), ("vblk", 512), ("Pc", 512), ("u", 4 * 288),
    ("qT", 1024), ("kT", 512), ("vsw", 512), ("gt", 48), ("hy", 64), ("ht", 64), ("hgk", 32), ("kcmpT", 32),
    ("Lc", 240), ("PcT", 512), ("tz", 1024), ("mgt", 6144), ("brT", 3072), ("brT_lo", 1024), ("L", 768),
    ("PT", 768), ("y", 1024), ("tmp", 512), ("yc", 1024)])


def within(name, skip, size):
    at = AREA_2[name][0] + skip
    return at, at + size


AREA_2["kcP"] = within("mgt", 0, 1024)
AREA_2["blk"] = within("mgt", 1024, 960)
AREA_2["blk_hi"] = within("mgt", 2048, 960)
AREA_2["PR"] = within("mgt", 2048, RET_H * 3 * P)
AREA_2["vr"] = within("mgt", 4096, 1024)
AREA_2["sgr"] = within("mgt", 5120, 1024)
AREA_2["or"] = within("brT", 0, 1024)
AREA_2["rT"] = within("brT", 1024, 1024)
AREA_2["acc"] = within("brT", 2048, 1024)
AREA_2["z"] = AREA_2["y"]
LOW_OF_BRANCH = (AREA_2["yc"], AREA_2["brT_lo"], within("L", 0, 1024))
AREA_2["ffT"] = within("qT", 0, 2 * 8192)
AREA_2["sq"] = within("qT", 2 * 8192, 2048)
AREA_2["gain"] = within("qT", 2 * 8192 + 1024, 1024)
END_2 = max(END_2, AREA_2["sq"][1])
AREA = max(END_1, END_2)


def block_kernel(nc, a, out):
    ctx = ExitStack()
    with ctx:
        def sb(name, *shape):
            return ctx.enter_context(nc.sbuf_tensor(name, [P, *shape], F32))

        def sem(name):
            return ctx.enter_context(nc.semaphore(name))

        def both_types(name, *shape):
            offset = -(-nc.sbuf_base // 32) * 32
            whole = sb(name, *shape)
            return whole, nc.alloc_sbuf_tensor_at(f"{name}_parts", [P, *shape], F32R, offset=offset)

        ring, ring_lo = both_types("ring", SLOTS, HALF)
        ring_hi = ctx.enter_context(nc.sbuf_tensor("ring_high", [P, HI_SLOTS, HALF], F32R))
        hT_hi = ctx.enter_context(nc.sbuf_tensor("hT_high", [P, KC, TOKENS], F32R))
        hT_lo = ctx.enter_context(nc.sbuf_tensor("hT_low", [P, KC, TOKENS], F32R))
        x = sb("x", NB, D)
        tok = sb("tok", NB, D)
        ident = sb("ident", P)
        rope = sb("rope", NB, 2, HD // 2)
        par = sb("par", PAR)
        first = sb("first", FIRST)
        cw = sb("cw", 4, TAPS)
        lnh = sb("lnh", 3, 4)
        stat = sb("stat", 256)
        area, area_r = both_types("area", AREA)
        decay, decay_r = both_types("decay", RET_H, TOKENS)
        tile = [ctx.enter_context(nc.psum_tensor(f"tile{i}", [P, 512], F32)) for i in range(TILES)]
        panel = [ctx.enter_context(nc.psum_tensor(f"panel{i}", [P, 2, 512], F32)) for i in range(2)]
        heads_out = ctx.enter_context(nc.psum_tensor("heads_out", [P, NB, GROUP * HD], F32))
        bias_rows = nc.dram_tensor("bias_rows", (5, H, 512), F32, kind="Internal").ap()
        bias_copies = nc.dram_tensor("bias_copies", (5, H, P, 512), F32, kind="Internal").ap()

        def toeplitz(head, step, n):
            return bass.AP(tensor=bias_copies.tensor, offset=head * P * 512 + 127,
                           ap=[[511, P], [step * P * 512, n], [1, TOEP]])


        def one(name):
            if name == "sga":
                return decay[:, :, :].rearrange("p h t -> p (h t)")
            s, e = AREA_1[name]
            return area[:, s:e]

        def two(name):
            s, e = AREA_2[name]
            return area[:, s:e]

        def parts(name, at, n):
            s = name[0] + at
            return area_r[:, s:s + n]

        def pars(name):
            s, e = PAR_AT[name]
            return par[:, s:e]

        def st(s, *shape):
            n = int(np.prod(shape))
            v = stat[:, s:s + n]
            if len(shape) == 2:
                v = v.rearrange("p (a b) -> p a b", a=shape[0])
            return v

        ss, rstd = st(0, 2), st(2, 2)
        hs, hr = st(4, 2, 8), st(20, 2, 8)
        mxs = [st(36, 2, 3), st(224, 2, 3)]
        negmax = stat[:, 42:74].rearrange("p (b u) -> p b u", b=2)
        den = stat[:, 74:106].rearrange("p (b u) -> p b u", b=2)
        sinks = stat[:, 106:122].rearrange("p (b u) -> p b u", b=2)
        cmx, cden, coef_c = st(122, 2, 8), st(138, 2, 8), st(154, 2, 8)
        half_power = stat[:, 170:178]
        bns, bna = sb("bns", 8, 6), sb("bna", 8, 2)
        brs = st(178, 2, 4)
        cns, cna, crs = sb("cns", 2, 6), sb("cna", 2, 2), st(186, 2)
        coef = stat[:, 190:222].rearrange("p (b u) -> p b u", b=2)
        zero = stat[:, 222:223]
        low = stat[:, 223:224]
        rstd_sq = st(232, 2)

        loaded = sem("constants_loaded")
        x_loaded = sem("x_loaded")
        par_loaded = sem("layer_parameters_loaded")
        bmerge_loaded = sem("merge_bias_loaded")
        gain_loaded = sem("norm_gain_loaded")
        x_high = sem("operand_high_part_ready")
        En_loaded = sem("layer_bias_loaded")
        E_loaded = [sem(f"head_bias{i}_loaded") for i in range(2)]
        E_used = sem("head_bias_used")
        half_loaded = [sem(f"half{i}_loaded") for i in range(SLOTS)]
        half_used = sem("half_used")
        high_ready = sem("high_part_ready")
        low_ready = sem("low_part_ready")
        merged_high = sem("merged_high_part_ready")
        decay_loaded = sem("decay_loaded")
        tile_done = [sem(f"tile{i}_done") for i in range(TILES)]
        tile_evicted = [sem(f"tile{i}_evicted") for i in range(TILES)]
        panel_done = [sem(f"panel{i}_done") for i in range(2)]
        panel_evicted = [sem(f"panel{i}_evicted") for i in range(2)]
        pad_ready = sem("constant_fill_ready")
        rows_stored = sem("bias_rows_stored")
        copies_stored = sem("bias_copies_stored")
        squares = sem("row_squares_ready")
        rstd_ready = sem("row_rstd_ready")
        h_ready = sem("h_ready")
        head_sq = sem("head_squares_ready")
        head_sum = sem("head_sums_ready")
        head_rstd = sem("head_rstd_ready")
        head_normed = sem("heads_normed")
        gate_tanh = sem("gate_tanh_ready")
        merge_sum = sem("merge_bias_added")
        merge_tanh = sem("merge_tanh_ready")
        logits = sem("logits_ready")
        probs = sem("probs_ready")
        pv_done = sem("pv_done")
        group_done = sem("head_group_done")
        group_evicted = sem("head_group_evicted")
        y_ready = sem("y_ready")
        merged = sem("merged_ready")
        x_updated = sem("x_updated")
        cw_ready = sem("half_weights_ready")
        conv_ready = sem("conv_sum_ready")
        conv_stats = sem("conv_stats_ready")
        conv_rstd = sem("conv_rstd_ready")
        conv_normed = sem("conv_normed")
        conv_z = sem("conv_z_tanh_ready")
        blocks_ready = sem("blocks_ready")
        hid_in = sem("gelu_argument_ready")
        hid_tanh = sem("gelu_tanh_ready")
        hid_ready = sem("hidden_ready")
        cmp_logits = sem("compressed_logits_ready")
        cmp_exp = sem("compressed_exp_ready")
        rot_ready = sem("rotated_ready")
        gr_tanh = sem("retention_gate_tanh_ready")
        ret_stats = sem("retention_stats_ready")
        ret_rstd = sem("retention_rstd_ready")
        ret_ready = sem("retention_output_ready")
        branch_ready = sem("conv_branch_ready")
        squares_high = sem("high_part_of_squares_ready")
        squares_full = sem("squares_of_relu_whole")
        y_high = sem("high_part_of_outputs_ready")
        squared = sem("squares_of_relu_ready")
        result_ready = sem("result_ready")
        stored = sem("output_stored")
        taken = sem("operands_taken")

        block = ctx.enter_context(nc.Block())
        part_1 = Part(TILES_1, PANELS_1, HALVES_1, HIGH_1, FIRST_HALVES, None)

        def layer(l):
            return Part(TILES_2, PANELS_2, HALVES_2, HIGH_2, LAYER_HALVES, l)

        def count(part, first_block, each, n):
            return n if part.l is None else part.l * each + (first_block + n)

        PER = dict(half_used=(len([1 for h, p in FIRST_HALVES if not last_half(h, p, FIRST_HALVES)]),
                              len([1 for h, p in LAYER_HALVES if not last_half(h, p, LAYER_HALVES)])))

        def wait_done(eng, sems, part, kind, name):
            b, before = part.turn(kind, name)
            eng.wait_ge(sems[b], before + 1)
            return b

        def wait_used(eng, part, name):
            p = dict(part.halves)[name]
            if p.startswith("cmpH"):
                wait_done(eng, tile_done, part, "tile", p)
            elif last_half(name, p, part.halves):
                wait_done(eng, panel_done, part, "panel", p)
            else:
                n = used_before(name, part.halves)
                eng.wait_ge(half_used, count(part, PER["half_used"][0], PER["half_used"][1], n + 1))

        def width_of(name):
            return 4 * 280 if name.startswith("vsg") else 4 * 256 if name.startswith("kava") else HALF

        def places(part, n):
            if n < len(part.halves):
                name = part.halves[n][0]
                slot, before = part.turn("half", name)
                return name, slot, before, part.turns["high"].at[name][0]
            name = LAYER_HALVES[n - len(part.halves)][0]
            slot, before = HALVES_2.at[name]
            if part.l is not None:
                before = part.l * HALVES_2.each[slot] + (HALVES_2.each[slot] + before)
            return name, slot, before, HIGH_2.at[name][0]

        def round_half(act, part, n):
            name, slot, before, hi = places(part, n)
            if n >= HI_SLOTS:
                wait_used(act, part, part.halves[n - HI_SLOTS][0])
            act.wait_ge(half_loaded[slot], before * 16 + 16)
            w = width_of(name)
            act.activation(ring_hi[:, hi, 0:w], ring[:, slot, 0:w], ACT.Copy).then_inc(high_ready, 1)

        def index_of(part, half):
            return [h for h, _ in part.halves].index(half)

        def round_after(act, part, *used):
            for half in used:
                round_half(act, part, index_of(part, half) + HI_SLOTS)

        def low_half(g, part, n):
            name, slot, _, hi = places(part, n)
            w = width_of(name)
            g.wait_ge(high_ready, count(part, len(FIRST_HALVES), N_HALVES, n + 1))
            g.sem_inc(taken, 1)
            g.tensor_tensor(ring_lo[:, slot, 0:w], ring[:, slot, 0:w], ring_hi[:, hi, 0:w], ALU.subtract).then_inc(low_ready, 1)

        def first_branch_parts(t):
            if t == 0:
                return (parts(AREA_1["qaT"], 0, 1024).rearrange("p (c t) -> p c t", c=4),
                        decay_r[:, :, :])
            return [parts(AREA_1["qbT"], 1024 * i, 1024).rearrange("p (c t) -> p c t", c=4) for i in range(2)]

        def branch_parts(i):
            return [parts(at, skip, 1024).rearrange("p (c t) -> p c t", c=4)
                    for at, skip in ((AREA_2["brT"], 1024 * i), (LOW_OF_BRANCH[i], 0))]

        def hidden_parts():
            return [parts(AREA_2["ffT"], 8192 * i, 8192).rearrange("p (k t) -> p k t", k=32) for i in range(2)]

        def tile_of(eng, part, name):
            return tile[wait_done(eng, tile_done, part, "tile", name)]

        def panel_of(eng, part, name):
            return panel[wait_done(eng, panel_done, part, "panel", name)]

        def tile_sem(part, name):
            return tile_evicted[part.turn("tile", name)[0]]

        def panel_sem(part, name):
            return panel_evicted[part.turn("panel", name)[0]]

        def wait_products(eng, part, u):
            if u % GROUP == GROUP - 1:
                eng.wait_ge(group_done, count(part, 4, 4, u // GROUP + 1))
            else:
                eng.wait_ge(pv_done, count(part, 12, 12, u - u // GROUP + 1))

        def normed_out(v, part, i):
            us = slice(GROUP * i, GROUP * (i + 1))
            c = coef[:, :, us]
            v.wait_ge(probs, GROUP * (i + 1))
            if i < 2:
                v.tensor_tensor(den[:, :, us], den[:, :, us], sinks[:, :, us], ALU.add)
                v.drain()
            v.reciprocal(c, den[:, :, us])
            v.drain()
            v.tensor_scalar(c, c, 0.5, None, ALU.mult)
            v.drain()
            hs_ = slice(GROUP * HD * (i % 2), GROUP * HD * (i % 2 + 1))
            gate = one(("sga", "sgb")[i // 2]).rearrange("p (b n) -> p b n", b=2)[:, :, hs_]
            for b in range(NB):
                v.tensor_tensor(gate[:, b, :].rearrange("p (h d) -> p h d", h=GROUP),
                                gate[:, b, :].rearrange("p (h d) -> p h d", h=GROUP),
                                c[:, b, :].unsqueeze(2).broadcast_to([P, GROUP, HD]), ALU.mult)
            v.drain()
            v.wait_ge(group_done, i + 1)
            for b in range(NB):
                v.tensor_tensor(gate[:, b, :], heads_out[:, b, :], gate[:, b, :], ALU.mult)
            v.drain().then_inc(group_evicted, 1)
            v.sem_inc(y_ready, 1)

        def sum_out(v, part, l, i):
            w = i // 2
            us = slice(GROUP * i, GROUP * (i + 1))
            c = coef[:, :, us]
            gt = two("gt").rearrange("p (b h i) -> p b h i", b=2, h=H)[:, :, GROUP * (i % 2):GROUP * (i % 2 + 1)]
            hs_ = slice(GROUP * HD * (i % 2), GROUP * HD * (i % 2 + 1))
            y = two("y").rearrange("p (b n) -> p b n", b=2)[:, :, hs_]
            tmp = two("tmp").rearrange("p (b n) -> p b n", b=2)
            v.wait_ge(probs, l * 16 + (16 + GROUP * (i + 1)))
            v.reciprocal(c, den[:, :, us])
            v.drain()
            v.scalar_tensor_tensor(c, gt[:, :, :, 1 + w], 1.0, c, ALU.add, ALU.mult)
            v.drain()
            v.wait_ge(group_done, l * 4 + (4 + i + 1))
            to = y if i < 2 else tmp
            for b in range(NB):
                v.tensor_tensor(to[:, b, :].rearrange("p (h d) -> p h d", h=GROUP),
                                heads_out[:, b, :].rearrange("p (h d) -> p h d", h=GROUP),
                                c[:, b, :].unsqueeze(2).broadcast_to([P, GROUP, HD]), ALU.mult)
            v.drain().then_inc(group_evicted, 1)
            if i >= 2:
                for b in range(NB):
                    e = v.tensor_tensor(y[:, b, :], y[:, b, :], tmp[:, b, :], ALU.add)
                v.drain()
                e = v.tensor_tensor(y, y, two("yc").rearrange("p (b n) -> p b n", b=2)[:, :, hs_], ALU.add)
                e.then_inc(y_ready, 1)

        @block.sync
        def _(sp):
            sp.dma_start(x[:, :, :], a["x"].rearrange("(b p) d -> p b d", p=P)).then_inc(x_loaded, 16)
            for name, to in (("ident", ident[:, :]), ("first", first[:, :]),
                             ("rope", rope[:, :, :, :])):
                sp.dma_start(to, a[name]).then_inc(loaded, 16)
            onehot = one("mgt")[0:33, 0:2560]
            sp.dma_start(onehot[0:33, :], a["onehot"]).then_inc(loaded, 16)
            tabs = one("mgt")[0:32, 2560:2600]
            sp.dma_start(tabs[:, 0:32], a["rel_bias"]).then_inc(loaded, 16)
            sp.dma_start(tabs[:, 32:40], a["rel_table"]).then_inc(loaded, 16)
            sp.dma_start(par[:, :], a["par"][0]).then_inc(par_loaded, 16)

            def load_half(part, name, source):
                i = [h for h, _ in part.halves].index(name)
                slot = part.turn("half", name)[0]
                if i >= SLOTS:
                    wait_used(sp, part, part.halves[i - SLOTS][0])
                w = width_of(name)
                sp.dma_start(ring[:, slot, 0:w], source[:, 0:w]).then_inc(half_loaded[slot], 16)

            def load_first(i):
                name = FIRST_HALVES[i][0]
                load_half(part_1, name, a["w_first"][i])
                if name == "mg0/0":
                    sp.dma_start(one("mgt").rearrange("p (c b n) -> p c b n", c=4, b=2)[:, :, 0, :],
                                 a["b_merge"].rearrange("(c n) -> c n", c=4).partition_broadcast(P)).then_inc(bmerge_loaded, 16)

            def copy_rows(n):
                t, h = n // 2, n % 2 * (H // 2)
                src = bass.AP(tensor=bias_rows.tensor, offset=(t * H + h) * 512, ap=[[512, H // 2], [0, P], [1, 512]])
                sp.dma_start(bias_copies[t, h:h + H // 2], src).then_inc(copies_stored, 16)

            for i in range(8):
                load_first(i)
            sp.wait_ge(rows_stored, 16 * 5)
            for n in range(10):
                copy_rows(n)
                load_first(8 + n)
            for i in range(18, 20):
                load_first(i)
            sp.wait_ge(copies_stored, 16 * 10)
            Es = one("E").rearrange("p (s t j) -> p s t j", s=2, t=3)

            def load_bias(n):
                if n >= 2:
                    sp.wait_ge(E_used, n - 1)
                if n < 4:
                    sp.dma_start(Es[:, n % 2, 0:2, :], toeplitz(2 * n, 1, 2)).then_inc(E_loaded[n % 2], 16)
                else:
                    sp.dma_start(Es[:, n % 2, :, :], toeplitz(H + n - 4, H, 3)).then_inc(E_loaded[n % 2], 16)

            names = [h for h, _ in FIRST_HALVES]
            first_wide = names.index("ga/0")
            bias_at = {}
            for n in range(2):
                load_bias(n)
            for n in range(2, 4 + H):
                unit = 2 * n if n < 4 else n + 4
                before_step = max(0, 3 * unit - 9)
                bias_at.setdefault(first_wide + SLOTS - 1 + before_step // 4, []).append(n)
            for i in range(20, len(FIRST_HALVES)):
                load_first(i)
                for n in bias_at.pop(i, []):
                    load_bias(n)
            for ns in bias_at.values():
                for n in ns:
                    load_bias(n)
            sp.wait_ge(group_done, 4)
            sp.dma_start(two("En").rearrange("p (h j) -> p h j", h=H), toeplitz(4 * H, 1, H)).then_inc(En_loaded, 16)

            sp.dma_start(two("gain"), a["gains"][0].partition_broadcast(P)).then_inc(gain_loaded, 16)
            wait_done(sp, panel_done, part_1, "panel", "br01")
            sp.dma_start(decay[:, :, :], a["decay"]).then_inc(decay_loaded, 16)

            for i in range(SLOTS):
                name = LAYER_HALVES[i][0]
                slot = HALVES_2.at[name][0]
                wait_used(sp, part_1, FIRST_HALVES[len(FIRST_HALVES) - SLOTS + i][0])
                sp.dma_start(ring[:, slot, :], a["w_layers"][i]).then_inc(half_loaded[slot], 16)

            with sp.Fori(0, LAYERS) as l:
                part = layer(l)
                for i, (name, p) in enumerate(LAYER_HALVES):
                    if i >= SLOTS:
                        load_half(part, name, a["w_layers"][l * N_HALVES + i])
                sp.wait_ge(squared, l * 8 + 8)
                sp.dma_start(two("gain"), a["gains"][l + 1].partition_broadcast(P)).then_inc(gain_loaded, 16)
                b, before = part.turn("panel", "ff7")
                sp.wait_ge(panel_done[b], before + 1)
                sp.dma_start(par[:, :], a["par"][l + 1]).then_inc(par_loaded, 16)
                for i in range(SLOTS):
                    name = LAYER_HALVES[i][0]
                    slot = HALVES_2.at[name][0]
                    wait_used(sp, part, LAYER_HALVES[len(LAYER_HALVES) - SLOTS + i][0])
                    sp.dma_start(ring[:, slot, :], a["w_layers"][l * N_HALVES + (N_HALVES + i)]).then_inc(half_loaded[slot], 16)

            for b in range(NB):
                sp.wait_ge(result_ready, b + 1)
                sp.dma_start(out.rearrange("(b p) d -> b p d", p=P)[b], tok[:, b, :]).then_inc(stored, 16)
            sp.wait_ge(stored, 32)
            sp.wait_ge(par_loaded, 16 * (LAYERS + 1))
            for s in range(SLOTS):
                sp.wait_ge(half_loaded[s], 16 * (HALVES_2.after[s] + (LAYERS - 1) * HALVES_2.each[s] + 1))

        @block.tensor
        def _(pe):
            def tile_for(part, name):
                b, before = part.turn("tile", name)
                if part.l is not None or before:
                    pe.wait_ge(tile_evicted[b], before)
                return tile[b], tile_done[b]

            def panel_for(part, name):
                b, before = part.turn("panel", name)
                if part.l is not None or before:
                    pe.wait_ge(panel_evicted[b], before * 2)
                return panel[b], panel_done[b]

            def wait_evicted(part, name):
                b, before = part.turn("tile", name)
                pe.wait_ge(tile_evicted[b], before + 1)

            def tile_after(part, name, names):
                for n in names:
                    if part.turn("tile", n)[0] != part.turn("tile", name)[0]:
                        wait_evicted(part, n)
                return tile_for(part, name)

            def wait_parts(part, name):
                pe.wait_ge(low_ready, count(part, len(FIRST_HALVES), N_HALVES, index_of(part, name) + 1))
                return ring_hi[:, part.turn("high", name)[0], :], ring_lo[:, part.turn("half", name)[0], :]

            def rows_out(part, name, of, halves, width=512, plan=None, step=None, ready=None, after={}):
                ps, done = panel_for(part, name)
                for i, half in enumerate(halves):
                    if ready:
                        ready(i)
                    hi, lo = (w[:, 0:4 * width].rearrange("p (k n) -> p k n", k=4) for w in wait_parts(part, half))
                    for k in range(4):
                        first, last = i == 0 and k == 0, i == len(halves) - 1 and k == 3
                        for b in range(NB):
                            high, low = (t[:, 4 * i + k, b * P:(b + 1) * P] for t in of)
                            pe.matmul(ps[:, b, 0:width], high, hi[:, k, :], start=first, stop=False)
                            pe.matmul(ps[:, b, 0:width], high, lo[:, k, :], start=False, stop=False)
                            mm = pe.matmul(ps[:, b, 0:width], low, hi[:, k, :], start=False, stop=last)
                        if last:
                            mm.then_inc(done, 1)
                        elif k == 3:
                            mm.then_inc(half_used, 1)
                        if plan:
                            for e, u in plan[name, 4 * i + k]:
                                step(e, u)
                        if 4 * i + k in after:
                            after[4 * i + k]()

            def columns_out(part, name):
                ps, done = panel_for(part, name)
                for i in range(2):
                    hi, lo = (w.rearrange("p (k n) -> p k n", k=KC) for w in wait_parts(part, f"{name}/{i}"))
                    for m in range(2):
                        cols, to = slice(m * P, (m + 1) * P), ps[:, i, m * TOKENS:(m + 1) * TOKENS]
                        for k in range(KC):
                            pe.matmul(to, hi[:, k, cols], hT_hi[:, k, :], start=(k == 0), stop=False)
                            pe.matmul(to, hi[:, k, cols], hT_lo[:, k, :], start=False, stop=False)
                            mm = pe.matmul(to, lo[:, k, cols], hT_hi[:, k, :], start=False, stop=(k == KC - 1))
                    mm.then_inc(half_used if i == 0 else done, 1)

            def turn(part, name, source, n=4, rows=P):
                ps, done = tile_for(part, name)
                for i in range(n):
                    mm = pe.transpose(ps[0:rows, i * P:(i + 1) * P], source(i), ident[:, :])
                mm.then_inc(done, 1)

            def turn_rows(part, name, ready, base):
                for b in range(NB):
                    pe.wait_ge(ready, base + b + 1 if part.l is None else base + (b + 1))
                    for i in range(2):
                        turn(part, f"{name}{b}{i}", lambda c: tok[:, b, (4 * i + c) * P:(4 * i + c + 1) * P])

            def turn_columns(part, name, rows, i, ready, base):
                pe.wait_ge(ready, base + (i + 1))
                for b in range(NB):
                    turn(part, f"{name}{b}{i}", lambda c: rows[:, b, (4 * i + c) * P:(4 * i + c + 1) * P])

            def columns_ready(part, name, i):
                for b in range(NB):
                    wait_evicted(part, f"{name}{b}{i}")

            def project_merged(part, branch, of, last_chunk, base):
                rows_out(part, branch, of, [f"{branch}/0"], after={2: lambda: turn_columns(part, "m", tok, 0, merged, base)})
                rows_out(part, "wo0", of_h, two_halves("wo0"), ready=lambda i: columns_ready(part, "m", i),
                         after={1: lambda: turn_columns(part, "m", tok, 1, merged, base)})
                rows_out(part, "wo1", of_h, two_halves("wo1"), after=last_chunk)

            def operand_ready(part, name):
                for b in range(NB):
                    for i in range(2):
                        wait_evicted(part, f"{name}{b}{i}")

            of_h = (hT_hi, hT_lo)
            two_halves = lambda n: [f"{n}/0", f"{n}/1"]

            part = part_1
            onehot = one("mgt")[0:33, 0:2560].rearrange("p (t j) -> p t j", t=5)
            tabs = one("mgt")[0:33, 2560:2600]
            pe.wait_ge(loaded, 16 * 6)
            pe.wait_ge(pad_ready, PADS)
            for t in range(5):
                ps, done = tile_for(part, f"bias{t}")
                pe.matmul(ps[0:H, :], tabs[:, t * H:(t + 1) * H], onehot[:, t, :], start=True, stop=True).then_inc(done, 1)
            turn_rows(part, "x", h_ready, 0)
            operand_ready(part, "x")
            staged = tok[:, :, :].rearrange("p b (s n) -> p b s n", s=2)

            def turn_heads(n):
                p = NORMED[n]
                for b in range(NB):
                    pe.wait_ge(head_normed, NB * n + b + 1)
                    turn(part, f"{p}{b}", lambda c: staged[:, b, n % 2, c * P:(c + 1) * P], n=1 if p == "kava" else 4)

            for n, p in enumerate(FIRST_PANELS[:11]):
                rows_out(part, p, of_h, two_halves(p), 256 if p == "kava" else 512)
                if 1 <= n <= len(NORMED):
                    turn_heads(n - 1)

            qaT, kaT = one("qaT").rearrange("p (c t) -> p c t", c=4), one("kaT")
            qbT = one("qbT").rearrange("p (g c t) -> p g c t", g=3, c=4)
            kbT = one("kbT").rearrange("p (g c t) -> p g c t", g=3, c=4)
            va = one("va").rearrange("p (b n) -> p b n", b=2)
            vb = one("vb").rearrange("p (g b n) -> p g b n", g=3, b=2)

            def head_rows(h):
                s = HD * (h // 4)
                return slice(s, s + HD), h % 4

            def scores_first(kind, h, g):
                ps, done = tile_for(part, f"S{kind}{h}{g}")
                for b in range(NB):
                    if kind == "A":
                        r, c = head_rows(h)
                        q, k = qaT[r, c, b * P:(b + 1) * P], kaT[r, :]
                    else:
                        r, c = slice(HD * (h % 2), HD * (h % 2) + HD), h // 2
                        q, k = qbT[r, g, c, b * P:(b + 1) * P], kbT[r, g, c, :]
                    mm = pe.matmul(ps[:, b * TOKENS:(b + 1) * TOKENS], q, k, start=True, stop=True)
                mm.then_inc(done, 1)

            units = units_first()
            def open_group(u, base):
                if u % GROUP == 0 and (base is not None or u):
                    pe.wait_ge(group_evicted, u // GROUP if base is None else base + u // GROUP)

            def turn_outputs(t):
                y = one(("sga", "sgb")[t]).rearrange("p (b n) -> p b n", b=2)
                for b in range(NB):
                    pe.wait_ge(y_ready, 2 * t + 2)
                    turn(part, f"{('yA', 'yB')[t]}{b}", lambda c: y[:, b, c * P:(c + 1) * P])

            def step_first(e, u):
                kind, h, n = units[u]
                L = one("L").rearrange("p (s b j) -> p s b j", s=2, b=2)[:, u % 2]
                PT = one("PT").rearrange("p (s g j) -> p s g j", s=2, g=3)[:, u % 2]
                if e == "yA":
                    turn_outputs(0)
                elif e == "S":
                    if u == 0:
                        for p in NORMED:
                            for b in range(NB):
                                wait_evicted(part, f"{p}{b}")
                    for g in range(n):
                        scores_first(kind, h, g)
                elif e == "T":
                    pe.wait_ge(probs, u + 1)
                    for g in range(n):
                        turn(part, f"T{kind}{h}{g}",
                             lambda c: L[:, c // 2, g * TOKENS + (c % 2) * P:g * TOKENS + (c % 2 + 1) * P])
                else:
                    if u == 0:
                        for p in ("kava", "vb0", "vb1", "vb2"):
                            bp, before = part.turn("panel", p)
                            pe.wait_ge(panel_evicted[bp], before * 2 + 2)
                    open_group(u, None)
                    for g in range(n):
                        wait_evicted(part, f"T{kind}{h}{g}")
                    hd = slice((h % GROUP) * HD, (h % GROUP + 1) * HD)
                    for b in range(NB):
                        for g in range(n):
                            for k in range(2):
                                val = va[:, k, HD * (h // 4):HD * (h // 4) + HD] if kind == "A" else \
                                    vb[:, g, k, h * HD:(h + 1) * HD]
                                mm = pe.matmul(heads_out[:, b, hd], PT[:, g, (2 * b + k) * P:(2 * b + k + 1) * P], val,
                                               start=(g == 0 and k == 0), stop=(g == n - 1 and k == 1))
                    mm.then_inc(group_done if u % GROUP == GROUP - 1 else pv_done, 1)

            for p in FIRST_WIDE:
                rows_out(part, p, of_h, two_halves(p), 512, FIRST_PLAN, step_first)

            for t, name in enumerate(("yA", "yB")):
                for b in range(NB):
                    wait_evicted(part, f"{name}{b}")
                for c in range(2 - t):
                    rows_out(part, f"br{t}{c}", first_branch_parts(t), [f"br{t}{c}/0"],
                             after={1: lambda: turn_outputs(1)} if t == c == 0 else {})
            project_merged(part, "br11", first_branch_parts(1), {}, 0)

            with pe.Fori(0, LAYERS) as l:
                part = layer(l)
                turn_rows(part, "x", h_ready, l * 2 + 2)
                operand_ready(part, "x")
                for p in ("cb", "ca", "q", "k4"):
                    columns_out(part, p)
                rows_out(part, "vsg", of_h, two_halves("vsg"), 280)

                staged = tok[:, :, :].rearrange("p b (s n) -> p b s n", s=2)
                qT = two("qT").rearrange("p (c t) -> p c t", c=4)
                kT = two("kT").rearrange("p (i t) -> p i t", i=2)
                vsw = two("vsw").rearrange("p (b n) -> p b n", b=2)
                rT = two("rT").rearrange("p (c t) -> p c t", c=4)
                PR = two("PR").rearrange("p (h n) -> p h n", h=RET_H)
                PcT = two("PcT").rearrange("p (s q) -> p s q", s=4)
                Pc = two("Pc").rearrange("p (s n) -> p s n", s=4)
                acc = two("acc").rearrange("p (c t) -> p c t", c=4)
                units = units_layer()

                def compress(i):
                    name, half = (("cmpHk", "w1k"), ("cmpHv", "w1v"))[i]
                    ps, done = tile_for(part, name)
                    pe.wait_ge(blocks_ready, l + 1)
                    hi, lo = (w.rearrange("p (j n) -> p j n", j=16) for w in wait_parts(part, half))
                    blk_hi, blk_lo = (parts(AREA_2[n], 480 * i, 480).rearrange("p (j n) -> p j n", j=16)
                                      for n in ("blk_hi", "blk"))
                    to = ps[:, 0:30]
                    for j in range(16):
                        pe.matmul(to, hi[:, j, :], blk_hi[:, j, :], start=(j == 0), stop=False)
                        pe.matmul(to, hi[:, j, :], blk_lo[:, j, :], start=False, stop=False)
                        mm = pe.matmul(to, lo[:, j, :], blk_hi[:, j, :], start=False, stop=(j == 15))
                    mm.then_inc(done, 1)

                def compress_2():
                    ps, done = tile_for(part, "cmp2")
                    pe.wait_ge(hid_ready, l * 2 + 2)
                    pe.matmul(ps[:, 0:30], pars("w2k"), two("hgk")[:, 0:30], start=True, stop=True)
                    hgv = two("hgv").rearrange("p (g n) -> p g n", g=2)
                    for g in range(2):
                        mm = pe.matmul(ps[:, 64 + g * HD:64 + (g + 1) * HD], hgv[:, g, :], pars("w2v"), start=True, stop=True)
                    mm.then_inc(done, 1)

                def compressed_scores():
                    for g in range(2):
                        ps, done = tile_after(part, f"cmpS{g}", ["cmp2"] if g == 0 else [])
                        for b in range(NB):
                            for i in range(4):
                                r, c = head_rows(4 * g + i)
                                s = (b * 4 + i) * N_CMP
                                mm = pe.matmul(ps[:, s:s + N_CMP], qT[r, c, b * P:(b + 1) * P],
                                               two("kcmpT")[r, g * N_CMP:(g + 1) * N_CMP], start=True, stop=True)
                        mm.then_inc(done, 1)

                def compressed_out():
                    ps, done = panel_for(part, "Oc")
                    wait_evicted(part, "PcT")
                    vblk = two("vblk").rearrange("p (g n) -> p g n", g=2)
                    for b in range(NB):
                        for g in range(2):
                            mm = pe.matmul(ps[:, b, g * 4 * HD:(g + 1) * 4 * HD], PcT[:, 2 * b + g, :], vblk[:, g, :],
                                           start=True, stop=True)
                    mm.then_inc(done, 1)

                def ret_scores(h):
                    ps, done = tile_after(part, f"R{h}", transposed("rot") if h == 0 else [])
                    r = slice(HD * (h % 2), HD * (h % 2) + HD)
                    pe.matmul(ps[:, 0:TOKENS], rT[r, 2 + h // 2, 0:P], rT[r, h // 2, :], start=True, stop=True)
                    pe.matmul(ps[:, TOKENS:TOKENS + P], rT[r, 2 + h // 2, P:TOKENS], rT[r, h // 2, P:TOKENS],
                              start=True, stop=True).then_inc(done, 1)

                def retention_out():
                    vr = two("vr").rearrange("p (b n) -> p b n", b=2)
                    ps, done = panel_for(part, "Or")
                    bv, before = part.turn("panel", "vr")
                    pe.wait_ge(panel_evicted[bv], before * 2 + 2)
                    for h in range(RET_H):
                        wait_evicted(part, f"R{h}")
                        hv = slice(h * P, (h + 1) * P)
                        pe.matmul(ps[:, 0, hv], PR[:, h, 0:P], vr[:, 0, hv], start=True, stop=True)
                        pe.matmul(ps[:, 1, hv], PR[:, h, P:TOKENS], vr[:, 0, hv], start=True, stop=False)
                        mm = pe.matmul(ps[:, 1, hv], PR[:, h, TOKENS:TOKENS + P], vr[:, 1, hv], start=False, stop=True)
                    mm.then_inc(done, 1)

                def step_layer(e, u):
                    kind, h, _ = units[u]
                    w = 0 if kind == "s" else 1
                    r, c = head_rows(h)
                    L = two("L").rearrange("p (s j) -> p s j", s=2)[:, u % 2]
                    PT = two("PT").rearrange("p (s j) -> p s j", s=2)[:, u % 2]
                    if e == "S":
                        if u == 0:
                            for p in ("q", "k4"):
                                bp, before = part.turn("panel", p)
                                pe.wait_ge(panel_evicted[bp], before * 2 + 2)
                        ps, done = tile_for(part, f"S{kind}{h}0")
                        pe.matmul(ps[:, 0:P], qT[r, c, 0:P], kT[r, w, 0:P], start=True, stop=True)
                        pe.matmul(ps[:, P:3 * P], qT[r, c, P:TOKENS], kT[r, w, :], start=True, stop=True).then_inc(done, 1)
                    elif e == "T":
                        pe.wait_ge(probs, l * 16 + (16 + u + 1))
                        turn(part, f"T{kind}{h}0", lambda c: L[:, c * P:(c + 1) * P], n=3)
                    elif e == "V":
                        if u == 0:
                            bp, before = part.turn("panel", "vsg")
                            pe.wait_ge(panel_evicted[bp], before * 2 + 2)
                        open_group(u, l * 4 + 4)
                        wait_evicted(part, f"T{kind}{h}0")
                        hd = slice((h % GROUP) * HD, (h % GROUP + 1) * HD)
                        s = w * P + HD * (h // 4)
                        pe.matmul(heads_out[:, 0, hd], PT[:, 0:P], vsw[:, 0, s:s + HD], start=True, stop=True)
                        pe.matmul(heads_out[:, 1, hd], PT[:, P:2 * P], vsw[:, 0, s:s + HD], start=True, stop=False)
                        mm = pe.matmul(heads_out[:, 1, hd], PT[:, 2 * P:3 * P], vsw[:, 1, s:s + HD], start=False, stop=True)
                        mm.then_inc(group_done if u % GROUP == GROUP - 1 else pv_done, 1)
                    elif e in ("cmpHk", "cmpHv"):
                        compress(int(e == "cmpHv"))
                    elif e == "cmp2":
                        compress_2()
                    elif e == "cmpS":
                        compressed_scores()
                    elif e == "PcT":
                        pe.wait_ge(cmp_exp, l + 1)
                        turn(part, "PcT", lambda c: Pc[:, c, :])
                    elif e[0] == "R":
                        ret_scores(int(e[1]))
                    elif e in ("ro0", "ro1"):
                        pass
                    elif e == "rot":
                        for b in range(NB):
                            pe.wait_ge(rot_ready, l * 2 + (b + 1))
                            turn(part, f"rot{b}", lambda c: staged[:, b, 0, c * P:(c + 1) * P])
                    elif e == "oR":
                        for b in range(NB):
                            pe.wait_ge(ret_ready, l * 2 + (b + 1))
                            turn(part, f"oR{b}", lambda c: two("or").rearrange("p (b n) -> p b n", b=2)[:, b, c * P:(c + 1) * P])
                    elif e == "cv":
                        pe.wait_ge(conv_ready, l + 1)
                        for b in range(NB):
                            turn(part, f"cv{b}", lambda c: acc[:, c, b * P:(b + 1) * P])
                    elif e == "cz":
                        for b in range(NB):
                            pe.wait_ge(conv_normed, l * 2 + (b + 1))
                            turn(part, f"cz{b}", lambda c: staged[:, b, 1, c * P:(c + 1) * P])
                    elif e == "y":
                        for b in range(NB):
                            pe.wait_ge(y_ready, l * 2 + (4 + 2))
                            turn(part, f"y{b}", lambda c: two("y").rearrange("p (b n) -> p b n", b=2)[:, b, c * P:(c + 1) * P])

                for p in LAYER_WIDE:
                    rows_out(part, p, of_h, two_halves(p), 512, LAYER_PLAN, step_layer)
                    if p == "mg0":
                        compressed_out()
                    elif p == "mg1":
                        retention_out()
                last = {}
                for name in transposed("oR") + transposed("y"):
                    last[part.turn("tile", name)[0]] = name
                for name in last.values():
                    wait_evicted(part, name)
                for i in range(3):
                    if i == 2:
                        pe.wait_ge(branch_ready, l + 1)
                    for c in range(1 if i == 2 else 2):
                        rows_out(part, f"br{i}{c}", branch_parts(i), [f"br{i}{c}/0"])
                project_merged(part, "br21", branch_parts(2),
                               {3: lambda: turn_columns(part, "z", x, 0, x_updated, l * 4 + 2)}, l * 2 + 2)
                turn_columns(part, "z", x, 1, x_updated, l * 4 + 2)
                operand_ready(part, "z")
                for i in range(FF_PANELS):
                    columns_out(part, f"ff{i}")
                for c in range(2):
                    rows_out(part, f"down{c}", hidden_parts(), [f"down{c}/{i}" for i in range(FF_PANELS)],
                             ready=lambda i: pe.wait_ge(squared, l * 8 + (i + 1)))

        @block.scalar
        def _(act):
            def row_squares(b, n):
                return act.activation(tok[:, b, :], x[:, b, :], ACT.Square, accum_out=ss[:, b:b + 1]).then_inc(squares, 1)

            part = part_1
            act.wait_ge(x_loaded, 16)
            for b in range(NB):
                row_squares(b, b)
            rows = one("PT")[:, 0:2560].rearrange("p (t j) -> p t j", t=5)
            for t in range(5):
                ps = tile_of(act, part, f"bias{t}")
                act.activation(rows[0:H, t, :], ps[0:H, :], ACT.Copy).then_inc(tile_sem(part, f"bias{t}"), 1)
            round_half(act, part, 0)
            for t in range(5):
                b, before = part.turn("tile", f"bias{t}")
                act.wait_ge(tile_evicted[b], before + 1)
                act.dma_start(bias_rows[t], rows[0:H, t, :]).then_inc(rows_stored, 16)

            for n in range(1, HI_SLOTS):
                round_half(act, part, n)

            squares_of = one("L").rearrange("p (b n) -> p b n", b=6)
            gain = dict(qa=0, kava=1, qb0=2, qb1=2, qb2=2, kb0=3, kb1=3, kb2=3)

            def evict_heads(n):
                p = NORMED[n]
                col = 8 + gain[p]
                for b in range(NB):
                    ps = tile_of(act, part, f"{p}{b}")
                    if n == 0 and b == 0:
                        act.wait_ge(cw_ready, 1)
                    if p == "kava":
                        to, w = one("kaT")[:, b * P:(b + 1) * P], P
                        src = ps[:, 0:P]
                    else:
                        g = int(p[2]) if len(p) == 3 else 0
                        region = "qaT" if p == "qa" else p[0:2] + "T"
                        base = AREA_1[region][0] + g * 1024
                        to = area[:, base:base + 1024].rearrange("p (c t) -> p c t", c=4)[:, :, b * P:(b + 1) * P]
                        src = ps[:, :].rearrange("p (c t) -> p c t", c=4)
                    act.activation(to, src, ACT.Identity, scale=first[:, col:col + 1])\
                       .then_inc(tile_sem(part, f"{p}{b}"), 1)

            act.wait_ge(pad_ready, PADS)
            units = units_first()

            def exp_first(u):
                kind, h, n = units[u]
                L = one("L").rearrange("p (s b j) -> p s b j", s=2, b=2)[:, u % 2]
                act.wait_ge(logits, u + 1)
                if kind == "A":
                    act.activation(sinks[:, :, u:u + 1], sinks[:, :, u:u + 1], ACT.Exp)
                for b in range(NB):
                    e = act.activation(L[:, b, 0:n * TOKENS], L[:, b, 0:n * TOKENS], ACT.Exp, bias=negmax[:, b, u:u + 1],
                                       accum_out=den[:, b, u:u + 1])
                e.then_inc(probs, 1)

            def evict_outputs(t):
                for b in range(NB):
                    ps = tile_of(act, part, f"{('yA', 'yB')[t]}{b}")
                    act.activation(first_branch_parts(t)[0][:, :, b * P:(b + 1) * P], ps[:, :].rearrange("p (c t) -> p c t", c=4), ACT.Copy)\
                       .then_inc(y_high, 1)

            def step_first(e, u):
                kind, h, n = units[u]
                if e == "yA":
                    evict_outputs(0)
                elif e == "S" and u == 0:
                    exp_first(0)
                elif e == "T":
                    PT = one("PT").rearrange("p (s g j) -> p s g j", s=2, g=3)[:, u % 2]
                    if u >= 2:
                        wait_products(act, part, u - 2)
                    for g in (0, 2)[:n]:
                        ps = tile_of(act, part, f"T{kind}{h}{g}")
                        act.activation(PT[:, g, :], ps[:, :], ACT.Copy).then_inc(tile_sem(part, f"T{kind}{h}{g}"), 1)
                elif e == "V" and u + 1 < len(units):
                    exp_first(u + 1)

            for n, p in enumerate(FIRST_PANELS[:17]):
                for s in range(KC):
                    if s == 4:
                        round_after(act, part, f"{p}/0")
                    for e, u in FIRST_PLAN.get((p, s), []):
                        step_first(e, u)
                ps = panel_of(act, part, p)
                if n < len(NORMED):
                    for b in range(NB):
                        w = P if p == "kava" else 512
                        if n >= 1:
                            act.wait_ge(head_sum, NB * (n - 1) + b + 1)
                        act.activation(squares_of[:, b, 0:w], ps[:, b, 0:w], ACT.Square).then_inc(head_sq, 1)
                elif p in ("vb0", "vb1", "vb2"):
                    g = int(p[2])
                    to = one("vb").rearrange("p (g b n) -> p g b n", g=3, b=2)
                    for b in range(NB):
                        act.activation(to[:, g, b, :], ps[:, b, :], ACT.Copy).then_inc(panel_sem(part, p), 1)
                elif p in ("ga", "gb"):
                    to = one("mgt").rearrange("p (c b n) -> p c b n", c=4, b=2)[:, :, 1, :]
                    for b in range(NB):
                        act.activation(to[:, b + 2 * (p == "gb"), :], ps[:, b, :], ACT.Tanh, scale=0.5).then_inc(gate_tanh, 1)
                else:
                    c = int(p[2])
                    to = one("mgt").rearrange("p (c b n) -> p c b n", c=4, b=2)
                    src = tok[:, :, :].rearrange("p b (s n) -> p b s n", s=2)
                    if c == 0:
                        bg, before = part.turn("panel", "gb")
                        act.wait_ge(panel_evicted[bg], before * 2 + 2)
                    for b in range(NB):
                        act.wait_ge(merge_sum, NB * c + NB)
                        act.activation(to[:, c, b, :], src[:, b, c % 2, :], ACT.Tanh, scale=0.5)\
                           .then_inc(merge_tanh, 1)
                round_after(act, part, f"{p}/1")
                if 1 <= n <= len(NORMED):
                    evict_heads(n - 1)

            evict_outputs(1)

            def evict_operand(part):
                for b in range(NB):
                    for i in range(2):
                        ps = tile_of(act, part, f"x{b}{i}")
                        act.activation(hT_hi[:, 4 * i:4 * i + 4, b * P:(b + 1) * P], ps[:, :].rearrange("p (c t) -> p c t", c=4),
                                       ACT.Copy).then_inc(x_high, 1)

            def evict_merged(part, i):
                for b in range(NB):
                    ps = tile_of(act, part, f"m{b}{i}")
                    act.activation(hT_hi[:, 4 * i:4 * i + 4, b * P:(b + 1) * P], ps[:, :].rearrange("p (c t) -> p c t", c=4),
                                   ACT.Copy, scale=0.5).then_inc(merged_high, 1)

            round_after(act, part, "br00/0", "br01/0", "br10/0")
            evict_merged(part, 0)
            round_after(act, part, "br11/0")
            evict_merged(part, 1)
            round_after(act, part, "wo0/0", "wo0/1", "wo1/0", "wo1/1")

            with act.Fori(0, LAYERS) as l:
                part = layer(l)
                act.wait_ge(x_updated, l * 4 + 2)
                for b in range(NB):
                    row_squares(b, 0)
                evict_operand(part)
                tz = two("tz").rearrange("p (b n) -> p b n", b=2)
                round_after(act, part, "cb/0")
                ps = panel_of(act, part, "cb")
                for b in range(NB):
                    act.activation(tz[:, b, :], ps[:, b, :], ACT.Tanh, scale=0.5).then_inc(panel_sem(part, "cb"), 1)
                qT = two("qT").rearrange("p (b n) -> p b n", b=2)
                round_after(act, part, "cb/1", "ca/0", "ca/1", "q/0")
                ps = panel_of(act, part, "q")
                for b in range(NB):
                    act.activation(qT[:, b, :], ps[:, b, :], ACT.Copy, scale=HD ** -0.5).then_inc(panel_sem(part, "q"), 1)
                round_after(act, part, "q/1", "k4/0")
                ps = panel_of(act, part, "k4")
                act.activation(two("kT"), ps[:, 1, :], ACT.Copy).then_inc(panel_sem(part, "k4"), 1)
                round_after(act, part, "k4/1", "vsg/0")
                ps = panel_of(act, part, "vsg")
                vsw = two("vsw").rearrange("p (b n) -> p b n", b=2)
                gt = two("gt").rearrange("p (b n) -> p b n", b=2)
                for b in range(NB):
                    act.activation(vsw[:, b, :], ps[:, b, 0:256], ACT.Copy)
                    act.activation(gt[:, b, :], ps[:, b, 256:280], ACT.Tanh, scale=0.5).then_inc(panel_sem(part, "vsg"), 1)
                round_after(act, part, "vsg/1")
                rT = two("rT").rearrange("p (c t) -> p c t", c=4)
                mgt = two("mgt").rearrange("p (i b n) -> p i b n", i=6, b=2)
                z = two("z").rearrange("p (c t) -> p c t", c=4)
                units = units_layer()

                def exp_layer(u):
                    L = two("L").rearrange("p (s j) -> p s j", s=2)[:, u % 2]
                    act.wait_ge(logits, l * 16 + (16 + u + 1))
                    act.activation(L[:, 0:P], L[:, 0:P], ACT.Exp, bias=negmax[:, 0, u:u + 1], accum_out=den[:, 0, u:u + 1])
                    act.activation(L[:, P:3 * P], L[:, P:3 * P], ACT.Exp, bias=negmax[:, 1, u:u + 1],
                                   accum_out=den[:, 1, u:u + 1]).then_inc(probs, 1)

                def step_layer(e, u):
                    kind, h, _ = units[u]
                    if e == "S" and u == 0:
                        exp_layer(0)
                    elif e == "T":
                        PT = two("PT").rearrange("p (s j) -> p s j", s=2)[:, u % 2]
                        if u >= 2:
                            wait_products(act, part, u - 2)
                        ps = tile_of(act, part, f"T{kind}{h}0")
                        act.activation(PT, ps[:, 0:3 * P], ACT.Copy).then_inc(tile_sem(part, f"T{kind}{h}0"), 1)
                    elif e == "V" and u + 1 < len(units):
                        exp_layer(u + 1)
                    elif e == "cmpHv":
                        act.wait_ge(hid_in, l + 1)
                        act.activation(two("ht"), two("hy"), ACT.Tanh, scale=GELU_C).then_inc(hid_tanh, 1)
                    elif e == "rot":
                        for b in range(NB):
                            ps = tile_of(act, part, f"rot{b}")
                            act.activation(rT[:, :, b * P:(b + 1) * P], ps[:, :].rearrange("p (c t) -> p c t", c=4), ACT.Copy)\
                               .then_inc(tile_sem(part, f"rot{b}"), 1)
                    elif e == "cmp2":
                        ps = tile_of(act, part, "cmp2")
                        act.activation(two("kcmpT")[:, 0:30], ps[:, 0:30], ACT.Copy, scale=0.5)
                        vblk = two("vblk").rearrange("p (g i d) -> p g i d", g=2, i=4)
                        for i in range(4):
                            r = slice(32 * i, 32 * i + 32)
                            c = act.activation(vblk[r, :, i, :], ps[r, 64:64 + 2 * HD].rearrange("p (g d) -> p g d", g=2),
                                               ACT.Copy, scale=0.5)
                        c.then_inc(tile_sem(part, "cmp2"), 1)
                    elif e == "cmpS":
                        act.wait_ge(cmp_logits, l + 1)
                        Pc = two("Pc").rearrange("p (s n) -> p s n", s=16)[:, :, 0:N_CMP]
                        act.activation(Pc, two("Lc").rearrange("p (s n) -> p s n", s=16), ACT.Exp).then_inc(cmp_exp, 1)
                    elif e == "PcT":
                        ps = tile_of(act, part, "PcT")
                        act.activation(two("PcT"), ps[:, :], ACT.Copy).then_inc(tile_sem(part, "PcT"), 1)
                    elif e == "y":
                        for b in range(NB):
                            ps = tile_of(act, part, f"y{b}")
                            act.activation(branch_parts(0)[0][:, :, b * P:(b + 1) * P], ps[:, :].rearrange("p (c t) -> p c t", c=4),
                                           ACT.Copy, scale=0.5).then_inc(y_high, 1)
                    elif e == "cz":
                        for b in range(NB):
                            ps = tile_of(act, part, f"cz{b}")
                            for c in range(4):
                                i = act.activation(z[:, c, b * P:(b + 1) * P], ps[:, c * P:(c + 1) * P], ACT.Identity,
                                                   scale=lnh[:, 0, c:c + 1], bias=lnh[:, 1, c:c + 1])
                            i.then_inc(tile_sem(part, f"cz{b}"), 1)
                        act.drain()
                        act.activation(two("tz"), two("z"), ACT.Tanh).then_inc(conv_z, 1)

                for p in LAYER_WIDE:
                    for s in range(KC):
                        if s == 4:
                            round_after(act, part, *(["vr/0", "w1v"] if p == "vr" else [f"{p}/0"]))
                        for e, u in LAYER_PLAN[p, s]:
                            step_layer(e, u)
                    if p == "qkr":
                        round_after(act, part, "qkr/1", "w1k")
                        continue
                    ps = panel_of(act, part, p)
                    for b in range(NB):
                        if p == "vr":
                            act.activation(two("vr").rearrange("p (b n) -> p b n", b=2)[:, b, :], ps[:, b, :], ACT.Copy)\
                               .then_inc(panel_sem(part, p), 1)
                        elif p == "gr":
                            act.activation(two("tz").rearrange("p (b n) -> p b n", b=2)[:, b, :], ps[:, b, :],
                                           ACT.Tanh, scale=0.5).then_inc(gr_tanh, 1)
                        else:
                            i = int(p[2])
                            act.activation(mgt[:, i, b, :], ps[:, b, :], ACT.Tanh, scale=0.5)\
                               .then_inc(panel_sem(part, p), 1)
                    round_after(act, part, f"{p}/1")
                round_after(act, part, "br00/0", "br01/0", "br10/0", "br11/0", "br20/0")
                evict_merged(part, 0)
                round_after(act, part, "br21/0")
                evict_merged(part, 1)
                round_after(act, part, "wo0/0", "wo0/1", "wo1/0", "wo1/1")
                act.wait_ge(x_updated, l * 4 + 4)
                for b in range(NB):
                    row_squares(b, 0)
                sq = two("sq").rearrange("p (s n) -> p s n", s=2)
                for i in range(FF_PANELS):
                    round_after(act, part, f"ff{i}/0")
                    act.wait_ge(squares_full, l * 8 + (i + 1))
                    act.activation(hidden_parts()[0][:, 4 * i:4 * i + 4, :], sq[:, i % 2, :].rearrange("p (k t) -> p k t", k=4),
                                   ACT.Copy).then_inc(squares_high, 1)
                    round_after(act, part, f"ff{i}/1")
                round_after(act, part, *[f"down{c}/{i}" for c in range(2) for i in range(FF_PANELS)])
            act.wait_ge(x_updated, X_UPDATES)
            for b in range(NB):
                row_squares(b, 0)

        @block.vector
        def _(v):
            part = part_1
            v.memset(one("mgt")[32:33, 2560:2600], 1.0).then_inc(pad_ready, 1)
            v.memset(zero, 0.0).then_inc(pad_ready, 1)
            v.memset(low, -3.0e38).then_inc(pad_ready, 1)
            v.memset(half_power, -0.5).then_inc(pad_ready, 1)
            v.wait_ge(loaded, 16 * 6)
            for c in (8, 10):
                e = v.tensor_scalar(first[:, c:c + 1], first[:, c:c + 1], HD ** -0.5, None, ALU.mult)
            e.then_inc(cw_ready, 1)

            def rows_normed(part, base, tiles, gain):
                for b in range(NB):
                    v.wait_ge(rstd_ready, base + 1)
                    v.tensor_scalar(tok[:, b, :], x[:, b, :], rstd[:, b:b + 1], None, ALU.mult).then_inc(h_ready, 1)
                for b in range(NB):
                    for i in range(2):
                        operand_parts(part, tiles, b, i, gain)

            def operand_parts(part, tiles, b, i, gain):
                ps = tile_of(v, part, f"{tiles}{b}{i}")
                bs = slice(b * P, (b + 1) * P)
                v.tensor_tensor(hT_hi[:, 4 * i:4 * i + 4, bs], ps[:, :].rearrange("p (c t) -> p c t", c=4),
                                gain[:, 4 * i:4 * i + 4].unsqueeze(2).broadcast_to([P, 4, P]), ALU.mult)
                v.drain()
                for c in range(4):
                    k = 4 * i + c
                    e = v.scalar_tensor_tensor(hT_lo[:, k, bs], ps[:, c * P:(c + 1) * P], gain[:, k:k + 1],
                                               hT_hi[:, k, bs], ALU.mult, ALU.subtract)
                e.then_inc(tile_sem(part, f"{tiles}{b}{i}"), 1)

            def outputs_low(part, name, to, scale, base):
                for b in range(NB):
                    ps = tile_of(v, part, f"{name}{b}")
                    v.wait_ge(y_high, base + (b + 1))
                    bs = slice(b * P, (b + 1) * P)
                    v.scalar_tensor_tensor(to[1][:, :, bs], ps[:, :].rearrange("p (c t) -> p c t", c=4), scale,
                                           to[0][:, :, bs], ALU.mult, ALU.subtract).then_inc(tile_sem(part, f"{name}{b}"), 1)

            def low_tile(part, name, i, b, scale):
                ps = tile_of(v, part, f"{name}{b}{i}")
                ks, bs = slice(4 * i, 4 * i + 4), slice(b * P, (b + 1) * P)
                v.scalar_tensor_tensor(hT_lo[:, ks, bs], ps[:, :].rearrange("p (c t) -> p c t", c=4), scale,
                                       hT_hi[:, ks, bs], ALU.mult, ALU.subtract).then_inc(tile_sem(part, f"{name}{b}{i}"), 1)

            def merged_low(part, i, base):
                for b in range(NB):
                    v.wait_ge(merged_high, base + (2 * i + b + 1))
                    low_tile(part, "m", i, b, 0.5)

            rows_normed(part, 0, "x", first[:, 0:8])
            squares_of = one("L").rearrange("p (b n) -> p b n", b=6)
            staged = tok[:, :, :].rearrange("p b (s n) -> p b s n", s=2)
            units = units_first()
            Es = one("E").rearrange("p (s t j) -> p s t j", s=2, t=3)

            def logits_first(u):
                kind, h, n = units[u]
                L = one("L").rearrange("p (s b j) -> p s b j", s=2, b=2)[:, u % 2]
                mx = mxs[u % 2]
                load = h // 2 if kind == "A" else 4 + h
                v.wait_ge(E_loaded[load % 2], 16 * (load // 2 + 1))
                if u >= 2:
                    k2, h2, n2 = units[u - 2]
                    for g in range(n2):
                        tile_of(v, part, f"T{k2}{h2}{g}")
                for g in range(n):
                    ps = tile_of(v, part, f"S{kind}{h}{g}")
                    E = Es[:, load % 2, h % 2 if kind == "A" else g, :]
                    for b in range(NB):
                        init = first[:, 12 + h:13 + h] if kind == "A" else low
                        e = v.tensor_tensor_reduce(L[:, b, g * TOKENS:(g + 1) * TOKENS], ps[:, b * TOKENS:(b + 1) * TOKENS],
                                                   E[:, P * (1 - b):P * (1 - b) + TOKENS], 1.0, init, ALU.add, ALU.max,
                                                   mx[:, b, g:g + 1])
                    e.then_inc(tile_sem(part, f"S{kind}{h}{g}"), 1)
                v.drain()
                r = v.tensor_reduce(negmax[:, :, u:u + 1], mx[:, :, 0:n], AX.X, ALU.max, negate=True)
                if kind == "A":
                    v.drain()
                    r = v.tensor_scalar(sinks[:, :, u:u + 1], negmax[:, :, u:u + 1], first[:, 12 + h:13 + h], None, ALU.add)
                r.then_inc(logits, 1)
                if kind == "B" or h % 2 == 1:
                    v.sem_inc(E_used, 1)

            def step_first(e, u):
                kind, h, n = units[u]
                if e == "S":
                    logits_first(u)
                elif e == "yA":
                    tile_of(v, part, "yA1")
                    outputs_low(part, "yA", first_branch_parts(0), 1.0, 0)
                elif e == "T" and n == 3:
                    if u >= 2:
                        wait_products(v, part, u - 2)
                    PT = one("PT").rearrange("p (s g j) -> p s g j", s=2, g=3)[:, u % 2]
                    ps = tile_of(v, part, f"T{kind}{h}1")
                    v.tensor_copy(PT[:, 1, :], ps[:, :]).then_inc(tile_sem(part, f"T{kind}{h}1"), 1)
                elif e == "V" and u % GROUP == GROUP - 1:
                    normed_out(v, part, u // GROUP)

            for n, p in enumerate(FIRST_PANELS[:17]):
                for s in range(KC):
                    for e, u in FIRST_PLAN.get((p, s), []):
                        step_first(e, u)
                if n < len(NORMED):
                    nh = 2 if p == "kava" else 8
                    for b in range(NB):
                        v.wait_ge(head_sq, NB * n + b + 1)
                        if n >= 1:
                            v.wait_ge(head_rstd, n)
                        v.tensor_reduce(hs[:, b, 0:nh], squares_of[:, b, 0:nh * HD].rearrange("p (h d) -> p h d", d=HD),
                                        AX.X, ALU.add).then_inc(head_sum, 1)
                    ps = panel_of(v, part, p)
                    v.wait_ge(head_rstd, n + 1)
                    for b in range(NB):
                        if n >= 2:
                            tile_of(v, part, f"{NORMED[n - 2]}{b}")
                        e = v.tensor_tensor(staged[:, b, n % 2, 0:nh * HD].rearrange("p (h d) -> p h d", d=HD),
                                            ps[:, b, 0:nh * HD].rearrange("p (h d) -> p h d", d=HD),
                                            hr[:, b, 0:nh].unsqueeze(2).broadcast_to([P, nh, HD]), ALU.mult)
                        e.then_inc(head_normed, 1)
                        if p == "kava":
                            va = one("va").rearrange("p (b n) -> p b n", b=2)
                            v.tensor_copy(va[:, b, :], ps[:, b, P:2 * P])\
                             .then_inc(panel_sem(part, p), 1)
                    if p != "kava":
                        for b in range(NB):
                            v.wait_ge(head_normed, NB * n + b + 1)
                            v.sem_inc(panel_sem(part, p), 1)
                elif p in ("ga", "gb"):
                    ps = panel_of(v, part, p)
                    i = int(p == "gb")
                    t = one("mgt").rearrange("p (c b n) -> p c b n", c=4, b=2)[:, :, 1, :]
                    to = one("sga" if p == "ga" else "sgb").rearrange("p (b n) -> p b n", b=2)
                    for b in range(NB):
                        v.wait_ge(gate_tanh, NB * i + b + 1)
                        v.scalar_tensor_tensor(to[:, b, :], t[:, b + 2 * i, :], 1.0, ps[:, b, :], ALU.add, ALU.mult)\
                         .then_inc(panel_sem(part, p), 1)
                elif p.startswith("mg"):
                    ps = panel_of(v, part, p)
                    c = int(p[2])
                    bm = one("mgt").rearrange("p (c b n) -> p c b n", c=4, b=2)[:, c, 0, :]
                    v.wait_ge(bmerge_loaded, 16)
                    if c == 0:
                        for b in range(NB):
                            tile_of(v, part, f"kb2{b}")
                            tile_of(v, part, f"kb1{b}")
                    for b in range(NB):
                        if c >= 2:
                            v.wait_ge(merge_tanh, NB * (c - 2) + b + 1)
                        v.tensor_tensor(staged[:, b, c % 2, :], ps[:, b, :], bm, ALU.add).then_inc(merge_sum, 1)
                    for b in range(NB):
                        v.wait_ge(merge_sum, NB * c + b + 1)
                        v.sem_inc(panel_sem(part, p), 1)

            def merge(part, branches, mgt, base):
                for i in range(branches):
                    for c in range(2):
                        ps = panel_of(v, part, f"br{i}{c}")
                        cs = slice(c * 512, (c + 1) * 512)
                        for b in range(NB):
                            g = mgt[:, 2 * i + c, b, :]
                            if i == 0:
                                v.scalar_tensor_tensor(tok[:, b, cs], g, 1.0, ps[:, b, :], ALU.add, ALU.mult)\
                                 .then_inc(panel_sem(part, f"br{i}{c}"), 1)
                            else:
                                v.scalar_tensor_tensor(g, g, 1.0, ps[:, b, :], ALU.add, ALU.mult)\
                                 .then_inc(panel_sem(part, f"br{i}{c}"), 1)
                        if i:
                            v.drain()
                            for b in range(NB):
                                g = mgt[:, 2 * i + c, b, :]
                                e = v.tensor_tensor(tok[:, b, cs], tok[:, b, cs], g, ALU.add)
                            if i == branches - 1:
                                e.then_inc(merged, 1)
                                merged_low(part, c, base)

            def add_columns(part, name, c, scale=None):
                ps = panel_of(v, part, name)
                cs = slice(c * 512, (c + 1) * 512)
                for b in range(NB):
                    if scale is None:
                        v.tensor_tensor(x[:, b, cs], x[:, b, cs], ps[:, b, :], ALU.add).then_inc(panel_sem(part, name), 1)
                    else:
                        v.scalar_tensor_tensor(x[:, b, cs], ps[:, b, :], scale[:, b:b + 1], x[:, b, cs], ALU.mult, ALU.add)\
                         .then_inc(panel_sem(part, name), 1)
                v.drain().then_inc(x_updated, 1)

            v.wait_ge(merge_tanh, NB * 4)
            outputs_low(part, "yB", first_branch_parts(1), 1.0, 2)
            merge(part, 2, one("mgt").rearrange("p (c b n) -> p c b n", c=4, b=2), 0)
            for c in range(2):
                add_columns(part, f"wo{c}", c)
            u_all = two("u").rearrange("p (c t) -> p c t", c=4)
            hgv = two("hgv").rearrange("p (g q n) -> p g q n", g=2, q=4)
            v.memset(u_all[:, :, 0:32], 0.0)
            v.memset(two("hgv"), 0.0)
            v.memset(two("Pc"), 0.0)
            v.memset(two("hx"), 0.0)
            v.memset(two("vblk"), 0.0)
            v.drain()

            with v.Fori(0, LAYERS) as l:
                part = layer(l)
                v.wait_ge(par_loaded, l * 16 + 16)
                v.tensor_scalar(cw[:, :, :], pars("conv_w").rearrange("p (c j) -> p c j", c=4), 0.5, None, ALU.mult)
                for i, name in enumerate(("ln_g", "ln_b", "gn")):
                    v.tensor_scalar(lnh[:, i, :], pars(name), 0.5, None, ALU.mult)
                v.drain().then_inc(cw_ready, 1)
                v.wait_ge(rstd_ready, l * 2 + 2)
                v.wait_ge(gain_loaded, l * 16 + 16)
                for b in range(NB):
                    v.scalar_tensor_tensor(tok[:, b, :], x[:, b, :], rstd[:, b:b + 1], two("gain"), ALU.mult, ALU.mult)\
                     .then_inc(h_ready, 1)
                for b in range(NB):
                    for i in range(2):
                        v.wait_ge(x_high, l * 4 + (2 * b + i + 1))
                        low_tile(part, "x", i, b, 1.0)
                tz = two("tz").rearrange("p (b n) -> p b n", b=2)
                bc, before = part.turn("panel", "cb")
                v.wait_ge(panel_evicted[bc], before * 2 + 2)
                ps = panel_of(v, part, "ca")
                for b in range(NB):
                    v.scalar_tensor_tensor(u_all[:, 2 * b:2 * b + 2, 32:288], tz[:, b, :].rearrange("p (c t) -> p c t", c=2), 1.0,
                                           ps[:, b, :].rearrange("p (c t) -> p c t", c=2), ALU.add, ALU.mult)\
                     .then_inc(panel_sem(part, "ca"), 1)
                v.drain()
                acc = two("acc").rearrange("p (c t) -> p c t", c=4)
                cb_ = pars("conv_b")

                def taps(first_tap, last_tap):
                    for j in range(first_tap, last_tap):
                        for c in range(4):
                            src = u_all[:, c, 2 + j:2 + j + TOKENS]
                            if j == 0:
                                v.tensor_scalar(acc[:, c, :], src, cw[:, c, 0:1], cb_[:, c:c + 1], ALU.mult, ALU.add)
                            else:
                                v.scalar_tensor_tensor(acc[:, c, :], src, cw[:, c, j:j + 1], acc[:, c, :], ALU.mult, ALU.add)
                        v.drain()

                ps = panel_of(v, part, "k4")
                kcP = two("kcP").rearrange("p (i g t) -> p i g t", i=2, g=2)
                for i in range(2):
                    for g in range(2):
                        s = i * TOKENS
                        rows = slice(HD * g, HD * g + HD)
                        v.tensor_copy(kcP[0:HD, i, g, :], ps[rows, 0, s:s + TOKENS])
                        e = v.tensor_copy(kcP[HD:P, i, g, 0:TOKENS - 1], ps[rows, 0, s + 1:s + TOKENS])
                e.then_inc(panel_sem(part, "k4"), 1)
                v.drain()
                blk = two("blk").rearrange("p (i j n) -> p i j n", i=2, j=16)
                pe_ = pars("pe").rearrange("p (i j) -> p i j", i=2)
                for i in range(2):
                    for g in range(2):
                        lo = kcP[:, i, g, :].rearrange("p (n j s) -> p j n s", j=8, s=2)
                        for half in range(2):
                            src = lo[:, :, half:half + N_CMP, 0]
                            e = v.tensor_tensor(blk[:, i, 8 * half:8 * half + 8, g * N_CMP:(g + 1) * N_CMP], src,
                                                pe_[:, i, 8 * half:8 * half + 8].unsqueeze(2).broadcast_to([P, 8, N_CMP]), ALU.add)
                v.drain()
                blk_hi = parts(AREA_2["blk_hi"], 0, 960)
                v.tensor_copy(blk_hi, two("blk"))
                v.drain()
                v.tensor_tensor(parts(AREA_2["blk"], 0, 960), two("blk"), blk_hi, ALU.subtract).then_inc(blocks_ready, 1)
                units = units_layer()
                En = two("En").rearrange("p (h j) -> p h j", h=H)
                Lc = two("Lc").rearrange("p (b h n) -> p b h n", b=2, h=H)
                PR = two("PR").rearrange("p (h n) -> p h n", h=RET_H)
                hx, hy, ht = two("hx"), two("hy"), two("ht")
                gt = two("gt").rearrange("p (b h i) -> p b h i", b=2, h=H)
                sgr = two("sgr").rearrange("p (b n) -> p b n", b=2)
                o_r = two("or").rearrange("p (b n) -> p b n", b=2)

                def logits_layer(u):
                    kind, h, _ = units[u]
                    mx = mxs[u % 2]
                    L = two("L").rearrange("p (s j) -> p s j", s=2)[:, u % 2]
                    if u >= 2:
                        k2, h2, _ = units[u - 2]
                        tile_of(v, part, f"T{k2}{h2}0")
                        v.sem_inc(taken, 1)
                    elif u == 0:
                        v.wait_ge(En_loaded, 16)
                    ps = tile_of(v, part, f"S{kind}{h}0")
                    v.sem_inc(taken, 1)
                    v.tensor_tensor_reduce(L[:, 0:P], ps[:, 0:P], En[:, h, P:2 * P], 1.0, -3.0e38, ALU.add, ALU.max, mx[:, 0, 0:1])
                    v.tensor_tensor_reduce(L[:, P:3 * P], ps[:, P:3 * P], En[:, h, 0:TOKENS], 1.0, -3.0e38, ALU.add, ALU.max,
                                           mx[:, 1, 0:1]).then_inc(tile_sem(part, f"S{kind}{h}0"), 1)
                    v.drain()
                    v.tensor_scalar(negmax[:, :, u:u + 1], mx[:, :, 0:1], -1.0, None, ALU.mult).then_inc(logits, 1)

                def gelu():
                    ps = tile_of(v, part, "cmpHv")
                    v.tensor_copy(hx[:, 32:62], ps[:, 0:30]).then_inc(tile_sem(part, "cmpHv"), 1)
                    v.drain()
                    v.tensor_tensor(hy, hx, hx, ALU.mult)
                    v.drain()
                    v.tensor_scalar(hy, hy, GELU_A, 1.0, ALU.mult, ALU.add)
                    v.drain()
                    v.tensor_tensor(hy, hy, hx, ALU.mult).then_inc(hid_in, 1)
                    v.wait_ge(hid_tanh, l + 1)
                    v.scalar_tensor_tensor(two("hgk"), ht[:, 0:32], 1.0, hx[:, 0:32], ALU.add, ALU.mult).then_inc(hid_ready, 1)
                    for g in range(2):
                        s = 32 + g * N_CMP
                        e = v.scalar_tensor_tensor(hgv[:, g, :, 0:N_CMP], ht[:, s:s + N_CMP].unsqueeze(1).broadcast_to([P, 4, N_CMP]),
                                                   1.0, hx[:, s:s + N_CMP].unsqueeze(1).broadcast_to([P, 4, N_CMP]), ALU.add, ALU.mult)
                    e.then_inc(hid_ready, 1)

                def rotate(b):
                    ps = panel_of(v, part, "qkr")
                    t4 = two("or").rearrange("p (i h d) -> p i h d", i=4, h=8)
                    src = ps[:, b, :].rearrange("p (h s d) -> p h s d", h=8, s=2)
                    dst = staged[:, b, 0, :].rearrange("p (h s d) -> p h s d", h=8, s=2)
                    cos, sin = (rope[:, b, i, :].unsqueeze(1).broadcast_to([P, 8, 32]) for i in range(2))
                    v.tensor_tensor(t4[:, 0], src[:, :, 0, :], cos, ALU.mult)
                    v.tensor_tensor(t4[:, 1], src[:, :, 1, :], sin, ALU.mult)
                    v.tensor_tensor(t4[:, 2], src[:, :, 0, :], sin, ALU.mult)
                    v.tensor_tensor(t4[:, 3], src[:, :, 1, :], cos, ALU.mult).then_inc(panel_sem(part, "qkr"), 1)
                    v.drain()
                    v.tensor_tensor(dst[:, :, 0, :], t4[:, 0], t4[:, 1], ALU.subtract)
                    v.tensor_tensor(dst[:, :, 1, :], t4[:, 2], t4[:, 3], ALU.add).then_inc(rot_ready, 1)
                    v.drain()

                def compressed_logits():
                    for g in range(2):
                        ps = tile_of(v, part, f"cmpS{g}")
                        for b in range(NB):
                            s = 31 + P * (1 - b)
                            src = ps[:, b * 4 * N_CMP:(b + 1) * 4 * N_CMP].rearrange("p (h n) -> p h n", h=4)
                            hg = slice(4 * g, 4 * g + 4)
                            e = v.tensor_tensor(Lc[:, b, hg], src, En[:, hg, s:s + (N_CMP - 1) * CMP_STRIDE + 1:CMP_STRIDE], ALU.add)
                        e.then_inc(tile_sem(part, f"cmpS{g}"), 1)
                    v.drain()
                    v.tensor_reduce(cmx[:, :, :], Lc[:, :, :, :], AX.X, ALU.max)
                    v.drain()
                    v.tensor_scalar(cmx[:, :, :], cmx[:, :, :], -1.0e29, None, ALU.max)
                    v.drain()
                    v.tensor_tensor(Lc[:, :, :, :], Lc[:, :, :, :], cmx[:, :, :].unsqueeze(3).broadcast_to([P, 2, H, N_CMP]),
                                    ALU.subtract).then_inc(cmp_logits, 1)

                def compressed_coefficients():
                    v.wait_ge(cmp_exp, l + 1)
                    Pc = two("Pc").rearrange("p (b h n) -> p b h n", b=2, h=H)
                    v.tensor_reduce(cden[:, :, :], Pc[:, :, :, 0:N_CMP], AX.X, ALU.add)
                    v.drain()
                    v.tensor_scalar(cden[:, :, :], cden[:, :, :], 1e-30, None, ALU.max)
                    v.drain()
                    v.reciprocal(cden[:, :, :], cden[:, :, :])
                    v.drain()
                    v.scalar_tensor_tensor(coef_c[:, :, :], gt[:, :, :, 0], 1.0, cden[:, :, :], ALU.add, ALU.mult)

                def decayed(h):
                    ps = tile_of(v, part, f"R{h}")
                    v.wait_ge(decay_loaded, 16)
                    v.tensor_tensor(PR[:, h, 0:TOKENS], ps[:, 0:TOKENS], decay[:, h, :], ALU.mult)
                    v.tensor_tensor(PR[:, h, TOKENS:TOKENS + P], ps[:, TOKENS:TOKENS + P], decay[:, h, 0:P], ALU.mult)\
                     .then_inc(tile_sem(part, f"R{h}"), 1)

                def compressed_out():
                    yc = two("yc").rearrange("p (b n) -> p b n", b=2)
                    ps = panel_of(v, part, "Oc")
                    for b in range(NB):
                        v.tensor_tensor(yc[:, b, :].rearrange("p (h d) -> p h d", h=H), ps[:, b, :].rearrange("p (h d) -> p h d", h=H),
                                        coef_c[:, b, :].unsqueeze(2).broadcast_to([P, H, HD]), ALU.mult)\
                         .then_inc(panel_sem(part, "Oc"), 1)

                def retention_norm():
                    ps = panel_of(v, part, "Or")
                    for b in range(NB):
                        for h in range(RET_H):
                            v.bn_stats(bns[:, 4 * b + h, :], ps[:, b, h * P:(h + 1) * P])
                    v.drain()
                    for i in range(8):
                        v.bn_aggr(bna[:, i, :], bns[:, i, :])
                    v.drain().then_inc(ret_stats, 1)
                    v.wait_ge(ret_rstd, l + 1)
                    for b in range(NB):
                        for h in range(RET_H):
                            hv = slice(h * P, (h + 1) * P)
                            v.tensor_scalar(o_r[:, b, hv], ps[:, b, hv], bna[:, 4 * b + h, 0:1], brs[:, b, h:h + 1],
                                            ALU.subtract, ALU.mult)
                        v.drain().then_inc(panel_sem(part, "Or"), 1)
                        v.tensor_tensor(o_r[:, b, :], o_r[:, b, :], sgr[:, b, :], ALU.mult).then_inc(ret_ready, 1)

                def step_layer(e, u):
                    if e == "S":
                        logits_layer(u)
                    elif e in ("T", "V"):
                        taps(2 * u + (e == "V"), min(2 * u + (e == "V") + 1, TAPS))
                        if e == "V" and u % GROUP == GROUP - 1:
                            sum_out(v, part, l, u // GROUP)
                        if 2 * u + (e == "V") == TAPS - 1:
                            v.sem_inc(conv_ready, 1)
                    elif e == "cmpHk":
                        ps = tile_of(v, part, e)
                        v.tensor_copy(hx[:, 0:30], ps[:, 0:30]).then_inc(tile_sem(part, e), 1)
                    elif e == "cmpHv":
                        gelu()
                    elif e in ("ro0", "ro1"):
                        rotate(int(e[2]))
                    elif e == "rot":
                        pass
                    elif e == "cmpS":
                        compressed_logits()
                    elif e == "PcT":
                        compressed_coefficients()
                    elif e[0] == "R":
                        decayed(int(e[1]))
                    elif e == "oR":
                        for b in range(NB):
                            ps = tile_of(v, part, f"oR{b}")
                            hi, lo = branch_parts(1)
                            bs = slice(b * P, (b + 1) * P)
                            v.tensor_tensor(hi[:, :, bs], ps[:, :].rearrange("p (c t) -> p c t", c=4),
                                            lnh[:, 2, :].unsqueeze(2).broadcast_to([P, 4, P]), ALU.mult)
                            v.drain()
                            for c in range(4):
                                r = v.scalar_tensor_tensor(lo[:, c, bs], ps[:, c * P:(c + 1) * P], lnh[:, 2, c:c + 1], hi[:, c, bs],
                                                           ALU.mult, ALU.subtract)
                            r.then_inc(tile_sem(part, f"oR{b}"), 1)
                    elif e == "y":
                        outputs_low(part, "y", branch_parts(0), 0.5, l * 2 + 4)
                    elif e == "cv":
                        pss = [tile_of(v, part, f"cv{b}") for b in range(NB)]
                        for b in range(NB):
                            v.bn_stats(cns[:, b, :], pss[b][:, :])
                        v.drain()
                        for b in range(NB):
                            v.bn_aggr(cna[:, b, :], cns[:, b, :])
                        v.drain().then_inc(conv_stats, 1)
                        v.wait_ge(conv_rstd, l + 1)
                        for b in range(NB):
                            v.tensor_scalar(staged[:, b, 1, :], pss[b][:, :], cna[:, b, 0:1], crs[:, b:b + 1], ALU.subtract, ALU.mult)
                            v.drain().then_inc(tile_sem(part, f"cv{b}"), 1)
                            v.sem_inc(conv_normed, 1)

                for p in LAYER_WIDE:
                    for s in range(KC):
                        for e, u in LAYER_PLAN[p, s]:
                            step_layer(e, u)
                    if p == "gr":
                        ps = panel_of(v, part, "gr")
                        tg = two("tz").rearrange("p (b n) -> p b n", b=2)
                        for b in range(NB):
                            v.wait_ge(gr_tanh, l * 2 + (b + 1))
                            v.scalar_tensor_tensor(sgr[:, b, :], tg[:, b, :], 1.0, ps[:, b, :], ALU.add, ALU.mult)\
                             .then_inc(panel_sem(part, "gr"), 1)
                    elif p == "mg0":
                        compressed_out()
                    elif p == "mg1":
                        retention_norm()
                v.wait_ge(conv_z, l + 1)
                v.scalar_tensor_tensor(two("z"), two("tz"), 1.0, two("z"), ALU.add, ALU.mult)
                v.drain()
                hi, lo = parts(AREA_2["brT"], 2048, 1024), parts(LOW_OF_BRANCH[2], 0, 1024)
                v.tensor_copy(hi, two("z"))
                v.drain()
                v.tensor_tensor(lo, two("z"), hi, ALU.subtract).then_inc(branch_ready, 1)
                merge(part, 3, two("mgt").rearrange("p (i b n) -> p i b n", i=6, b=2), l * 4 + 4)
                for c in range(2):
                    add_columns(part, f"wo{c}", c)
                    for b in range(NB):
                        operand_parts(part, "z", b, c, pars("mlp"))
                hi, lo = hidden_parts()
                sq = two("sq").rearrange("p (s b n) -> p s b n", s=2, b=2)

                def squares_low(i):
                    ks = slice(4 * i, 4 * i + 4)
                    v.wait_ge(squares_high, l * 8 + (i + 1))
                    v.tensor_tensor(lo[:, ks, :], sq[:, i % 2].rearrange("p b (k t) -> p (b k) t", k=2), hi[:, ks, :],
                                    ALU.subtract).then_inc(squared, 1)

                for i in range(FF_PANELS):
                    if i >= 2:
                        v.drain()
                    ps = panel_of(v, part, f"ff{i}")
                    for b in range(NB):
                        v.tensor_scalar(sq[:, i % 2, b, :], ps[:, b, :], 0.0, None, ALU.max).then_inc(panel_sem(part, f"ff{i}"), 1)
                    v.drain()
                    v.tensor_tensor(sq[:, i % 2], sq[:, i % 2], sq[:, i % 2], ALU.mult).then_inc(squares_full, 1)
                    squares_low(i)
                v.wait_ge(rstd_ready, l * 2 + 3)
                v.tensor_tensor(rstd_sq, rstd, rstd, ALU.mult)
                v.drain()
                for c in range(2):
                    add_columns(part, f"down{c}", c, rstd_sq)
            v.wait_ge(rstd_ready, 2 * LAYERS + 2)
            v.wait_ge(gain_loaded, 16 * (LAYERS + 1))
            for b in range(NB):
                v.scalar_tensor_tensor(tok[:, b, :], x[:, b, :], rstd[:, b:b + 1], two("gain"), ALU.mult, ALU.mult)\
                 .then_inc(result_ready, 1)

        @block.gpsimd
        def _(g):
            def inverse_root(to, of, scale, out_sem, shape_power):
                g.sem_inc(taken, 1)
                g.tensor_scalar(to, of, scale, EPS, ALU.mult, ALU.add)
                g.drain()
                g.tensor_tensor(to, to, shape_power, ALU.pow).then_inc(out_sem, 1)

            g.wait_ge(pad_ready, PADS)
            g.wait_ge(squares, 2)
            inverse_root(rstd, ss, 1.0 / D, rstd_ready, half_power[:, 0:2])
            for n in range(HI_SLOTS):
                low_half(g, part_1, n)
            low = HI_SLOTS
            for n, p in enumerate(NORMED):
                until = index_of(part_1, f"{p}/0") + HI_SLOTS + 1
                for i in range(low, until):
                    low_half(g, part_1, i)
                low = until
                nh = 2 if p == "kava" else 8
                g.wait_ge(head_sum, NB * (n + 1))
                if n >= 1:
                    g.wait_ge(head_normed, NB * n)
                inverse_root(hr[:, :, 0:nh], hs[:, :, 0:nh], 1.0 / HD, head_rstd,
                             half_power[:, 0:nh].unsqueeze(1).broadcast_to([P, 2, nh]))
            for n in range(low, len(FIRST_HALVES) + HI_SLOTS):
                low_half(g, part_1, n)
            with g.Fori(0, LAYERS) as l:
                part = layer(l)
                g.wait_ge(squares, l * 4 + 4)
                inverse_root(rstd, ss, 1.0 / D, rstd_ready, half_power[:, 0:2])
                after_mg1, after_mg4, in_mlp = (index_of(part, h) + HI_SLOTS + 1 for h in ("mg1/1", "mg4/1", "ff0/1"))
                for n in range(HI_SLOTS, after_mg1):
                    low_half(g, part, n)
                g.wait_ge(ret_stats, l + 1)
                inverse_root(brs[:, :, :], bna[:, :, 1:2].rearrange("p (b h) o -> p b (h o)", b=2), 1.0, ret_rstd,
                             half_power[:, 0:4].unsqueeze(1).broadcast_to([P, 2, 4]))
                for n in range(after_mg1, after_mg4):
                    low_half(g, part, n)
                g.wait_ge(conv_stats, l + 1)
                inverse_root(crs, cna[:, :, 1], 1.0, conv_rstd, half_power[:, 0:2])
                for n in range(after_mg4, in_mlp):
                    low_half(g, part, n)
                g.wait_ge(squares, l * 4 + 6)
                inverse_root(rstd, ss, 1.0 / D, rstd_ready, half_power[:, 0:2])
                for n in range(in_mlp, N_HALVES + HI_SLOTS):
                    low_half(g, part, n)
            g.wait_ge(squares, 4 * LAYERS + 4)
            inverse_root(rstd, ss, 1.0 / D, rstd_ready, half_power[:, 0:2])


PAIRS = [0, 4, 1, 5, 2, 6, 3, 7]


def t5_bucket(rel):
    n = np.abs(rel)
    nf = np.maximum(n, 8).astype(np.float32)
    large = 8 + (np.log(nf / np.float32(8)) / np.float32(np.log(1024 / 8)) * np.float32(8)).astype(np.int32)
    return (rel > 0) * 16 + np.where(n < 8, n, np.minimum(large, 15))


def causal_bucket(dist):
    n = np.maximum(dist, 0)
    nf = np.maximum(n, 1).astype(np.float32)
    large = 16 + (np.log(nf / np.float32(16)) / np.float32(np.log(128 / 16)) * np.float32(16)).astype(np.int32)
    return np.where(n < 16, n, np.minimum(large, 31))


def position_table():
    t = np.zeros((33, 5, 512), np.float32)
    rel = np.arange(512) - 255
    kinds = [(np.abs(rel) <= P, t5_bucket(rel))]
    for window, dilation in GROUPS:
        reach = window // (2 * dilation) * dilation
        kinds.append(((rel % dilation == 0) & (np.abs(rel) <= reach), t5_bucket(rel)))
    kinds.append((rel <= 0, causal_bucket(-rel)))
    for i, (valid, bucket) in enumerate(kinds):
        for j in range(512):
            if valid[j]:
                t[bucket[j], i, j] = 1.0
            else:
                t[32, i, j] = MASKED
    return t.reshape(33, -1)


def decay_table():
    log_g = np.log1p(-np.exp2(-5.0 - np.arange(RET_H)))
    d = np.arange(TOKENS)[None, None, :] - np.arange(P)[:, None, None]
    return (np.where(d >= 0, np.exp(log_g[None, :, None] * np.maximum(d, 0)), 0.0) * HD ** -0.5).astype(np.float32)


def rope_table():
    half = HD // 2
    inv = np.float32(10000.0) ** (-np.arange(half, dtype=np.float32) / np.float32(half))
    ang = (np.arange(TOKENS, dtype=np.float32)[:, None] * inv[None, :]).astype(np.float32)
    t = np.stack([np.cos(ang), np.sin(ang)], 1).astype(np.float32)
    return np.ascontiguousarray(t.reshape(NB, P, 2, half).transpose(1, 0, 2, 3))


def chunks(w):
    k, n = w.shape
    return [np.ascontiguousarray(w[i * 512:(i + 1) * 512].reshape(4, P, n).transpose(1, 0, 2)).reshape(P, 4 * n)
            for i in range(k // 512)]


def column_chunks(w):
    return [w[:, i * 256:(i + 1) * 256].reshape(KC, P, 256).transpose(1, 0, 2).reshape(P, HALF) for i in range(2)]


def pad_half(h):
    return np.pad(h, ((0, 0), (0, HALF - h.shape[1])))


def by_partition(v):
    return v.reshape(-1, P).T


def pack(inputs):
    f = {k: np.asarray(v) for k, v in inputs.items()}
    w = f["w_in"][0]
    cols = {"qa": w[:, 0:512].reshape(D, H, HD)[:, PAIRS].reshape(D, 512), "kava": w[:, 512:768]}
    for g in range(3):
        for i, n in enumerate(("qb", "kb", "vb")):
            s = 768 + i * 1536 + g * 512
            cols[f"{n}{g}"] = w[:, s:s + 512]
    cols["ga"], cols["gb"] = w[:, 5376:5888], w[:, 5888:6400]
    for i in range(4):
        cols[f"mg{i}"] = w[:, 6400 + 512 * i:6912 + 512 * i]
    for c in range(2):
        cs = slice(512 * c, 512 * c + 512)
        cols[f"br0{c}"], cols[f"br1{c}"] = f["w_branch_a"][0][:, cs], f["w_branch_b"][0][:, cs]
        cols[f"wo{c}"] = f["w_out"][0][:, cs]
    halves = {p: chunks(c) for p, c in cols.items()}
    w_first = np.stack([pad_half(halves[p][int(n.split("/")[1])]) for n, p in FIRST_HALVES])

    w_layers, par = [], []
    for l in range(LAYERS):
        w = f["w_in_2"][l]
        at = dict(kc=512, vc=640, ks=768, vs=896, kw=1024, vw=1152)
        k = {n: w[:, s:s + P] for n, s in at.items()}
        cols = {"q": w[:, 0:512].reshape(D, H, HD)[:, PAIRS].reshape(D, 512),
                "k4": np.concatenate([k["kc"], k["vc"], k["ks"], k["kw"]], 1),
                "vsg": np.concatenate([k["vs"], k["vw"], w[:, 1280:1304]], 1),
                "qkr": w[:, 1304:1816], "vr": w[:, 1816:2328], "gr": w[:, 2328:2840],
                "ca": w[:, 2840:3352], "cb": w[:, 3352:3864]}
        for i in range(6):
            cols[f"mg{i}"] = w[:, 3864 + 512 * i:4376 + 512 * i]
        for c in range(2):
            cs = slice(512 * c, 512 * c + 512)
            for i in range(3):
                cols[f"br{i}{c}"] = f["w_branch_2"][l, i][:, cs]
            cols[f"wo{c}"] = f["w_out_2"][l][:, cs]
            cols[f"down{c}"] = f["w_ff2_2"][l][:, cs]
        for i in range(FF_PANELS):
            cols[f"ff{i}"] = f["w_ff1_2"][l][:, 512 * i:512 * i + 512]
        halves = {p: column_chunks(c) if p in BY_COLUMNS else chunks(c) for p, c in cols.items()}
        for n, p in LAYER_HALVES:
            if p.startswith("cmpH"):
                w1 = f["cmp_w1_" + n[2] + "_2"][l]
                w_layers.append(w1.reshape(16, 2 * HD, P).transpose(1, 0, 2).reshape(P, HALF))
            else:
                w_layers.append(pad_half(halves[p][int(n.split("/")[1])]))
        pe = [f[f"cmp_pe_{n}_2"][l].reshape(16, 2 * HD).T for n in "kv"]
        par.append(np.concatenate(
            [by_partition(f["norm_mlp_2"][l]), by_partition(f["ret_gn_2"][l]),
             by_partition(f["conv_ln_g_2"][l]), by_partition(f["conv_ln_b_2"][l]), by_partition(f["conv_b_2"][l]),
             f["conv_w_2"][l].T.reshape(4, P, TAPS).transpose(1, 0, 2).reshape(P, 4 * TAPS), *pe,
             f["cmp_w2_k_2"][l], f["cmp_w2_k_2"][l], f["cmp_w2_v_2"][l]], 1))
    w_layers += [np.zeros((P, HALF), np.float32)] * SLOTS
    par.append(np.zeros((P, PAR), np.float32))
    gains = np.stack([np.concatenate([f[n][0], f[n][0]]) for n in ("q_norm_a", "k_norm_a", "q_norm_b", "k_norm_b")], 1)
    return dict(
        x=f["x"][0], w_first=w_first, w_layers=np.stack(w_layers), par=np.stack(par),
        first=np.concatenate([by_partition(f["norm_gain"][0]), gains, np.tile(f["sink_a"][0:1], (P, 1))], 1),
        rel_bias=f["rel_bias"], rel_table=f["rel_table_2"], b_merge=f["b_merge"][0].reshape(-1),
        gains=np.concatenate([f["norm_mix_2"], f["norm_final_2"][None]]), ident=np.eye(P, dtype=np.float32), onehot=position_table(),
        decay=decay_table(), rope=rope_table())


def kernel(**inputs):
    import concourse.bacc as bacc
    from concourse.bass_utils import run_bass_kernel_spmd

    nc = bacc.Bacc("TRN2", target_bir_lowering=False, num_devices=1)
    arrays, args = {}, {}
    for name, v in pack(inputs).items():
        v = np.ascontiguousarray(v)
        arrays[f"in_{name}_dram"] = v
        args[name] = nc.dram_tensor(f"in_{name}_dram", v.shape, mybir.dt.from_np(v.dtype), kind="ExternalInput").ap()
    out = nc.dram_tensor("out_0_dram", (TOKENS, D), F32, kind="ExternalOutput").ap()
    block_kernel(nc, args, out)
    r = run_bass_kernel_spmd(nc, [arrays], core_ids=[0])
    return r.results[0]["out_0_dram"].reshape(1, TOKENS, D)
```
